# Optimizing a Trainium2 kernel written in Bass

```python
import jax, jax.numpy as jnp
from jax import lax
import numpy as np

D_MODEL = 1024
BATCH = 1
SEQ = 512
DEPTH = 2
DEC_BATCH = 8
DEC_SEQ = 1
PAST_LEN = 2048
PAGE_SIZE = 128

N_A = DEPTH // 2
N_B = DEPTH - N_A
RWKV_HEAD = 64
RWKV_H = D_MODEL // RWKV_HEAD
DECAY_LORA = 64
AAA_LORA = 64
N_MIX = 6
GN_EPS = 64e-5
MLA_H = 8
QK_NOPE = 128
QK_ROPE = 64
V_HEAD = 128
Q_LORA = 384
KV_LORA = 256
ROPE_THETA = 10000.0
ATTN_SCALE = (QK_NOPE + QK_ROPE) ** -0.5
Q_BLOCK = 128
EPS = 1e-6

kernel_name = "yoco_rwkv7_mla_step"

def rmsnorm(x, g):
    xf = x.astype(jnp.float32)
    y = xf * lax.rsqrt(jnp.mean(xf * xf, axis=-1, keepdims=True) + EPS)
    return (y * g.astype(jnp.float32)).astype(x.dtype)

def rope(x, pos):
    half = x.shape[-1] // 2
    inv = ROPE_THETA ** (-jnp.arange(half, dtype=jnp.float32) / half)
    ang = pos.astype(jnp.float32)[:, None] * inv[None, :]
    cos, sin = jnp.cos(ang)[:, None, :], jnp.sin(ang)[:, None, :]
    x1 = x[..., :half].astype(jnp.float32)
    x2 = x[..., half:].astype(jnp.float32)
    return jnp.concatenate([x1 * cos - x2 * sin, x1 * sin + x2 * cos], axis=-1).astype(x.dtype)

def rwkv7_time_mix(h, h_prev, S0, mu, w_in, w0, w1, w2, a0, a1, a2, k_k, k_a, r_k, gn_w, gn_b, w_out):
    B, T, D = h.shape
    f32 = jnp.float32
    xx = jnp.concatenate([h_prev[:, None, :].astype(h.dtype), h[:, :-1]], axis=1) - h
    xm = h[:, :, None, :] + xx[:, :, None, :] * mu
    proj = jnp.einsum('btmd,mde->btme', xm[:, :, :4], w_in)
    r, k, v, g = proj[:, :, 0], proj[:, :, 1], proj[:, :, 2], proj[:, :, 3]
    xw, xa = xm[:, :, 4], xm[:, :, 5]
    w_log = -jax.nn.softplus(-(w0 + jnp.tanh(xw @ w1) @ w2).astype(f32)) - 0.5
    decay = jnp.exp(-jnp.exp(w_log))
    a = jax.nn.sigmoid((a0 + (xa @ a1) @ a2).astype(f32))
    heads = lambda t: t.astype(f32).reshape(B, T, RWKV_H, RWKV_HEAD)
    kk = heads(k * k_k)
    kk = kk / jnp.maximum(jnp.sqrt(jnp.sum(kk * kk, axis=-1, keepdims=True)), 1e-12)
    k_mod = k.astype(f32) * (1.0 + (a - 1.0) * k_a.astype(f32))
    r_h, k_h, v_h, w_h, a_h = heads(r), heads(k_mod), heads(v), heads(decay), heads(a)
    seqs = tuple(jnp.moveaxis(t, 1, 0) for t in (r_h, w_h, k_h, v_h, kk, a_h))

    def step(S, inp):
        r_t, w_t, k_t, v_t, kk_t, a_t = inp
        sa = jnp.einsum('bhij,bhj->bhi', S, -kk_t)
        S = (S * w_t[:, :, None, :] + sa[..., None] * (kk_t * a_t)[:, :, None, :]
             + v_t[..., None] * k_t[:, :, None, :])
        return S, jnp.einsum('bhij,bhj->bhi', S, r_t)

    S_fin, ys = lax.scan(step, S0.astype(f32), seqs)
    y = jnp.moveaxis(ys, 0, 1)
    mean = jnp.mean(y, axis=-1, keepdims=True)
    var = jnp.mean(jnp.square(y - mean), axis=-1, keepdims=True)
    y = ((y - mean) * lax.rsqrt(var + GN_EPS)).reshape(B, T, D) * gn_w.astype(f32) + gn_b.astype(f32)
    bonus = jnp.sum(r_h * k_h * r_k.astype(f32), axis=-1, keepdims=True) * v_h
    y = (y + bonus.reshape(B, T, D)) * jax.nn.silu(g.astype(f32))
    return y.astype(h.dtype) @ w_out, S_fin.astype(S0.dtype), h[:, -1]

def shared_kv(x, c, pos, kv_ada_w, kv_ada_b, kv_norm, kv_w_a, kv_a_norm):
    shift, scale = jnp.split(c @ kv_ada_w + kv_ada_b, 2, axis=-1)
    h = rmsnorm(x, kv_norm) * (1.0 + scale[:, None, :]) + shift[:, None, :]
    kv = h @ kv_w_a
    c_kv = rmsnorm(kv[..., :KV_LORA], kv_a_norm)
    k_pe = rope(kv[..., None, KV_LORA:], pos)[:, :, 0]
    return c_kv, k_pe

def _attend_block(q_lat, q_pe, c_kv, k_pe, q_pos, k_pos):
    s = (jnp.einsum('bqhc,bkc->bhqk', q_lat, c_kv).astype(jnp.float32)
         + jnp.einsum('bqhr,bkr->bhqk', q_pe, k_pe).astype(jnp.float32)) * ATTN_SCALE
    s = jnp.where(k_pos[None, None, None, :] <= q_pos[None, None, :, None], s, -jnp.inf)
    p = jax.nn.softmax(s, axis=-1)
    return jnp.einsum('bhqk,bkc->bqhc', p.astype(c_kv.dtype), c_kv)

def mla_attend(q_lat, q_pe, c_kv, k_pe, q_pos, k_pos):
    B, T = q_lat.shape[0], q_lat.shape[1]
    if T <= Q_BLOCK or T % Q_BLOCK:
        return _attend_block(q_lat, q_pe, c_kv, k_pe, q_pos, k_pos)
    nb = T // Q_BLOCK
    split = lambda t: jnp.moveaxis(t.reshape(B, nb, Q_BLOCK, *t.shape[2:]), 1, 0)

    def blk(args):
        ql, qp, qpos = args
        return _attend_block(ql, qp, c_kv, k_pe, qpos, k_pos)

    out = lax.map(blk, (split(q_lat), split(q_pe), q_pos.reshape(nb, Q_BLOCK)))
    return jnp.moveaxis(out, 0, 1).reshape(B, T, MLA_H, KV_LORA)

def mla_mix(h, pos, c_kv, k_pe, k_pos, kv_w_b, w_in, q_norm, w_q, w_out):
    B, T, _ = h.shape
    qg = h @ w_in
    q_a, gate = qg[..., :Q_LORA], qg[..., Q_LORA:]
    q = jnp.einsum('btr,rhe->bthe', rmsnorm(q_a, q_norm), w_q)
    q_nope, q_pe = q[..., :QK_NOPE], rope(q[..., QK_NOPE:], pos)
    w_uk, w_uv = kv_w_b[..., :QK_NOPE], kv_w_b[..., QK_NOPE:]
    q_lat = jnp.einsum('bthn,chn->bthc', q_nope, w_uk)
    o_lat = mla_attend(q_lat, q_pe, c_kv, k_pe, pos, k_pos)
    o = jnp.einsum('bthc,chv->bthv', o_lat, w_uv).reshape(B, T, MLA_H * V_HEAD)
    return (o * jax.nn.silu(gate)) @ w_out

def trunk(x, c, pos, shift0, S0, past_ckv, past_kpe, layer_p, a_p, kv_p, kv_w_b, b_p):
    ada_w, ada_b, norm_pre, norm_post = layer_p
    new_S, new_shift = [], []
    c_kv = k_pe = keys = None
    for i in range(DEPTH):
        shift, scale, gate = jnp.split(c @ ada_w[i] + ada_b[i], 3, axis=-1)
        h = rmsnorm(x, norm_pre[i]) * (1.0 + scale[:, None, :]) + shift[:, None, :]
        if i < N_A:
            y, S_i, sh_i = rwkv7_time_mix(h, shift0[i], S0[i], *(p[i] for p in a_p))
            new_S.append(S_i)
            new_shift.append(sh_i)
        else:
            if keys is None:
                c_kv, k_pe = shared_kv(x, c, pos, *kv_p)
                if past_ckv is None:
                    keys = (c_kv, k_pe, pos)
                else:
                    k_pos = jnp.arange(past_ckv.shape[1] + x.shape[1], dtype=jnp.int32)
                    keys = (jnp.concatenate([past_ckv, c_kv], axis=1),
                            jnp.concatenate([past_kpe, k_pe], axis=1), k_pos)
            y = mla_mix(h, pos, keys[0], keys[1], keys[2], kv_w_b, *(p[i - N_A] for p in b_p))
        x = x + gate[:, None, :] * rmsnorm(y, norm_post[i])
    return x, jnp.stack(new_S), jnp.stack(new_shift), c_kv, k_pe

def setup_inputs(seed: int = 0) -> dict:
    key = jax.random.key(seed)
    ks = iter(jax.random.split(key, 64))

    def nrm(shape, scale=1.0):
        return jax.random.normal(next(ks), shape, jnp.float32) * scale

    D = D_MODEL
    n_pages = PAST_LEN // PAGE_SIZE
    n_used = DEC_BATCH * n_pages
    n_phys = n_used + n_used // 4
    page_table = jax.random.permutation(next(ks), n_phys)[:n_used].reshape(DEC_BATCH, n_pages).astype(jnp.int32)
    H, K = RWKV_H, RWKV_HEAD
    return {
        "x_prompt": nrm((BATCH, SEQ, D)),
        "x_sample": nrm((DEC_BATCH, DEC_SEQ, D)),
        "c_prompt": nrm((BATCH, D)),
        "c_sample": nrm((DEC_BATCH, D)),
        "state_wkv": nrm((N_A, DEC_BATCH, H, K, K), 0.3),
        "state_shift": nrm((N_A, DEC_BATCH, D)),
        "cache_kv_latent": nrm((n_phys, PAGE_SIZE, KV_LORA)),
        "cache_k_rope": nrm((n_phys, PAGE_SIZE, QK_ROPE)),
        "page_table": page_table,
        "ada_w": nrm((DEPTH, D, 3 * D), 0.5 * D ** -0.5),
        "ada_b": nrm((DEPTH, 3 * D), 0.02),
        "norm_pre": 1.0 + nrm((DEPTH, D), 0.02),
        "norm_post": 1.0 + nrm((DEPTH, D), 0.02),
        "a_mu": jax.random.uniform(next(ks), (N_A, N_MIX, D), jnp.float32),
        "a_w_in": nrm((N_A, 4, D, D), D ** -0.5),
        "a_w0": -2.0 + nrm((N_A, D), 0.5),
        "a_w1": nrm((N_A, D, DECAY_LORA), D ** -0.5),
        "a_w2": nrm((N_A, DECAY_LORA, D), 0.5 * DECAY_LORA ** -0.5),
        "a_a0": nrm((N_A, D), 0.3),
        "a_a1": nrm((N_A, D, AAA_LORA), D ** -0.5),
        "a_a2": nrm((N_A, AAA_LORA, D), 0.5 * AAA_LORA ** -0.5),
        "a_k_k": 0.85 + nrm((N_A, D), 0.02),
        "a_k_a": 1.0 + nrm((N_A, D), 0.02),
        "a_r_k": nrm((N_A, H, K), 0.1),
        "a_gn_w": 1.0 + nrm((N_A, D), 0.02),
        "a_gn_b": nrm((N_A, D), 0.02),
        "a_w_out": nrm((N_A, D, D), D ** -0.5),
        "kv_ada_w": nrm((D, 2 * D), 0.5 * D ** -0.5),
        "kv_ada_b": nrm((2 * D,), 0.02),
        "kv_norm": 1.0 + nrm((D,), 0.02),
        "kv_w_a": nrm((D, KV_LORA + QK_ROPE), D ** -0.5),
        "kv_a_norm": 1.0 + nrm((KV_LORA,), 0.02),
        "kv_w_b": nrm((KV_LORA, MLA_H, QK_NOPE + V_HEAD), KV_LORA ** -0.5),
        "b_w_in": nrm((N_B, D, Q_LORA + MLA_H * V_HEAD), D ** -0.5),
        "b_q_norm": 1.0 + nrm((N_B, Q_LORA), 0.02),
        "b_w_q": nrm((N_B, Q_LORA, MLA_H, QK_NOPE + QK_ROPE), Q_LORA ** -0.5),
        "b_w_out": nrm((N_B, MLA_H * V_HEAD, D), (MLA_H * V_HEAD) ** -0.5),
    }

def reference(x_prompt, x_sample, c_prompt, c_sample, state_wkv, state_shift, cache_kv_latent,
              cache_k_rope, page_table, ada_w, ada_b, norm_pre, norm_post, a_mu, a_w_in, a_w0,
              a_w1, a_w2, a_a0, a_a1, a_a2, a_k_k, a_k_a, a_r_k, a_gn_w, a_gn_b, a_w_out,
              kv_ada_w, kv_ada_b, kv_norm, kv_w_a, kv_a_norm, kv_w_b, b_w_in, b_q_norm, b_w_q,
              b_w_out):
    layer_p = (ada_w, ada_b, norm_pre, norm_post)
    a_p = (a_mu, a_w_in, a_w0, a_w1, a_w2, a_a0, a_a1, a_a2, a_k_k, a_k_a, a_r_k, a_gn_w, a_gn_b, a_w_out)
    kv_p = (kv_ada_w, kv_ada_b, kv_norm, kv_w_a, kv_a_norm)
    b_p = (b_w_in, b_q_norm, b_w_q, b_w_out)

    B, T, D = x_prompt.shape
    pos_p = jnp.arange(T, dtype=jnp.int32)
    shift0_p = jnp.zeros((N_A, B, D), x_prompt.dtype)
    S0_p = jnp.zeros((N_A, B, RWKV_H, RWKV_HEAD, RWKV_HEAD), x_prompt.dtype)
    y_prompt, wkv_p, shift_p, ckv_p, kpe_p = trunk(
        x_prompt, c_prompt, pos_p, shift0_p, S0_p, None, None, layer_p, a_p, kv_p, kv_w_b, b_p)

    DB, n_pages = page_table.shape
    past_len = n_pages * cache_kv_latent.shape[1]
    past_ckv = cache_kv_latent[page_table].reshape(DB, past_len, KV_LORA)
    past_kpe = cache_k_rope[page_table].reshape(DB, past_len, QK_ROPE)
    pos_s = past_len + jnp.arange(x_sample.shape[1], dtype=jnp.int32)
    y_sample, wkv_s, shift_s, ckv_s, kpe_s = trunk(
        x_sample, c_sample, pos_s, state_shift, state_wkv, past_ckv, past_kpe,
        layer_p, a_p, kv_p, kv_w_b, b_p)

    return (y_prompt, y_sample, wkv_p, shift_p, ckv_p, kpe_p, wkv_s, shift_s, ckv_s, kpe_s)


_drawn_inputs = setup_inputs


def setup_inputs(seed=0):
    import zlib

    import numpy as np

    out = dict(_drawn_inputs(seed))
    spreads = {}
    factors = {'norm_post': 4.63, 'a_gn_w': 6.062, 'a_gn_b': 6.429, 'kv_norm': 3.155, 'b_q_norm': 6.515}
    for name, (base, spread) in spreads.items():
        noise = np.random.default_rng([zlib.crc32(name.encode()), seed]).standard_normal(out[name].shape)
        drawn = base * np.exp(spread * noise) if base else spread * noise
        out[name] = __import__('jax').numpy.asarray(drawn.astype(out[name].dtype))
    for name, factor in factors.items():
        out[name] = (out[name] * factor).astype(out[name].dtype)
    return out
```

```python
from contextlib import ExitStack

import numpy as np

import concourse.bass as bass
from concourse import mybir

F32 = mybir.dt.float32
I32 = mybir.dt.int32
ALU = mybir.AluOpType
ACT = mybir.ActivationFunctionType
AX_X = mybir.AxisListType.X

P = 128
D = 1024
KT = D // P
T = 512
NS = 8
N = T + NS
HALF = N // 2
HD = 64
PAIRS = D // P
C = 64
NCH = T // C
TT = T // P
BLK = 2 * TT
LEVELS = (2, 4, 8, 16, 32)
NLEV = len(LEVELS)
LORA = 64
GN_EPS = 64e-5
EPS = 1e-6
H = 8
NOPE = 128
ROPE = 64
QL = 384
QT = QL // P
KVL = 256
ROPE_THETA = 10000.0
SCALE = float(NOPE + ROPE) ** -0.5
PAGE = 128
NPAGES = 16
NPHYS = 160
PAST = NPAGES * PAGE
NEG = -1e30
(V_PRE0, V_PRE1, V_POST0, V_POST1, V_MU, V_W0, V_A0, V_KK, V_KA, V_RK, V_GNW, V_GNB, V_KVN) = (
    0, 1, 2, 3, 4, 10, 11, 12, 13, 14, 15, 16, 17)
NVEC = 18
ADA_COLS = 512
ADA_GROUPS = 8 * D // ADA_COLS
ADA_MT = ADA_COLS // P
MOD_TILES = 8 * KT
M_SH0, M_SC0, M_G0, M_SH1, M_SC1, M_G1, M_SHK, M_SCK = (KT * i for i in range(8))
E05 = float(np.exp(np.float32(-0.5)))
U_R, U_K, U_V, U_G, U_W, U_A, U_SS, U_BO, U_TV, U_TB = range(10)
NUSE = 10
ARENA = 9580


def build(nc, d, o):
    ctx = ExitStack()
    with ctx:
        def sb(name, shape, dt=F32):
            return ctx.enter_context(nc.sbuf_tensor(name, shape, dt))

        def sem(name):
            return ctx.enter_context(nc.semaphore(name))

        ring = sb("ring", [P, 3, 4096])
        R0 = sb("R0", [P, KT, N])
        R1 = sb("R1", [P, KT, N])
        R2 = sb("R2", [P, KT, N])
        XM = sb("XM", [P, 4, KT, N])
        vecs = sb("vecs", [P, NVEC, KT])
        ident = sb("ident", [P, P])
        ones = sb("ones", [P, P])
        cT = sb("cT", [P, KT, 1 + NS])
        adab = sb("adab", [P, MOD_TILES])
        mod = sb("mod", [P, MOD_TILES, 1 + NS])
        A0 = sb("A0", [P, KT, 1 + NS])
        decbuf = sb("decbuf", [P, 8, PAIRS, NS])
        arena = sb("arena", [P, ARENA])

        def cutter(flat, size):
            used = [0]

            def cut(n):
                a = flat[:, used[0]:used[0] + n]
                used[0] += n
                assert used[0] <= size, (used[0], size)
                return a
            return cut

        cutA = cutter(arena, ARENA)
        cutX = cutter(ring[:, 2, :], 4096)
        cut0 = cutter(R0[:, :, :].rearrange("p a b -> p (a b)"), KT * N)
        cut2 = cutter(R2[:, :, :].rearrange("p a b -> p (a b)"), KT * N)

        maskM = cutA(256)
        lowm = cutA(C)
        lv1 = cutA(2 * C).rearrange("p (a t) -> p a t", a=2)
        lvm = cutA(NLEV * C).rearrange("p (l t) -> p l t", l=NLEV)
        id64 = cutA(C)
        bones = cutA(P)
        scanm = cutA(N)
        omka, nw0, na0 = cutA(KT), cutA(KT), cutA(KT)
        lhid = cutA(N)
        lora2 = cutA(2 * P).rearrange("p (s e) -> p s e", s=2)
        stat = arena[:, ARENA - N:ARENA]
        SAx = cutA(192)
        rhs = cutA(P)
        S = cutA(P)
        stmp = cutA(P)
        Sout = rhs
        AR = [cutA(2 * T).rearrange("p (c a t) -> p c a t", c=NCH, a=2) for _ in range(2)]
        Vx = [cutA(TT * 192).rearrange("p (c x) -> p c x", c=TT) for _ in range(2)]
        BK = [cutA(2 * T).rearrange("p (a c j) -> p a c j", a=2, c=TT) for _ in range(2)]
        pc = cutA(2 * NCH).rearrange("p (s c) -> p s c", s=2)
        MM = cutX(BLK * 256).rearrange("p (b q t) -> p b q t", b=BLK, q=4)
        Mab, Tm, Tt, Zt = (cutX(BLK * C).rearrange("p (b t) -> p b t", b=BLK) for _ in range(4))
        rT, kT, vT, bT, kmT = (cut0(N) for _ in range(5))
        wa = cut0(2 * N).rearrange("p (a n) -> p a n", a=2)
        sg, aT = wa[:, 0, :], wa[:, 1, :]
        cum, cumx = cut2(N), sg
        ecum, einv = cut0(N), cut2(N)
        kkT, sqk = cut2(N), cut2(N)
        tmb = sqk
        gT = [cut2(N) for _ in range(2)]
        bon = [cut2(N) for _ in range(2)]
        Bt, Kt_ = cutA(T), cutA(T)
        yc = Zt.rearrange("p b t -> p (b t)")
        ysq = Tm.rearrange("p b t -> p (b t)")
        lora1 = ring[:, 2, 0:KT * P].rearrange("p (k e) -> p k e", k=KT)
        shin = ring[:, 2, KT * P:KT * P + KT * NS].rearrange("p (k n) -> p k n", k=KT)
        shout = ring[:, 2, 1200:1200 + KT * (1 + NS)].rearrange("p (k n) -> p k n", k=KT)

        pj = ctx.enter_context(nc.psum_tensor("pj", [P, 2, 2, 512], F32))
        bk = ctx.enter_context(nc.psum_tensor("bk", [P, 4, 512], F32))
        pjs = [pj[:, s, :, 0:HALF] for s in range(2)]

        def two(ap):
            return ap.rearrange("p (a n) -> p a n", a=2)

        Sd = XM[:, 0, :, :].rearrange("p k n -> p (k n)")[:, 0:HD * HD].rearrange("p (i j) -> p i j", i=HD)
        Wd1 = XM[:, 1, :, :].rearrange("p k n -> p (k n)")[:, 0:HD * HD].rearrange("p (i j) -> p i j", i=HD)
        Wd2 = XM[:, 2, :, :].rearrange("p k n -> p (k n)")[:, 0:HD * HD].rearrange("p (i j) -> p i j", i=HD)
        cut0b = cutter(R2[:, :, :].rearrange("p a b -> p (a b)"), KT * N)
        dturn = cut0b(6 * P).rearrange("p (q j) -> p q j", q=6)
        dq = cut0b(6 * HD).rearrange("p (q j) -> p q j", q=6)
        sa = cut0b(HD)
        yd = cut0b(HD)
        bst, bag, rsd = cut0b(6), cut0b(2), cut0b(1)
        ydt = cut0b(P)
        Y = XM[:, 3, :, :]
        GATE = XM[:, 3, :, :]
        HN = XM[:, 1, :, :]
        HK = XM[:, 2, :, :]
        H1 = XM[:, 0, :, :]
        SQ = R2[:, :, :]
        QN = XM[:, 2, :, :]
        R2g = R2[:, :, :].rearrange("p a b -> p (a b)")
        QP = R2g[:, 0:4 * N].rearrange("p (i n) -> p i n", i=4)
        UV = R2g[:, 4 * N:4 * N + 2048].rearrange("p (a e) -> p a e", a=2)
        KN = XM[:, 1, :, :].rearrange("p k n -> p (k n)")[:, 0:H * T].rearrange("p (h t) -> p h t", h=H)
        VN = XM[:, 0, :, :].rearrange("p k n -> p (k n)")[:, 0:TT * D].rearrange("p (t e) -> p t e", t=TT)
        OG = R1
        cutB = cutter(arena, ARENA)
        kvn = cutB(5 * 384).rearrange("p (t e) -> p t e", t=5)
        ckvT = cutB(2 * N).rearrange("p (a n) -> p a n", a=2)
        kpeT = cutB(N)
        qa = cutB(QT * N).rearrange("p (a n) -> p a n", a=QT)
        cosT, sinT = cutB(N), cutB(N)
        cosN, sinN = cutB(5 * ROPE).rearrange("p (t e) -> p t e", t=5), cutB(5 * ROPE).rearrange("p (t e) -> p t e", t=5)
        kvg = cutB(KVL)
        qng = cutB(QT)
        st = cutB(N)
        kss = cutB(8)
        rtmp = cutB(N)
        qlat = cutB(2 * H * NS).rearrange("p (a h s) -> p a h s", a=2, h=H)
        A1 = cutB(KT * 9).rearrange("p (k n) -> p k n", k=KT)
        rt64 = cutB(ROPE)
        qpd = cutB(H * NS).rearrange("p (h s) -> p h s", h=H)
        olat = cutB(2 * H * NS).rearrange("p (a h s) -> p a h s", a=2, h=H)
        causal = cutB(P)
        mx, nmx, den = cutB(4), cutB(4), cutB(4)
        scb = cutB((NPAGES + 1) * H).rearrange("p (g h) -> p g h", g=NPAGES + 1)
        dmx, dmg, dsum, drc = cutB(H), cutB(H), cutB(H), cutB(H)
        PN = rtmp[:, 0:T]
        PTb = st[:, 0:T].rearrange("p (b q) -> p b q", b=TT)
        ckr = kvg
        CK = [ring[:, i, :].rearrange("p (t c) -> p t c", t=NPAGES) for i in range(2)]
        CR = [ring[:, 2, i * 1024:(i + 1) * 1024].rearrange("p (t c) -> p t c", t=NPAGES) for i in range(2)]
        KG = ring[:, 2, 2048:2048 + 3 * 512].rearrange("p (a k) -> p a k", a=3)
        ptab = sb("ptab", [P, NS], I32)
        pidx = sb("pidx", [P, NS], I32)
        prow = sb("prow", [P, 1])

        s_const = sem("constants_loaded")
        s_mask = sem("masks_loaded")
        s_x = sem("x_loaded")
        s_ada = [sem("ada_group_loaded0"), sem("ada_group_loaded1")]
        s_ada_mm = sem("ada_products_done")
        s_ada_out = sem("ada_tiles_stored")
        s_sq = sem("squares_ready")
        s_ss = sem("square_sums_done")
        s_ms = sem("mean_squares_ready")
        s_rstd = sem("rstd_ready")
        s_xm = sem("mixed_input_ready")
        s_l1 = sem("lora1_loaded")
        s_hid = sem("lora_hidden_products")
        s_hida = sem("lora_hidden_by_act")
        s_hidr = sem("lora_hidden_ready")
        s_shout = sem("shift_rows_ready")
        s_store = sem("outputs_stored")
        s_dve, s_act, s_pool = sem("dve_steps"), sem("act_steps"), sem("pool_steps")
        s_pw = [sem("pair_weights_loaded0"), sem("pair_weights_loaded1")]
        s_pjm = sem("projection_slot_filled")
        s_ra = sem("projection_slot_read_by_act")
        s_rd = sem("projection_slot_read_by_dve")
        s_pa = sem("pair_factors_by_act")
        s_pd = sem("pair_factors_by_dve")
        s_pp = sem("pair_factors_by_pool")
        s_M = sem("chunk_products_done")
        s_Me = sem("chunk_products_masked")
        s_Z = sem("inverse_z_product")
        s_Ze = sem("inverse_z_stored")
        s_T = sem("inverse_t_product")
        s_Te = sem("inverse_t_stored")
        s_sc = sem("scan_products")
        s_sce = sem("scan_operand_stored")
        s_Se = sem("state_updated")
        s_gna = sem("group_norm_by_act")
        s_gnd = sem("group_norm_centered")
        s_gnp = sem("group_norm_sums")
        s_yT = sem("mixer_tile_ready")
        s_So = sem("state_transposed")
        s_Soa = sem("state_out_ready")
        s_Sst = sem("state_out_stored")
        s_zero = sem("padding_cleared")
        s_zp = sem("pair_vectors_ready")

        s_xr = sem("x_loaded_again")
        s_w = [sem(f"weights_loaded{i}") for i in range(3)]
        s_wu = sem("weights_used")
        s_adb = sem("later_ada_tiles_stored")
        s_dt = sem("decode_factors_turned")
        s_dta = sem("decode_factors_stored")
        s_dq = sem("decode_factors_moved")
        s_sd = sem("decode_state_loaded")
        s_dd = sem("decode_step_by_dve")
        s_dp = sem("decode_step_by_pool")
        s_dso = sem("decode_state_stored")
        s_dr = sem("decode_rstd_ready")
        s_ydm = sem("decode_y_moved")
        s_ydt = sem("decode_y_turned")
        s_r1 = sem("decode_mixer_tile_ready")
        s_om = sem("output_tile_product")
        s_oa = sem("output_tile_stored")
        s_ns = sem("norm_sums_done")
        s_nd = sem("norm_mean_ready")
        s_na = sem("norm_rstd_ready")
        s_nq = sem("norm_squares_ready")
        s_res = sem("residual_ready")
        s_hh = sem("inputs_of_layer1_by_dve")
        s_hha = sem("inputs_of_layer1_by_act")
        s_cb = sem("second_half_constants_loaded")
        s_kvm = sem("kv_tile_product")
        s_kva = sem("kv_square_sums")
        s_kvd = sem("kv_mean_ready")
        s_kvr = sem("kv_rstd_ready")
        s_kvn = sem("kv_tile_ready")
        s_kvt = sem("kv_tile_turned")
        s_kvs = sem("kv_tile_turned_stored")
        s_kvo = sem("kv_outputs_stored")
        s_bm = sem("layer1_projection_product")
        s_ba = sem("layer1_projection_by_act")
        s_bd = sem("layer1_projection_by_dve")
        s_qn = sem("q_latent_normed")
        s_uv = sem("uv_loaded")
        s_pidx = sem("page_rows_ready")
        s_pt = sem("page_table_loaded")
        s_ck = [sem("cache_loaded0"), sem("cache_loaded1")]
        s_sm = sem("attention_scores_done")
        s_sd1 = sem("attention_row_max")
        s_sa1 = sem("attention_exp_done")
        s_sd2 = sem("attention_rows_scaled")
        s_pt1 = sem("attention_rows_turned")
        s_pa1 = sem("attention_rows_turned_stored")
        s_po = sem("attention_output_done")
        s_pog = sem("attention_output_gated")
        s_kt = sem("cache_tiles_turned")
        s_kta = sem("cache_tiles_turned_by_act")
        s_ktd = sem("cache_tiles_turned_by_dve")
        s_ds = sem("decode_scores_done")
        s_dsd = sem("decode_softmax_by_dve")
        s_dsp = sem("decode_max_all_partitions")
        s_dsa = sem("decode_exp_done")
        s_dn = sem("decode_sums_done")
        s_dv = sem("decode_values_done")
        s_dvd = sem("decode_latent_ready")
        s_qpd = sem("decode_q_rope_moved")
        s_ckr = sem("decode_new_row_moved")
        s_do = sem("decode_output_done")
        s_y = sem("result_stored")

        stream = [("ada", g) for g in range(6, ADA_GROUPS)] + [("w_out", 0), ("w_out", 1), ("kv_w_a", 0),
                  ("b_w_in", 0), ("b_w_in", 1), ("b_w_in", 2), ("w_q", 0), ("w_q", 1), ("uk", 0)]
        SI = {key: n for n, key in enumerate(stream)}
        NST = len(stream)
        B_Q, B_PE, B_K, B_V, B_L = 11, 19, 27, 35, 43

        def used(n):
            name, g = stream[n]
            if name == "ada":
                return s_wu, n + 1
            return {"w_out": (s_om, 4 * g + 4), "kv_w_a": (s_kvm, 5), "b_w_in": (s_bm, QT + 4 * g),
                    "w_q": (s_bm, B_K if g else B_PE), "uk": (s_bm, B_L + 1)}[name]

        block = ctx.enter_context(nc.Block())

        def counter(eng, own):
            count = {}

            def mark(ins, s=None):
                s = own if s is None else s
                count[id(s)] = count.get(id(s), 0) + 1
                ins.then_inc(s, 1)
                return s, count[id(s)]

            def then(ins, s=None):
                eng.wait_ge(*mark(ins, s))
            return then, mark

        def store_state(sp, m):
            sp.wait_ge(s_Soa, m + 1)
            for h in range(2):
                sp.dma_start(o["wkv_p"][2 * m + h], Sout[h * HD:(h + 1) * HD, h * HD:(h + 1) * HD]).then_inc(s_Sst, 16)

        @block.sync
        def _(sp):
            for name, dst in (("ident", ident[:, :]), ("ones", ones[:, :]), ("vecs", vecs[:, :, :]),
                              ("adab", adab[:, :]), ("cT", cT[:, :, :])):
                sp.dma_start(dst, d[name]).then_inc(s_const, 16)
            sp.dma_start(R0[:, :, :], d["xT"]).then_inc(s_x, 16)
            for g in range(6):
                if g >= 2:
                    sp.wait_ge(s_ada_mm, g - 1)
                sp.dma_start(ring[:, g % 2, :], d["ada"][g]).then_inc(s_ada[g % 2], 16)
            for m in range(PAIRS):
                if m < 2:
                    sp.wait_ge(s_ada_mm, 5 + m)
                else:
                    sp.wait_ge(s_pjm, NUSE * (m - 2) + U_A + 1)
                sp.dma_start(ring[:, m % 2, :], d["w_in"][m]).then_inc(s_pw[m % 2], 16)
                sp.dma_start(lora2[:, m % 2, :], d["lora2"][m]).then_inc(s_pw[m % 2], 16)
                if m >= 2:
                    store_state(sp, m - 2)
            store_state(sp, PAIRS - 2)
            store_state(sp, PAIRS - 1)
            sp.wait_ge(s_yT, PAIRS)
            sp.wait_ge(s_pp, 3 * PAIRS)
            sp.wait_ge(s_pa, 4 * PAIRS)
            sp.dma_start(R0[:, :, :], d["xT"]).then_inc(s_xr, 16)
            sp.dma_start(Sd, d["Sd"]).then_inc(s_sd, 16)
            for n, (name, g) in enumerate(stream):
                if n >= 3:
                    sp.wait_ge(*used(n - 3))
                src = d[name][g]
                sp.dma_start(ring[:, n % 3, 0:src.shape[1]], src).then_inc(s_w[n % 3], 16)
            for n in range(NS):
                sp.wait_ge(s_kvn, 5)
                sp.wait_ge(s_dvd, n)
                sp.dma_start(ckr[0:1, :], kvn[n:n + 1, TT, 0:KVL]).then_inc(s_ckr, 16)
            for i in range(2):
                sp.wait_ge(s_dvd, NS)
                sp.dma_start(ring[:, i, :], d["b_w_out"][i]).then_inc(s_w[i], 16)
            sp.wait_ge(s_res, 2)
            sp.dma_start(o["y"], R0[:, :, :]).then_inc(s_y, 16)
            sp.wait_ge(s_y, 16)
            sp.wait_ge(s_Sst, 32 * PAIRS)
            sp.wait_ge(s_store, 16)
            sp.wait_ge(s_dso, 16)
            sp.wait_ge(s_kvo, 160)

        @block.scalar
        def _(act):
            then, mark = counter(act, s_act)
            A = nc.scalar.activation
            nc.scalar.preload_act_table_set("natural_log_exp_and_others")
            for name, dst in (("scanm", scanm), ("maskM", maskM), ("lowm", lowm), ("lv1", lv1), ("lvm", lvm),
                              ("id64", id64), ("bones", bones)):
                act.dma_start(dst, d[name]).then_inc(s_mask, 16)
            act.dma_start(lora1, d["lora1"]).then_inc(s_l1, 16)
            act.dma_start(shin, d["shiftT"]).then_inc(s_l1, 16)
            act.wait_ge(s_x, 16)
            mark(A(R2[:, :, :], R0[:, :, :], ACT.Square), s_sq)
            act.wait_ge(s_ms, 1)
            then(A(stat, stat, ACT.Ln))
            mark(A(stat, stat, ACT.Exp, scale=-0.5), s_rstd)
            act.wait_ge(s_shout, 1)
            act.dma_start(o["shift"], shout).then_inc(s_store, 16)
            act.wait_ge(s_hid, 1)
            then(A(two(lhid)[0:LORA], pjs[0][0:LORA], ACT.Exp, scale=2.0))
            then(A(lhid[0:LORA], lhid[0:LORA], ACT.Ln, bias=1.0))
            mark(A(lhid[0:LORA], lhid[0:LORA], ACT.Exp, scale=-1.0), s_hida)
            act.wait_ge(s_hid, 2)
            mark(A(two(lhid)[LORA:P], pjs[1][LORA:P], ACT.Identity), s_hida)

            def prep(m, part):
                v = m % 2
                if part == "r":
                    act.wait_ge(s_pjm, NUSE * m + U_R + 1)
                    if m >= 1:
                        act.wait_ge(s_pd, 4 * m)
                        act.wait_ge(s_pp, 3 * m)
                    if m >= 2:
                        act.wait_ge(s_yT, m - 1)
                    mark(A(two(rT), pjs[0], ACT.Identity), s_ra)
                if part == "k":
                    act.wait_ge(s_pjm, NUSE * m + U_K + 1)
                    mark(A(two(kT), pjs[1], ACT.Identity))
                    mark(A(two(sqk), pjs[1], ACT.Square, scale=vecs[:, V_KK, m:m + 1]), s_ra)
                if part == "v":
                    act.wait_ge(s_pjm, NUSE * m + U_V + 1)
                    mark(A(two(vT), pjs[0], ACT.Identity), s_ra)
                if part == "g":
                    act.wait_ge(s_pjm, NUSE * m + U_G + 1)
                    then(A(two(gT[v]), pjs[1], ACT.Exp, scale=-1.0))
                    then(A(gT[v], gT[v], ACT.Ln, bias=1.0))
                    mark(A(gT[v], gT[v], ACT.Exp, scale=-1.0), s_pa)
                if part == "wa":
                    act.wait_ge(s_pjm, NUSE * m + U_W + 1)
                    if m == 0:
                        act.wait_ge(s_zp, 3)
                    mark(A(two(sg), pjs[0], ACT.Exp, scale=-1.0, bias=nw0[:, m:m + 1]), s_ra)
                    act.wait_ge(s_pjm, NUSE * m + U_A + 1)
                    then(A(two(aT), pjs[1], ACT.Exp, scale=-1.0, bias=na0[:, m:m + 1]), s_ra)
                    then(A(wa, wa, ACT.Ln, bias=1.0))
                    mark(A(wa, wa, ACT.Exp, scale=-1.0), s_pa)
                if part == "kk":
                    act.wait_ge(s_rd, 3 * m + 2)
                    then(A(sqk, sqk, ACT.Ln))
                    mark(A(sqk, sqk, ACT.Exp, scale=-0.5), s_pa)
                if part == "cum":
                    act.wait_ge(s_pd, 4 * m + 1)
                    mark(A(ecum, cum, ACT.Exp, scale=-E05))
                    mark(A(einv, cum, ACT.Exp, scale=E05))
                    mark(A(cumx, cumx, ACT.Exp, scale=-E05), s_pa)
                if part == "tv":
                    act.wait_ge(s_pjm, NUSE * m + U_TV + 1)
                    act.wait_ge(s_zero, 1)
                    mark(A(Vx[v].rearrange("p c (h x) -> p c h x", x=HD)[:, :, 0:3:2, :],
                           pj[:, 0, 0, :].rearrange("p (c h x) -> p c h x", c=TT, h=2), ACT.Identity), s_ra)
                if part == "tb":
                    act.wait_ge(s_pjm, NUSE * m + U_TB + 1)
                    mark(A(BK[v].rearrange("p a c j -> p a (c j)"), pj[:, 1, :, :], ACT.Identity), s_ra)

            def scan(m, ch):
                pr = slice((ch % 2) * C, (ch % 2) * C + C)
                n = 4 * (NCH * m + ch)
                act.wait_ge(s_sc, n + 1)
                if ch == 0 and m >= 1:
                    act.wait_ge(s_Sst, 32 * m)
                mark(A(rhs[pr], bk[pr, 3, 0:P], ACT.Copy, scale=-1.0), s_sce)
                act.wait_ge(s_sc, n + 2)
                mark(A(SAx[pr].rearrange("p (h x) -> p h x", x=HD)[:, 0:3:2, :],
                       bk[pr, 0, 0:P].rearrange("p (h x) -> p h x", h=2), ACT.Identity), s_sce)

            def norm(m):
                act.wait_ge(s_sc, 4 * NCH * (m + 1))
                mark(A(yc, bk[:, 2, :], ACT.Identity), s_gna)
                act.wait_ge(s_So, m + 1)
                mark(A(Sout, bk[:, 3, 0:P], ACT.Identity), s_Soa)
                act.wait_ge(s_gnd, m + 1)
                mark(A(ysq, yc, ACT.Square), s_gna)
                act.wait_ge(s_gnp, 2 * m + 2)
                then(A(ysq, bk[:, 1, :], ACT.Ln, scale=1.0 / HD, bias=GN_EPS))
                mark(A(ysq, ysq, ACT.Exp, scale=-0.5), s_gna)

            for part in ("r", "k", "v", "g", "wa", "kk", "cum", "tv", "tb"):
                prep(0, part)
            for m in range(PAIRS):
                more = m + 1 < PAIRS
                if more:
                    for part in ("r", "k", "v", "g", "wa"):
                        prep(m + 1, part)
                for ch in range(NCH):
                    scan(m, ch)
                    if more and ch == 1:
                        prep(m + 1, "kk")
                    if more and ch == 2:
                        prep(m + 1, "cum")
                    if more and ch == 6:
                        prep(m + 1, "tv")
                norm(m)
                if more:
                    prep(m + 1, "tb")

            act.wait_ge(s_yT, PAIRS)
            act.wait_ge(s_pp, 3 * PAIRS)
            act.wait_ge(s_Sst, 32 * PAIRS)
            for name, dst in (("cosT", cosT), ("sinT", sinT), ("cosN", cosN), ("sinN", sinN), ("kvg", kvg),
                              ("qng", qng), ("causal", causal), ("prow", prow[:, :])):
                act.dma_start(dst, d[name]).then_inc(s_cb, 16)
            act.dma_start(ptab[:, :], d["page_table"]).then_inc(s_pt, 16)

            def ada(n):
                g = stream[n][1]
                act.wait_ge(s_wu, n + 1)
                for t in range(ADA_MT):
                    mark(A(mod[:, ADA_MT * g + t, :], bk[:, n % 2, 9 * t:9 * t + 9], ACT.Identity,
                           bias=adab[:, ADA_MT * g + t:ADA_MT * g + t + 1]), s_adb)

            def turn_factors():
                act.wait_ge(s_dt, 1)
                mark(A(dturn[0:HD, 0:4, :], pj[0:HD, 0, 0, :].rearrange("p (q j) -> p q j", q=4), ACT.Identity))
                then(A(dturn[0:HD, 4:6, :], pj[0:HD, 0, 1, 0:256].rearrange("p (q j) -> p q j", q=2), ACT.Identity))
                for hp in range(2):
                    act.dma_start(dq[hp * HD:(hp + 1) * HD], dturn[0:HD, :, hp * HD:(hp + 1) * HD]).then_inc(s_dq, 16)

            turn_factors()
            for n in range(5):
                ada(n)
            act.wait_ge(s_dd, 4)
            act.dma_start(o["wkv_s"], Sd).then_inc(s_dso, 16)
            act.wait_ge(s_dd, 5)
            then(A(rsd, bag[:, 1:2], ACT.Ln, bias=GN_EPS))
            mark(A(rsd, rsd, ACT.Exp, scale=-0.5), s_dr)
            act.wait_ge(s_dd, 6)
            for hp in range(2):
                act.dma_start(ydt[0:HD, hp * HD:(hp + 1) * HD], yd[hp * HD:(hp + 1) * HD]).then_inc(s_ydm, 16)
            for n in range(5, 10):
                ada(n)

            def out_tiles(layer):
                for t in range(KT):
                    act.wait_ge(s_om, KT * layer + t + 1)
                    mark(A(two(SQ[:, t, :]), pjs[t % 2], ACT.Square), s_nq)
                    mark(A(two(Y[:, t, :]), pjs[t % 2], ACT.Identity), s_oa)

            nn = [0]

            def rstd(x):
                nn[0] += 1
                act.wait_ge(s_nd, nn[0])
                then(A(x, x, ACT.Ln))
                mark(A(x, x, ACT.Exp, scale=-0.5), s_na)

            out_tiles(0)
            rstd(st)
            act.wait_ge(s_res, 1)
            mark(A(SQ[:, :, :], R0[:, :, :], ACT.Square), s_nq)
            rstd(st)
            act.wait_ge(s_hh, 1)
            act.wait_ge(s_dso, 16)
            for k in range(KT):
                mark(A(H1[:, k, 0:T], HN[:, k, 0:T], ACT.Identity, scale=A0[:, k, 0:1], bias=mod[:, M_SH1 + k, 0:1]), s_hha)

            for t in range(5):
                n = P if t < TT else NS
                act.wait_ge(s_kvm, t + 1)
                then(A(rtmp[0:n, 0:KVL], pj[0:n, t % 2, 0, 0:KVL], ACT.Square, accum_out=kss[0:n, 0:1]), s_kva)
                act.wait_ge(s_kvd, t + 1)
                then(A(kss[0:n, 1:2], kss[0:n, 1:2], ACT.Ln))
                mark(A(kss[0:n, 1:2], kss[0:n, 1:2], ACT.Exp, scale=-0.5), s_kvr)
                act.wait_ge(s_kvt, t + 1)
                mark(A(ckvT[:, :, t * P:t * P + n], bk[:, 2, 0:2 * n].rearrange("p (a n) -> p a n", a=2), ACT.Identity))
                mark(A(kpeT[:, t * P:t * P + n], bk[:, 2, 2 * n:3 * n], ACT.Identity), s_kvs)
                act.wait_ge(s_kvn, t + 1)
                act.dma_start(o["ckv"][t * P:t * P + n, :], kvn[0:n, t, 0:KVL]).then_inc(s_kvo, 16)
                act.dma_start(o["kpe"][t * P:t * P + n, :], kvn[0:n, t, KVL:KVL + ROPE]).then_inc(s_kvo, 16)

            for t in range(QT + KT):
                act.wait_ge(s_bm, t + 1)
                if t < QT:
                    mark(A(two(SQ[:, t, :]), pjs[t % 2], ACT.Square), s_nq)
                    mark(A(two(qa[:, t, :]), pjs[t % 2], ACT.Identity), s_ba)
                else:
                    g = GATE[:, t - QT, :]
                    then(A(two(g), pjs[t % 2], ACT.Exp, scale=-1.0))
                    then(A(g, g, ACT.Ln, bias=1.0))
                    mark(A(g, g, ACT.Exp, scale=-1.0), s_ba)
                    if t == QT:
                        rstd(st)
                        act.dma_start(UV, d["uv"]).then_inc(s_uv, 16)
            for t in range(H):
                act.wait_ge(s_bm, B_Q + t + 1)
                mark(A(two(QN[:, t, :]), pjs[(B_Q + t) % 2], ACT.Identity), s_ba)
            act.wait_ge(s_bd, KT + 4)
            for hp in range(2):
                act.dma_start(qpd[0:ROPE, hp:H:2, :], QP[hp * ROPE:(hp + 1) * ROPE, :, T:N]).then_inc(s_qpd, 16)
            base = B_K
            for t in range(H):
                act.wait_ge(s_bm, base + t + 1)
                mark(A(KN[:, t, :], bk[:, t % 2, :], ACT.Identity), s_ba)
            for t in range(2 * TT):
                act.wait_ge(s_bm, base + H + t + 1)
                mark(A(VN[:, t // 2, (t % 2) * 512:(t % 2) * 512 + 512], bk[:, t % 2, :], ACT.Identity), s_ba)
            act.wait_ge(s_bm, base + H + 2 * TT + 1)
            mark(A(qlat, bk[:, 2, 0:2 * H * NS].rearrange("p (a h s) -> p a h s", a=2, h=H), ACT.Identity), s_ba)

            def prompt(h):
                for q in range(TT):
                    n = TT * h + q
                    w = (q + 1) * P
                    act.wait_ge(s_sd1, n + 1)
                    act.wait_ge(s_pt1, n)
                    mark(A(PN[:, 0:w], bk[:, 0, 0:w], ACT.Exp, scale=SCALE, bias=nmx[:, 0:1], accum_out=den[:, 0:1]), s_sa1)
                    act.wait_ge(s_pt1, n + 1)
                    act.wait_ge(s_po, n)
                    mark(A(PTb[:, 0:q + 1, :], bk[:, 1, 0:w].rearrange("p (b q) -> p b q", q=P), ACT.Identity), s_pa1)

            def decode(s):
                for g in range(NPAGES // 4):
                    n = s * 4 + g
                    act.wait_ge(s_kt, n + 1)
                    act.wait_ge(s_ds, 5 * s + g)
                    mark(A(KG[:, 0:2, :], pj[:, 0, :, :], ACT.Identity), s_kta)
                act.wait_ge(s_dsd, 3 * s + 2)
                mark(A(scb, scb, ACT.Exp, scale=SCALE), s_dsa)

            for i in range(H):
                prompt(i)
                decode(i)
            out_tiles(1)
            rstd(st)

        @block.tensor
        def _(pe):
            mm, tr = nc.tensor.matmul, nc.tensor.transpose
            pe.wait_ge(s_const, 80)
            for g in range(6):
                pe.wait_ge(s_ada[g % 2], 16 * (g // 2 + 1))
                if g >= 2:
                    pe.wait_ge(s_ada_out, g - 1)
                w = ring[:, g % 2, :].rearrange("p (k e) -> p k e", k=KT)
                for t in range(ADA_MT):
                    for k in range(KT):
                        last = mm(bk[:, g % 2, 9 * t:9 * t + 9], w[:, k, t * P:(t + 1) * P], cT[:, k, :],
                                  start=(k == 0), stop=(k == KT - 1))
                last.then_inc(s_ada_mm, 1)
                if g == 1:
                    pe.wait_ge(s_sq, 1)
                    for k in range(KT):
                        for a in range(2):
                            last = mm(pj[:, 0, a, 0:HALF], ones[:, :], R2[:, k, a * HALF:(a + 1) * HALF],
                                      start=(k == 0), stop=(k == KT - 1))
                    last.then_inc(s_ss, 1)
            pe.wait_ge(s_l1, 32)
            for e in range(2):
                pe.wait_ge(s_xm, e + 1)
                for k in range(KT):
                    for a in range(2):
                        last = mm(pj[e * LORA:(e + 1) * LORA, e, a, 0:HALF], lora1[:, k, e * LORA:(e + 1) * LORA],
                                  XM[:, e, k, a * HALF:(a + 1) * HALF], start=(k == 0), stop=(k == KT - 1))
                last.then_inc(s_hid, 1)

            def project(m, e):
                s = e % 2
                if m == 0:
                    pe.wait_ge(s_xm, (5, 6, 3, 4)[e])
                if e == U_R:
                    pe.wait_ge(s_pw[m % 2], 32 * (m // 2 + 1))
                    if m >= 1:
                        pe.wait_ge(s_ra, 7 * m - 1)
                    else:
                        pe.wait_ge(s_hida, 2)
                if e == U_K and m >= 1:
                    pe.wait_ge(s_ra, 7 * m)
                if e == U_V:
                    pe.wait_ge(s_ra, 7 * m + 1)
                if e == U_G:
                    pe.wait_ge(s_ra, 7 * m + 2)
                w = ring[:, m % 2, :].rearrange("p (e k c) -> p e k c", e=4, k=KT)
                for k in range(KT):
                    for a in range(2):
                        last = mm(pj[:, s, a, 0:HALF], w[:, e, k, :], XM[:, e, k, a * HALF:(a + 1) * HALF],
                                  start=(k == 0), stop=(k == KT - 1))
                last.then_inc(s_pjm, 1)

            def lora(m, e):
                if m == 0:
                    pe.wait_ge(s_hidr, 1)
                    pe.wait_ge(s_hida, 2)
                if e == 0:
                    pe.wait_ge(s_ra, 7 * m + 3)
                else:
                    pe.wait_ge(s_rd, 3 * m + 1)
                r = slice(e * LORA, (e + 1) * LORA)
                for a in range(2):
                    last = mm(pj[:, e, a, 0:HALF], lora2[r, m % 2, :], lhid[r, a * HALF:(a + 1) * HALF],
                              start=True, stop=True)
                last.then_inc(s_pjm, 1)

            def head_sums(m, which):
                if which == 0:
                    pe.wait_ge(s_ra, 7 * m + 4)
                else:
                    pe.wait_ge(s_pd, 4 * m + 3)
                    pe.wait_ge(s_ra, 7 * m + 5)
                x = sqk if which == 0 else tmb
                for a in range(2):
                    last = mm(pj[:, which, a, 0:HALF], bones, x[:, a * HALF:(a + 1) * HALF], start=True, stop=True)
                last.then_inc(s_pjm, 1)

            def turn_v(m):
                pe.wait_ge(s_rd, 3 * m + 2)
                for t in range(TT):
                    last = tr(pj[:, 0, 0, t * P:(t + 1) * P], vT[:, t * P:(t + 1) * P], ident[:, :])
                last.then_inc(s_pjm, 1)

            def turn_bk(m):
                pe.wait_ge(s_pd, 4 * m + 4)
                pe.wait_ge(s_rd, 3 * m + 3)
                for a, x in ((0, cum), (1, sqk)):
                    for t in range(TT):
                        last = tr(pj[:, 1, a, t * P:(t + 1) * P], x[:, t * P:(t + 1) * P], ident[:, :])
                last.then_inc(s_pjm, 1)

            def chunk_products(m):
                v = m % 2
                pe.wait_ge(s_pd, 4 * m + 4)
                if m >= 1:
                    pe.wait_ge(s_yT, m)
                    pe.wait_ge(s_Soa, m)
                for half in range(2):
                    for h in range(2):
                        r = slice(h * HD, (h + 1) * HD)
                        for u in range(4):
                            t, cp = 2 * half + u // 2, u % 2
                            ch = 2 * t + cp
                            for a, x in ((0, Bt), (1, Kt_)):
                                c0 = (u // 2) * 256 + a * P
                                last = mm(bk[cp * C:(cp + 1) * C, 2 * half + h, c0:c0 + P], x[r, ch * C:(ch + 1) * C],
                                          AR[v][r, ch, :, :].rearrange("p a t -> p (a t)"), start=True, stop=True)
                        last.then_inc(s_M, 1)
                pe.wait_ge(s_Me, 5 * m + 2)
                for h in range(2):
                    r = slice(h * HD, (h + 1) * HD)
                    for ch in range(NCH):
                        t, cp = ch // 2, ch % 2
                        last = mm(bk[cp * C:(cp + 1) * C, h, t * C:(t + 1) * C], AR[v][r, ch, 0, :],
                                  Bt[r, ch * C:(ch + 1) * C], start=True, stop=True)
                last.then_inc(s_M, 1)

            def blocks(out, lhsT, rhs_):
                for b in range(BLK):
                    for cp in range(2):
                        r = slice(cp * C, (cp + 1) * C)
                        last = mm(bk[r, out, b * C:(b + 1) * C], lhsT[r, b, :], rhs_[r, b, :], start=True, stop=True)
                return last

            def level_z(m, l):
                pe.wait_ge(s_Te, (NLEV + 1) * m + l + 1)
                blocks(0, Mab, Tt).then_inc(s_Z, 1)

            def level_t(m, l):
                pe.wait_ge(s_Ze, NLEV * m + l + 1)
                last = blocks(2, Tm, Zt)
                if l < NLEV - 1:
                    last = blocks(1, Zt, Tm)
                last.then_inc(s_T, 1)

            def scan(m, ch):
                v = m % 2
                t, cp = ch // 2, ch % 2
                pr = slice(cp * C, (cp + 1) * C)
                n = NCH * m + ch
                both = lambda x: x.rearrange("p (h x) -> p h x", x=HD)[:, 0:3:2, :]
                pe.wait_ge(s_Se, n + m + 1)
                if ch == 0:
                    pe.wait_ge(s_Te, (NLEV + 1) * (m + 1))
                mm(bk[pr, 3, 0:P], AR[v][:, ch, 0, :], S, start=True, stop=False)
                for h in range(2):
                    last = mm(bk[pr, 3, h * HD:(h + 1) * HD], MM[pr, h * TT + t, 2, :],
                              Vx[v][pr, t, h * P:h * P + HD], start=False, stop=(h == 1))
                last.then_inc(s_sc, 1)
                pe.wait_ge(s_sce, 2 * n + 1)
                for h in range(2):
                    last = mm(bk[pr, 0, h * HD:(h + 1) * HD], Tt[pr, h * TT + t, :], rhs[pr, h * HD:(h + 1) * HD],
                              start=True, stop=True)
                last.then_inc(s_sc, 1)
                pe.wait_ge(s_sce, 2 * n + 2)
                mm(bk[:, 1, 0:P], BK[v][pr, 0, t, :], both(SAx[pr]), start=True, stop=False)
                mm(bk[:, 1, 0:P], BK[v][pr, 1, t, :], both(Vx[v][pr, t, :]), start=False, stop=True).then_inc(s_sc, 1)
                y = bk[:, 2, ch * C:(ch + 1) * C]
                mm(y, S, AR[v][:, ch, 1, :], start=True, stop=False)
                for h in range(2):
                    mm(y, SAx[pr, h * HD:h * HD + P], MM[pr, h * TT + t, 1, :], start=False, stop=False)
                    last = mm(y, Vx[v][pr, t, h * HD:h * HD + P], MM[pr, h * TT + t, 3, :],
                              start=False, stop=(h == 1))
                last.then_inc(s_sc, 1)

            def norm(m):
                pe.wait_ge(s_gna, 3 * m + 1)
                mm(bk[:, 0, :], bones, yc, start=True, stop=True).then_inc(s_gnp, 1)
                pe.wait_ge(s_Se, (NCH + 1) * (m + 1))
                tr(bk[:, 3, 0:P], S, ident[:, :]).then_inc(s_So, 1)
                pe.wait_ge(s_gna, 3 * m + 2)
                mm(bk[:, 1, :], bones, ysq, start=True, stop=True).then_inc(s_gnp, 1)

            pe.wait_ge(s_mask, 112)
            for e in range(4):
                project(0, e)
            lora(0, 0)
            lora(0, 1)
            head_sums(0, 0)
            head_sums(0, 1)
            turn_v(0)
            turn_bk(0)
            for m in range(PAIRS):
                more = m + 1 < PAIRS
                chunk_products(m)
                if more:
                    project(m + 1, 0)
                for l in range(NLEV):
                    level_z(m, l)
                    if more:
                        if l < 3:
                            project(m + 1, l + 1)
                        else:
                            lora(m + 1, l - 3)
                    level_t(m, l)
                for ch in range(NCH):
                    scan(m, ch)
                    if more and ch == 0:
                        head_sums(m + 1, 0)
                    if more and ch == 4:
                        head_sums(m + 1, 1)
                    if more and ch == 5:
                        turn_v(m + 1)
                norm(m)
                if more:
                    turn_bk(m + 1)

            def arrived(n):
                pe.wait_ge(s_w[n % 3], 16 * (n // 3 + 1))

            pe.wait_ge(s_yT, PAIRS)
            pe.wait_ge(s_Soa, PAIRS)
            pe.wait_ge(s_pp, 3 * PAIRS)
            for q in range(6):
                last = tr(pj[0:HD, 0, q // 4, (q % 4) * P:(q % 4 + 1) * P], decbuf[:, q, :, :].rearrange("p m s -> p (m s)"),
                          ident[:, :])
            last.then_inc(s_dt, 1)
            for n in range(10):
                arrived(n)
                if n >= 2:
                    pe.wait_ge(s_adb, ADA_MT * (n - 1))
                w = ring[:, n % 3, :].rearrange("p (k e) -> p k e", k=KT)
                for t in range(ADA_MT):
                    for k in range(KT):
                        last = mm(bk[:, n % 2, 9 * t:9 * t + 9], w[:, k, t * P:(t + 1) * P], cT[:, k, :],
                                  start=(k == 0), stop=(k == KT - 1))
                last.then_inc(s_wu, 1)
                if n == 6:
                    pe.wait_ge(s_ydm, 32)
                    tr(pj[:, 1, 0, 0:HD], ydt[0:HD, :], ident[0:HD, 0:HD]).then_inc(s_ydt, 1)

            def sums(src, k, last):
                for a in range(2):
                    i = mm(bk[:, 2 + a, 0:HALF], ones[:, :], src[:, k, a * HALF:(a + 1) * HALF], start=(k == 0), stop=last)
                return i

            def out_tiles(layer, src):
                for t in range(KT):
                    if layer == 0:
                        n = SI[("w_out", t // 4)]
                        arrived(n)
                        w = ring[:, n % 3, :]
                        if t == 0:
                            pe.wait_ge(s_r1, 1)
                    else:
                        w = ring[:, t // 4, :]
                        pe.wait_ge(s_w[t // 4], 16 * (len(range(t // 4, NST, 3)) + 1))
                        if t == 0:
                            pe.wait_ge(s_pog, H + 1)
                    w = w.rearrange("p (k e) -> p k e", k=KT)
                    if t >= 2:
                        pe.wait_ge(s_oa, KT * layer + t - 1)
                    for k in range(KT):
                        for a in range(2):
                            last = mm(pj[:, t % 2, a, 0:HALF], w[:, k, (t % 4) * P:(t % 4 + 1) * P],
                                      src[:, k, a * HALF:(a + 1) * HALF], start=(k == 0), stop=(k == KT - 1))
                    last.then_inc(s_om, 1)
                for t in range(KT):
                    pe.wait_ge(s_nq, (0, 12)[layer] + t + 1)
                    last = sums(SQ, t, t == KT - 1)
                last.then_inc(s_ns, 1)

            out_tiles(0, R1)
            pe.wait_ge(s_nq, KT + 1)
            pe.wait_ge(s_nd, 1)
            for k in range(KT):
                last = sums(SQ, k, k == KT - 1)
            last.then_inc(s_ns, 1)

            n = SI[("kv_w_a", 0)]
            arrived(n)
            kw = ring[:, n % 3, 0:KT * 384].rearrange("p (k e) -> p k e", k=KT)
            pe.wait_ge(s_hh, 2)
            pe.wait_ge(s_oa, KT)

            def kv_turn(t):
                c = P if t < TT else NS
                pe.wait_ge(s_kvn, t + 1)
                pe.wait_ge(s_kvs, t)
                pe.wait_ge(s_nd, 2)
                for a in range(3):
                    last = tr(bk[:, 2, a * c:(a + 1) * c], kvn[0:c, t, a * P:(a + 1) * P], ident[0:c, 0:c])
                last.then_inc(s_kvt, 1)

            for t in range(5):
                c = P if t < TT else NS
                if t >= 2:
                    pe.wait_ge(s_kvn, t - 1)
                for k in range(KT):
                    last = mm(pj[0:c, t % 2, 0, 0:384], HK[:, k, t * P:t * P + c], kw[:, k, :],
                              start=(k == 0), stop=(k == KT - 1))
                last.then_inc(s_kvm, 1)
                if t >= 1:
                    kv_turn(t - 1)
            kv_turn(TT)

            pe.wait_ge(s_hha, KT)
            pe.wait_ge(s_kvn, 5)
            for t in range(QT + KT):
                g = 0 if t < QT else 1 + (t - QT) // 4
                n = SI[("b_w_in", g)]
                arrived(n)
                wid = 384 if g == 0 else 512
                e = t if g == 0 else (t - QT) % 4
                w = ring[:, n % 3, 0:KT * wid].rearrange("p (k e) -> p k e", k=KT)
                if 2 <= t < QT + 2:
                    pe.wait_ge(s_ba, t - 1)
                if t >= QT + 2:
                    pe.wait_ge(s_bd, t - 2 - QT + 1)
                for k in range(KT):
                    for a in range(2):
                        last = mm(pj[:, t % 2, a, 0:HALF], w[:, k, e * P:(e + 1) * P], H1[:, k, a * HALF:(a + 1) * HALF],
                                  start=(k == 0), stop=(k == KT - 1))
                last.then_inc(s_bm, 1)
                if t == QT:
                    pe.wait_ge(s_nq, KT + 1 + QT)
                    pe.wait_ge(s_kvs, 5)
                    for k in range(QT):
                        last = sums(SQ, k, k == QT - 1)
                    last.then_inc(s_ns, 1)
            pe.wait_ge(s_qn, 1)
            for u in range(16):
                n = SI[("w_q", u // 8)]
                arrived(n)
                w = ring[:, n % 3, 0:QT * D].rearrange("p (k e) -> p k e", k=QT)
                slot = (B_Q + u) % 2 if u < 8 else u % 2
                if u < 2:
                    pe.wait_ge(s_bd, KT - 1 + u)
                elif u < 8:
                    pe.wait_ge(s_ba, B_Q + u - 1)
                elif u < 10:
                    pe.wait_ge(s_ba, B_PE)
                else:
                    pe.wait_ge(s_bd, KT + (u - 8) // 2)
                e = u if u < 8 else (u - 8) // 2 + 4 * (u % 2)
                for k in range(QT):
                    for a in range(2):
                        last = mm(pj[:, slot, a, 0:HALF], w[:, k, e * P:(e + 1) * P], qa[:, k, a * HALF:(a + 1) * HALF],
                                  start=(k == 0), stop=(k == QT - 1))
                last.then_inc(s_bm, 1)
            n = SI[("uk", 0)]
            arrived(n)
            uk = ring[:, n % 3, 0:2048].rearrange("p (a e) -> p a e", a=2)
            ukT = ring[:, n % 3, 2048:4096].rearrange("p (h c) -> p h c", h=H)
            for h in range(H):
                if h >= 2:
                    pe.wait_ge(s_ba, B_PE + h - 1)
                for a in range(2):
                    last = mm(bk[:, h % 2, :], uk[:, a, h * P:(h + 1) * P], ckvT[:, a, 0:T], start=(a == 0), stop=(a == 1))
                last.then_inc(s_bm, 1)
            pe.wait_ge(s_uv, 16)
            for t in range(2 * TT):
                pe.wait_ge(s_ba, B_PE + H + t - 1)
                for a in range(2):
                    last = mm(bk[:, t % 2, :], ckvT[:, a, (t // 2) * P:(t // 2 + 1) * P],
                              UV[:, a, (t % 2) * 512:(t % 2) * 512 + 512], start=(a == 0), stop=(a == 1))
                last.then_inc(s_bm, 1)
            pe.wait_ge(s_nd, 3)
            for a in range(2):
                for h in range(H):
                    c0 = (a * H + h) * NS
                    last = mm(bk[:, 2, c0:c0 + NS], ukT[:, h, a * P:(a + 1) * P], QN[:, h, T:N], start=True, stop=True)
            last.then_inc(s_bm, 1)

            def prompt(h):
                r = slice((h % 2) * ROPE, (h % 2 + 1) * ROPE)
                for q in range(TT):
                    n = TT * h + q
                    w = (q + 1) * P
                    qs = slice(q * P, (q + 1) * P)
                    pe.wait_ge(s_sa1, n)
                    mm(bk[:, 0, 0:w], QN[:, h, qs], KN[:, h, 0:w], start=True, stop=False)
                    mm(bk[:, 0, 0:w], QP[r, h // 2, qs], kpeT[r, 0:w], start=False, stop=True).then_inc(s_sm, 1)
                    pe.wait_ge(s_sd2, n + 1)
                    pe.wait_ge(s_pa1, n)
                    for b in range(q + 1):
                        last = tr(bk[:, 1, b * P:(b + 1) * P], PN[:, b * P:(b + 1) * P], ident[:, :])
                    last.then_inc(s_pt1, 1)
                    pe.wait_ge(s_pa1, n + 1)
                    if q == 0:
                        pe.wait_ge(s_pog, h)
                    for b in range(q + 1):
                        last = mm(bk[:, 2, qs], VN[:, b, h * P:(h + 1) * P], PTb[:, b, :], start=(b == 0), stop=(b == q))
                    last.then_inc(s_po, 1)

            def decode(s):
                v = s % 2
                pe.wait_ge(s_ck[v], 32 * (s // 2 + 1))
                for g in range(NPAGES // 4):
                    n = 4 * s + g
                    pe.wait_ge(s_kta, n)
                    pe.wait_ge(s_ktd, n)
                    for k in range(4):
                        ks = slice(k * P, (k + 1) * P)
                        for a in range(2):
                            tr(pj[:, 0, a, ks], CK[v][:, 4 * g + k, a * P:(a + 1) * P], ident[:, :])
                        last = tr(pj[0:ROPE, 1, 0, ks], CR[v][:, 4 * g + k, :], ident[:, :])
                    last.then_inc(s_kt, 1)
                    pe.wait_ge(s_kta, n + 1)
                    pe.wait_ge(s_ktd, n + 1)
                    if g == 0:
                        pe.wait_ge(s_dsd, 3 * s)
                    for k in range(4):
                        ks = slice(k * P, (k + 1) * P)
                        out = pj[:, 1, 1, (4 * g + k) * H:(4 * g + k + 1) * H]
                        mm(out, KG[:, 0, ks], qlat[:, 0, :, s], start=True, stop=False)
                        mm(out, KG[:, 1, ks], qlat[:, 1, :, s], start=False, stop=False)
                        last = mm(out, KG[0:ROPE, 2, ks], qpd[0:ROPE, :, s], start=False, stop=True)
                    last.then_inc(s_ds, 1)
                out = pj[0:1, 1, 1, NPAGES * H:(NPAGES + 1) * H]
                me = slice(T + s, T + s + 1)
                mm(out, ckvT[:, 0, me], qlat[:, 0, :, s], start=True, stop=False)
                mm(out, ckvT[:, 1, me], qlat[:, 1, :, s], start=False, stop=False)
                mm(out, kpeT[0:ROPE, me], qpd[0:ROPE, :, s], start=False, stop=True).then_inc(s_ds, 1)
                pe.wait_ge(s_dsd, 3 * s + 3)
                pe.wait_ge(s_dvd, s)
                mm(bk[:, 3, 0:H], ones[:, :], dsum, start=True, stop=True).then_inc(s_dn, 1)
                pe.wait_ge(s_ckr, 16 * (s + 1))
                for a in range(2):
                    out = bk[:, 3, (2 + a) * H:(3 + a) * H]
                    for g in range(NPAGES):
                        mm(out, CK[v][:, g, a * P:(a + 1) * P], scb[:, g, :], start=(g == 0), stop=False)
                    last = mm(out, ckr[0:1, a * P:(a + 1) * P], scb[0:1, NPAGES, :], start=False, stop=True)
                last.then_inc(s_dv, 1)

            pe.wait_ge(s_ba, B_L + 1 - 8)
            pe.wait_ge(s_qpd, 32)
            for i in range(H):
                prompt(i)
                decode(i)
            pe.wait_ge(s_dvd, NS)
            for h in range(H):
                for a in range(2):
                    last = mm(bk[:, 3, P + h * NS:P + (h + 1) * NS], UV[:, a, h * P:(h + 1) * P], olat[:, a, h, :],
                              start=(a == 0), stop=(a == 1))
            last.then_inc(s_do, 1)
            out_tiles(1, OG)

        @block.gpsimd
        def _(pool):
            then, mark = counter(pool, s_pool)
            G = nc.gpsimd
            pool.wait_ge(s_const, 80)
            then(G.tensor_scalar(nw0, vecs[:, V_W0, :], -1.0, None, ALU.mult), s_zp)
            then(G.tensor_scalar(na0, vecs[:, V_A0, :], -1.0, None, ALU.mult), s_zp)
            then(G.tensor_scalar(omka, vecs[:, V_KA, :], -1.0, 1.0, ALU.mult, ALU.add), s_zp)
            then(G.memset(SAx[:, HD:2 * HD], 0.0), s_zero)
            then(G.memset(Vx[0].rearrange("p c x -> p c x")[:, :, HD:2 * HD], 0.0), s_zero)
            then(G.memset(Vx[1][:, :, HD:2 * HD], 0.0), s_zero)
            for m in range(PAIRS):
                v = m % 2
                col = lambda n: vecs[:, n, m:m + 1]
                pool.wait_ge(s_pa, 4 * m + 2)
                if m >= 1:
                    pool.wait_ge(s_pd, 4 * m)
                    pool.wait_ge(s_rd, 3 * m)
                then(G.tensor_scalar(kmT, aT, col(V_KA), omka[:, m:m + 1], ALU.mult, ALU.add))
                pool.wait_ge(s_ra, 7 * m + 2)
                then(G.tensor_tensor(kmT, kmT, kT, ALU.mult), s_pp)
                pool.wait_ge(s_pd, 4 * m + 2)
                then(G.tensor_tensor(bT, kkT, aT, ALU.mult), s_pp)
                pool.wait_ge(s_pa, 4 * m + 4)
                pool.wait_ge(s_rd, 3 * m + 3)
                for q, x in enumerate((rT, kmT, vT, kkT, bT, ecum, bon[v], gT[v])):
                    last = G.tensor_copy(decbuf[:, q, m, :], x[:, T:N])
                    if q < 7:
                        mark(last)
                then(last, s_pp)
            bi = lambda q: dq[:, q, :].unsqueeze(1).to_broadcast([P, HD, HD])
            bj = lambda x: x.unsqueeze(2).to_broadcast([P, HD, HD])
            pool.wait_ge(s_dq, 32)
            mark(G.tensor_tensor(Wd2, bj(dq[:, 2, :]), bi(1), ALU.mult), s_dp)
            pool.wait_ge(s_dd, 1)
            mark(G.tensor_tensor(Sd, Sd, bi(5), ALU.mult), s_dp)
            def reduce_max(s_):
                pool.wait_ge(s_dsd, 3 * s_ + 1)
                mark(G.partition_all_reduce(dmg, dmx, P, bass.bass_isa.ReduceOp.max), s_dsp)

            pool.wait_ge(s_pidx, 1)
            pool.wait_ge(s_bm, B_L + 1)
            for s_ in range(NS):
                v = s_ % 2
                if s_ >= 2:
                    pool.wait_ge(s_dvd, s_ - 1)
                off = bass.IndirectOffsetOnAxis(ap=pidx[:, s_:s_ + 1], axis=0)
                G.indirect_dma_start(ring[:, v, :], None, d["cache_c"], off).then_inc(s_ck[v], 16)
                G.indirect_dma_start(ring[:, 2, v * 1024:(v + 1) * 1024], None, d["cache_r"], off).then_inc(s_ck[v], 16)
                if s_ >= 1:
                    reduce_max(s_ - 1)
            reduce_max(NS - 1)

        @block.vector
        def _(dve):
            then, mark = counter(dve, s_dve)
            V = nc.vector
            dve.wait_ge(s_const, 80)

            def ada(g):
                dve.wait_ge(s_ada_mm, g + 1)
                mark(V.tensor_tensor(mod[:, ADA_MT * g:ADA_MT * (g + 1), :],
                                     bk[:, g % 2, 0:36].rearrange("p (t n) -> p t n", n=9),
                                     adab[:, ADA_MT * g:ADA_MT * (g + 1)].unsqueeze(2).to_broadcast([P, ADA_MT, 9]),
                                     ALU.add), s_ada_out)
            ada(0)
            ada(1)
            dve.wait_ge(s_ss, 1)
            then(V.tensor_scalar(two(stat), pjs[0], 1.0 / D, EPS, ALU.mult, ALU.add), s_ms)
            dve.wait_ge(s_rstd, 1)
            dve.wait_ge(s_x, 16)
            then(V.tensor_tensor(R1[:, :, :], R0[:, :, :], stat.unsqueeze(1).to_broadcast([P, KT, N]), ALU.mult))
            for g in range(2, 6):
                ada(g)
            dve.wait_ge(s_ada_out, 6)
            then(V.tensor_scalar(A0[:, :, :], mod[:, M_SC0:M_SC0 + KT, :], 1.0, None, ALU.add))
            then(V.tensor_tensor(A0[:, :, :], A0[:, :, :],
                                 vecs[:, V_PRE0, :].unsqueeze(2).to_broadcast([P, KT, 9]), ALU.mult))
            for k in range(KT):
                mark(V.tensor_scalar(R1[:, k, 0:T], R1[:, k, 0:T], A0[:, k, 0:1], mod[:, M_SH0 + k, 0:1],
                                     ALU.mult, ALU.add))
            then(V.tensor_tensor(R1[:, :, T:N], R1[:, :, T:N], A0[:, :, 1:9], ALU.mult))
            then(V.tensor_tensor(R1[:, :, T:N], R1[:, :, T:N], mod[:, M_SH0:M_SH0 + KT, 1:9], ALU.add))
            then(V.tensor_copy(shout, R1[:, :, T - 1:N]), s_shout)
            mark(V.tensor_tensor(R2[:, :, 1:T], R1[:, :, 0:T - 1], R1[:, :, 1:T], ALU.subtract))
            mark(V.tensor_scalar(R2[:, :, 0:1], R1[:, :, 0:1], -1.0, None, ALU.mult))
            dve.wait_ge(s_l1, 32)
            then(V.tensor_tensor(R2[:, :, T:N], shin, R1[:, :, T:N], ALU.subtract))
            for n, (e, dst) in enumerate(((4, 0), (5, 1), (2, 2), (3, 3), (0, 0), (1, 1))):
                if n >= 4:
                    dve.wait_ge(s_hid, n - 3)
                for k in range(KT):
                    last = V.scalar_tensor_tensor(XM[:, dst, k, :], R2[:, k, :], vecs[:, V_MU + e, k:k + 1],
                                                  R1[:, k, :], ALU.mult, ALU.add)
                    if k < KT - 1:
                        mark(last)
                then(last, s_xm)
            dve.wait_ge(s_hida, 1)
            then(V.tensor_scalar(lhid[0:LORA], lhid[0:LORA], -2.0, 1.0, ALU.mult, ALU.add), s_hidr)

            def chunk(x, t0=0):
                return x[:, 0:T].rearrange("p (c t) -> p c t", c=NCH)

            def prep(m, part):
                v = m % 2
                col = lambda n: vecs[:, n, m:m + 1]
                if part == "g":
                    dve.wait_ge(s_pa, 4 * m + 1)
                    if m >= 1:
                        dve.wait_ge(s_pp, 3 * m)
                        dve.wait_ge(s_pjm, NUSE * m)
                    then(V.tensor_tensor(two(gT[v]), pjs[1], two(gT[v]), ALU.mult), s_rd)
                if part == "cum":
                    dve.wait_ge(s_pa, 4 * m + 2)
                    dve.wait_ge(s_mask, 112)
                    then(V.tensor_tensor_scan(cum, scanm, sg, 0.0, ALU.mult, ALU.add))
                    then(V.tensor_tensor(cumx, cum, sg, ALU.subtract), s_pd)
                if part == "ss":
                    dve.wait_ge(s_pjm, NUSE * m + U_SS + 1)
                    then(V.tensor_scalar(two(sqk), pjs[0], 1e-24, None, ALU.max), s_rd)
                if part == "kk":
                    dve.wait_ge(s_pa, 4 * m + 3)
                    then(V.scalar_tensor_tensor(kkT, kT, col(V_KK), sqk, ALU.mult, ALU.mult), s_pd)
                if part == "rk":
                    dve.wait_ge(s_pp, 3 * m + 1)
                    then(V.scalar_tensor_tensor(tmb, rT, col(V_RK), kmT, ALU.mult, ALU.mult), s_pd)
                if part == "bon":
                    dve.wait_ge(s_pjm, NUSE * m + U_BO + 1)
                    then(V.tensor_tensor(two(bon[v]), pjs[1], two(vT), ALU.mult), s_rd)
                if part == "ar":
                    dve.wait_ge(s_pa, 4 * m + 4)
                    then(V.tensor_tensor(AR[v][:, :, 0, :], chunk(kkT), chunk(cumx), ALU.mult))
                    then(V.tensor_tensor(AR[v][:, :, 1, :], chunk(rT), chunk(ecum), ALU.mult))
                    then(V.tensor_copy(pc[:, v, :], ecum[:, C - 1:T:C]))
                if part == "bt":
                    dve.wait_ge(s_pp, 3 * m + 2)
                    then(V.tensor_tensor(Bt, bT[:, 0:T], einv[:, 0:T], ALU.mult))
                    then(V.tensor_tensor(Kt_, kmT[:, 0:T], einv[:, 0:T], ALU.mult))
                if part == "bh":
                    pcb = pc[:, v, :].unsqueeze(2).to_broadcast([P, NCH, C])
                    then(V.tensor_tensor(chunk(cum), chunk(Bt), pcb, ALU.mult))
                    then(V.tensor_tensor(chunk(sqk), chunk(Kt_), pcb, ALU.mult), s_pd)

            def masks(m):
                if m == 0:
                    dve.wait_ge(s_store, 16)
                for n in range(4):
                    half, h = n // 2, n % 2
                    dve.wait_ge(s_M, 5 * m + n + 1)
                    b0 = h * TT + 2 * half
                    then(V.tensor_tensor(MM[:, b0:b0 + 2, :, :].rearrange("p b q t -> p b (q t)"),
                                         bk[:, n, :].rearrange("p (b x) -> p b x", b=2),
                                         maskM.unsqueeze(1).to_broadcast([P, 2, 256]), ALU.mult), s_Me)
                dve.wait_ge(s_M, 5 * m + 5)
                then(V.tensor_tensor(Mab.rearrange("p (h b) t -> p h b t", h=2),
                                     bk[:, 0:2, 0:256].rearrange("p h (b t) -> p h b t", b=TT),
                                     lowm.unsqueeze(1).unsqueeze(1).to_broadcast([P, 2, TT, C]), ALU.mult), s_Me)
                idb = id64.unsqueeze(1).to_broadcast([P, BLK, C])
                for x, dst, a in ((Mab, Tm, 0), (MM[:, :, 0, :], Tt, 1)):
                    then(V.scalar_tensor_tensor(dst, x, -1.0, lv1[:, a, :].unsqueeze(1).to_broadcast([P, BLK, C]),
                                                ALU.mult, ALU.mult))
                    then(V.tensor_tensor(dst, dst, idb, ALU.add), s_Te if a else None)

            def level_z(m, l):
                dve.wait_ge(s_Z, NLEV * m + l + 1)
                then(V.tensor_tensor(Zt, bk[:, 0, :].rearrange("p (b t) -> p b t", b=BLK),
                                     lvm[:, l, :].unsqueeze(1).to_broadcast([P, BLK, C]), ALU.mult), s_Ze)

            def level_t(m, l):
                dve.wait_ge(s_T, NLEV * m + l + 1)
                if l < NLEV - 1:
                    then(V.tensor_tensor(Tm, Tm, bk[:, 1, :].rearrange("p (b t) -> p b t", b=BLK), ALU.subtract))
                then(V.tensor_tensor(Tt, Tt, bk[:, 2, :].rearrange("p (b t) -> p b t", b=BLK), ALU.subtract), s_Te)

            def scan(m, ch):
                v = m % 2
                n = 4 * (NCH * m + ch)
                dve.wait_ge(s_sc, n + 3)
                then(V.tensor_tensor(stmp, bk[:, 1, 0:P], bones, ALU.mult))
                dve.wait_ge(s_sc, n + 4)
                then(V.scalar_tensor_tensor(S, S, pc[:, v, ch:ch + 1], stmp, ALU.mult, ALU.add), s_Se)

            def norm(m):
                v = m % 2
                dve.wait_ge(s_gnp, 2 * m + 1)
                then(V.scalar_tensor_tensor(yc, bk[:, 0, :], -1.0 / HD, yc, ALU.mult, ALU.add), s_gnd)
                dve.wait_ge(s_gna, 3 * m + 3)
                then(V.tensor_tensor(yc, yc, ysq, ALU.mult))
                then(V.tensor_scalar(yc, yc, vecs[:, V_GNW, m:m + 1], vecs[:, V_GNB, m:m + 1], ALU.mult, ALU.add))
                then(V.tensor_tensor(yc, yc, bon[v][:, 0:T], ALU.add))
                then(V.tensor_tensor(R1[:, m, 0:T], yc, gT[v][:, 0:T], ALU.mult), s_yT)

            for part in ("g", "cum", "ss", "kk", "rk", "bon", "ar", "bt", "bh"):
                prep(0, part)
            for m in range(PAIRS):
                more = m + 1 < PAIRS
                if m >= 1:
                    dve.wait_ge(s_So, m)
                then(V.memset(S, 0.0), s_Se)
                masks(m)
                for l in range(NLEV):
                    level_z(m, l)
                    if more and l == 3:
                        prep(m + 1, "g")
                    level_t(m, l)
                if more:
                    prep(m + 1, "cum")
                for ch in range(NCH):
                    scan(m, ch)
                    if more and 1 <= ch <= 7:
                        prep(m + 1, (None, "ss", "kk", "rk", "bon", "ar", None, "bt")[ch])
                if more:
                    prep(m + 1, "bh")
                norm(m)

            bi = lambda q: dq[:, q, :].unsqueeze(1).to_broadcast([P, HD, HD])
            bj = lambda x: x.unsqueeze(2).to_broadcast([P, HD, HD])
            dve.wait_ge(s_pt, 16)
            dve.wait_ge(s_cb, 128)
            then(V.tensor_scalar(pidx[:, :], ptab[:, :], 8.0, prow[:, 0:1], ALU.mult, ALU.add), s_pidx)
            dve.wait_ge(s_dq, 32)
            dve.wait_ge(s_sd, 16)
            then(V.tensor_tensor(Wd1, Sd, bi(3), ALU.mult), s_dd)
            then(V.tensor_reduce(sa, Wd1, AX_X, ALU.add))
            then(V.tensor_tensor(Wd1, bj(sa), bi(4), ALU.mult), s_dd)
            dve.wait_ge(s_dp, 1)
            then(V.tensor_tensor(Wd2, Wd2, Wd1, ALU.subtract), s_dd)
            dve.wait_ge(s_dp, 2)
            then(V.tensor_tensor(Sd, Sd, Wd2, ALU.add), s_dd)
            then(V.tensor_tensor(Wd1, Sd, bi(0), ALU.mult))
            then(V.tensor_reduce(yd, Wd1, AX_X, ALU.add))
            then(V.bn_stats(bst, yd))
            then(V.bn_aggr(bag, bst), s_dd)
            dve.wait_ge(s_dr, 1)
            then(V.tensor_scalar(yd, yd, bag[:, 0:1], rsd, ALU.subtract, ALU.mult), s_dd)
            dve.wait_ge(s_ydt, 1)
            r1d = R1[:, :, T:N]
            bc = lambda x: x.unsqueeze(2).to_broadcast([P, KT, NS])
            then(V.tensor_tensor(r1d, pj[:, 1, 0, 0:HD].rearrange("p (m s) -> p m s", m=PAIRS), bc(vecs[:, V_GNW, :]), ALU.mult))
            then(V.tensor_tensor(r1d, r1d, bc(vecs[:, V_GNB, :]), ALU.add))
            then(V.tensor_tensor(r1d, r1d, decbuf[:, 6, :, :], ALU.add))
            then(V.tensor_tensor(r1d, r1d, decbuf[:, 7, :, :], ALU.mult), s_r1)

            nn = [0]

            def mean(width):
                nn[0] += 1
                dve.wait_ge(s_ns, nn[0])
                then(V.tensor_scalar(two(st), bk[:, 2:4, 0:HALF], 1.0 / width, EPS, ALU.mult, ALU.add), s_nd)
                return nn[0]

            all_k = lambda x: x.unsqueeze(1).to_broadcast([P, KT, N])
            b9 = lambda x: x.unsqueeze(2).to_broadcast([P, KT, 9])

            def residual(layer, gate, post):
                n = mean(D)
                then(V.tensor_tensor(A0[:, :, :], mod[:, gate:gate + KT, :], b9(vecs[:, post, :]), ALU.mult))
                dve.wait_ge(s_na, n)
                dve.wait_ge(s_oa, KT * (layer + 1))
                then(V.tensor_tensor(Y, Y, all_k(st), ALU.mult))
                dve.wait_ge(s_xr, 16)
                for k in range(KT):
                    mark(V.scalar_tensor_tensor(R0[:, k, 0:T], Y[:, k, 0:T], A0[:, k, 0:1], R0[:, k, 0:T], ALU.mult, ALU.add))
                then(V.tensor_tensor(Y[:, :, T:N], Y[:, :, T:N], A0[:, :, 1:9], ALU.mult))
                then(V.tensor_tensor(R0[:, :, T:N], R0[:, :, T:N], Y[:, :, T:N], ALU.add), s_res)

            dve.wait_ge(s_adb, 40)
            residual(0, M_G0, V_POST0)
            n = mean(D)
            for a, sc, g in ((A0, M_SC1, V_PRE1), (A1, M_SCK, V_KVN)):
                then(V.tensor_scalar(a[:, :, :], mod[:, sc:sc + KT, :], 1.0, None, ALU.add))
                then(V.tensor_tensor(a[:, :, :], a[:, :, :], b9(vecs[:, g, :]), ALU.mult))
            dve.wait_ge(s_na, n)
            then(V.tensor_tensor(HN, R0[:, :, :], all_k(st), ALU.mult), s_hh)
            for k in range(KT):
                mark(V.tensor_scalar(HK[:, k, 0:T], HN[:, k, 0:T], A1[:, k, 0:1], mod[:, M_SHK + k, 0:1], ALU.mult, ALU.add))
            dve.wait_ge(s_dso, 16)
            for x, a, sh, nm in ((H1, A0, M_SH1, None), (HK, A1, M_SHK, s_hh)):
                then(V.tensor_tensor(x[:, :, T:N], HN[:, :, T:N], a[:, :, 1:9], ALU.mult))
                then(V.tensor_tensor(x[:, :, T:N], x[:, :, T:N], mod[:, sh:sh + KT, 1:9], ALU.add), nm)

            for t in range(5):
                c = P if t < TT else NS
                ps = pj[0:c, t % 2, 0, :]
                dve.wait_ge(s_kva, t + 1)
                then(V.tensor_scalar(kss[0:c, 1:2], kss[0:c, 0:1], 1.0 / KVL, EPS, ALU.mult, ALU.add), s_kvd)
                mark(V.tensor_tensor(kvn[0:c, t, 256:320], ps[:, 256:320], cosN[0:c, t, :], ALU.mult))
                then(V.tensor_tensor(rt64[0:c], ps[:, 320:384], sinN[0:c, t, :], ALU.mult))
                then(V.tensor_tensor(kvn[0:c, t, 256:320], kvn[0:c, t, 256:320], rt64[0:c], ALU.add))
                mark(V.tensor_copy(kvn[0:c, t, 320:384], kvn[0:c, t, 256:320]))
                dve.wait_ge(s_kvr, t + 1)
                then(V.scalar_tensor_tensor(kvn[0:c, t, 0:KVL], ps[:, 0:KVL], kss[0:c, 1:2], kvg[0:c], ALU.mult, ALU.mult), s_kvn)

            n = mean(QL)
            for t in range(KT):
                dve.wait_ge(s_ba, QT + t + 1)
                then(V.tensor_tensor(two(GATE[:, t, :]), two(GATE[:, t, :]), pjs[(QT + t) % 2], ALU.mult), s_bd)
                if t == 0:
                    dve.wait_ge(s_na, n)
                    then(V.tensor_tensor(qa, qa, st.unsqueeze(1).to_broadcast([P, QT, N]), ALU.mult))
                    for k in range(QT):
                        last = V.tensor_scalar(qa[:, k, :], qa[:, k, :], qng[:, k:k + 1], None, ALU.mult)
                        if k < QT - 1:
                            mark(last)
                    then(last, s_qn)
            for i in range(4):
                dve.wait_ge(s_bm, B_PE + 2 * i + 2)
                then(V.tensor_tensor(two(QP[:, i, :]), pjs[0], two(cosT), ALU.mult))
                then(V.tensor_tensor(two(rtmp), pjs[1], two(sinT), ALU.mult))
                then(V.tensor_tensor(QP[:, i, :], QP[:, i, :], rtmp, ALU.add), s_bd)

            def prompt(h):
                for q in range(TT):
                    n = TT * h + q
                    w = (q + 1) * P
                    dve.wait_ge(s_sm, n + 1)
                    dve.wait_ge(s_sa1, n)
                    then(V.tensor_tensor(bk[:, 0, w - P:w], bk[:, 0, w - P:w], causal, ALU.add))
                    then(V.tensor_reduce(mx[:, 0:1], bk[:, 0, 0:w], AX_X, ALU.max))
                    then(V.tensor_scalar(nmx[:, 0:1], mx[:, 0:1], -SCALE, None, ALU.mult), s_sd1)
                    dve.wait_ge(s_sa1, n + 1)
                    then(V.reciprocal(mx[:, 1:2], den[:, 0:1]))
                    then(V.tensor_scalar(PN[:, 0:w], PN[:, 0:w], mx[:, 1:2], None, ALU.mult), s_sd2)
                dve.wait_ge(s_po, TT * (h + 1))
                then(V.tensor_tensor(OG[:, h, 0:T], bk[:, 2, :], GATE[:, h, 0:T], ALU.mult), s_pog)

            def decode(s):
                for g in range(NPAGES // 4):
                    n = 4 * s + g
                    dve.wait_ge(s_kt, n + 1)
                    dve.wait_ge(s_ds, 5 * s + g)
                    mark(V.tensor_copy(KG[0:ROPE, 2, :], pj[0:ROPE, 1, 0, :]), s_ktd)
                dve.wait_ge(s_ds, 5 * s + 5)
                dve.wait_ge(s_dv, s)
                mark(V.tensor_copy(scb[:, 0:NPAGES, :], pj[:, 1, 1, 0:NPAGES * H].rearrange("p (g h) -> p g h", g=NPAGES)))
                then(V.memset(scb[:, NPAGES, :], NEG))
                then(V.tensor_copy(scb[0:1, NPAGES, :], pj[0:1, 1, 1, NPAGES * H:(NPAGES + 1) * H]))
                then(V.tensor_reduce(dmx, scb.rearrange("p g h -> p h g"), AX_X, ALU.max), s_dsd)
                dve.wait_ge(s_dsp, s + 1)
                then(V.tensor_tensor(scb, scb, dmg.unsqueeze(1).to_broadcast([P, NPAGES + 1, H]), ALU.subtract), s_dsd)
                dve.wait_ge(s_dsa, s + 1)
                then(V.tensor_reduce(dsum, scb.rearrange("p g h -> p h g"), AX_X, ALU.add), s_dsd)
                dve.wait_ge(s_dn, s + 1)
                dve.wait_ge(s_dv, s + 1)
                then(V.reciprocal(drc, bk[:, 3, 0:H]))
                then(V.tensor_tensor(olat[:, :, :, s], bk[:, 3, 2 * H:4 * H].rearrange("p (a h) -> p a h", a=2),
                                     drc.unsqueeze(1).to_broadcast([P, 2, H]), ALU.mult), s_dvd)

            for i in range(H):
                prompt(i)
                decode(i)
            dve.wait_ge(s_do, 1)
            then(V.tensor_tensor(OG[:, :, T:N], bk[:, 3, P:P + H * NS].rearrange("p (h s) -> p h s", h=H),
                                 GATE[:, :, T:N], ALU.mult), s_pog)
            residual(1, M_G1, V_POST1)


def host_layout(i):
    f = np.float32

    def feat(a):
        a = np.asarray(a)
        lead = a.shape[:-1]
        a = a.reshape(*lead, KT, P)
        return np.moveaxis(a, -1, 0)

    def cols(a, width):
        k, n = a.shape
        return np.ascontiguousarray(a.reshape(k // P, P, n // width, width).transpose(2, 1, 0, 3))

    r = {}
    x = np.concatenate([i["x_prompt"][0], i["x_sample"][:, 0]], 0)
    r["xT"] = np.ascontiguousarray(x.T.reshape(KT, P, N).transpose(1, 0, 2))
    c = np.concatenate([i["c_prompt"], i["c_sample"]], 0)
    r["cT"] = np.ascontiguousarray(c.T.reshape(KT, P, 1 + NS).transpose(1, 0, 2))
    r["shiftT"] = np.ascontiguousarray(i["state_shift"][0].T.reshape(KT, P, NS).transpose(1, 0, 2))
    ada = np.concatenate([i["ada_w"][0], i["ada_w"][1], i["kv_ada_w"]], 1)
    r["ada"] = cols(ada, ADA_COLS).reshape(ADA_GROUPS, P, 4096)
    r["adab"] = np.ascontiguousarray(np.concatenate([i["ada_b"][0], i["ada_b"][1], i["kv_ada_b"]]).reshape(MOD_TILES, P).T)
    vs = [i["norm_pre"][0], i["norm_pre"][1], i["norm_post"][0], i["norm_post"][1], *i["a_mu"][0],
          i["a_w0"][0], i["a_a0"][0], i["a_k_k"][0], i["a_k_a"][0], i["a_r_k"][0].reshape(-1),
          i["a_gn_w"][0], i["a_gn_b"][0], i["kv_norm"]]
    r["vecs"] = np.ascontiguousarray(np.stack([v.reshape(KT, P).T for v in vs], 1))
    w = i["a_w_in"][0]
    r["w_in"] = np.ascontiguousarray(w.reshape(4, KT, P, PAIRS, P).transpose(3, 2, 0, 1, 4)).reshape(PAIRS, P, 4096)
    l1 = np.concatenate([i["a_w1"][0], i["a_a1"][0]], 1)
    r["lora1"] = np.ascontiguousarray(l1.reshape(KT, P, P).transpose(1, 0, 2))
    l2 = np.concatenate([i["a_w2"][0], i["a_a2"][0]], 0)
    r["lora2"] = np.ascontiguousarray(l2.reshape(P, PAIRS, P).transpose(1, 0, 2))
    st = i["state_wkv"][0].reshape(NS, PAIRS, 2, HD, HD).transpose(2, 1, 0, 3, 4)
    r["Sd"] = np.ascontiguousarray(st.reshape(P, HD, HD))
    r["w_out"] = cols(i["a_w_out"][0], 512).reshape(2, P, 4096)
    r["b_w_out"] = cols(i["b_w_out"][0], 512).reshape(2, P, 4096)
    swap = np.r_[ROPE // 2:ROPE, 0:ROPE // 2]
    kva = i["kv_w_a"]
    r["kv_w_a"] = cols(np.concatenate([kva, kva[:, KVL + swap]], 1), 384).reshape(1, P, KT * 384)
    bw = i["b_w_in"][0]
    pad = np.zeros((P, KT * 128), f)
    r["b_w_in"] = np.stack([np.concatenate([cols(bw[:, 0:QL], QL).reshape(P, KT * QL), pad], 1),
                            *cols(bw[:, QL:], 512).reshape(2, P, 4096)])
    wq = i["b_w_q"][0]
    pe = wq[:, :, NOPE:]
    r["w_q"] = np.stack([cols(wq[:, :, 0:NOPE].reshape(QL, H * NOPE), H * NOPE).reshape(P, QT * D),
                         cols(np.concatenate([pe.reshape(QL, -1), pe[:, :, swap].reshape(QL, -1)], 1), D).reshape(P, QT * D)])
    kvb = i["kv_w_b"]
    uk = kvb[:, :, 0:NOPE]
    r["uk"] = np.concatenate([uk.reshape(2, P, H * NOPE).transpose(1, 0, 2).reshape(P, -1),
                              uk.transpose(2, 1, 0).reshape(P, -1)], 1)[None]
    r["uv"] = np.ascontiguousarray(kvb[:, :, NOPE:].reshape(2, P, H * P).transpose(1, 0, 2))
    r["kvg"] = np.broadcast_to(i["kv_a_norm"], (P, KVL)).copy()
    r["qng"] = np.ascontiguousarray(i["b_q_norm"][0].reshape(QT, P).T)
    r["page_table"] = np.ascontiguousarray(np.repeat(i["page_table"].T, PAGE // 16, axis=0))
    r["cache_c"] = i["cache_kv_latent"].reshape(-1, NPAGES * KVL)
    r["cache_r"] = i["cache_k_rope"].reshape(-1, NPAGES * ROPE)
    inv = f(ROPE_THETA) ** (-np.arange(ROPE // 2, dtype=f) / f(ROPE // 2))
    pos = np.concatenate([np.arange(T), np.full(NS, PAST)]).astype(f)
    ang = pos[:, None] * inv[None, :]
    cs = np.concatenate([np.cos(ang), np.cos(ang)], 1).astype(f)
    sn = np.concatenate([-np.sin(ang), np.sin(ang)], 1).astype(f)
    r["cosT"], r["sinT"] = (np.concatenate([a.T, a.T], 0).copy() for a in (cs, sn))
    r["cosN"], r["sinN"] = (np.ascontiguousarray(np.concatenate([a, np.zeros((5 * P - N, ROPE), f)], 0)
                            .reshape(5, P, ROPE).transpose(1, 0, 2)) for a in (cs, sn))
    r["causal"] = np.where(np.arange(P)[None, :] <= np.arange(P)[:, None], 0, NEG).astype(f)
    r["prow"] = (np.arange(P) % 8).astype(f)[:, None]
    r["ident"] = np.eye(P, dtype=f)
    r["ones"] = np.ones((P, P), f)
    s, t = np.meshgrid(np.arange(P) % C, np.arange(C), indexing="ij")
    r["maskM"] = np.concatenate([t > s, t >= s, t > s, t >= s], 1).astype(f)
    r["lowm"] = (t < s).astype(f)
    off = lambda a, b, m: (a // (2 * m) == b // (2 * m)) & (a % (2 * m) >= m) & (b % (2 * m) < m)
    r["lv1"] = np.stack([off(s, t, 1), off(t, s, 1)], 1).astype(f)
    r["lvm"] = np.stack([off(t, s, m) for m in LEVELS], 1).astype(f)
    r["id64"] = (s == t).astype(f)
    hb = np.arange(P) // HD
    r["bones"] = (hb[:, None] == hb[None, :]).astype(f)
    r["scanm"] = np.broadcast_to(np.where(np.arange(N) < T, np.arange(N) % C != 0, False).astype(f), (P, N)).copy()
    return r


OUTS = {"shift": (P, KT, 1 + NS), "wkv_p": (2 * PAIRS, HD, HD), "wkv_s": (P, HD, HD), "ckv": (N, KVL),
        "kpe": (N, ROPE), "y": (P, KT, N)}


def kernel(**inputs):
    import concourse.bacc as bacc
    from concourse.bass_utils import run_bass_kernel_spmd

    nc = bacc.Bacc("TRN2", target_bir_lowering=False, num_devices=1)
    arrays = host_layout({k: np.asarray(v) for k, v in inputs.items()})
    d = {k: nc.dram_tensor(f"in_{k}", a.shape, mybir.dt.from_np(a.dtype), kind="ExternalInput").ap()
         for k, a in arrays.items()}
    o = {k: nc.dram_tensor(f"out_{k}", s, F32, kind="ExternalOutput").ap() for k, s in OUTS.items()}
    build(nc, d, o)
    r = run_bass_kernel_spmd(nc, [{f"in_{k}": a for k, a in arrays.items()}], core_ids=[0]).results[0]
    sh = np.asarray(r["out_shift"]).transpose(2, 1, 0).reshape(1 + NS, D)
    y = np.asarray(r["out_y"]).transpose(2, 1, 0).reshape(N, D)
    wkv_s = np.asarray(r["out_wkv_s"]).reshape(2, PAIRS, NS, HD, HD).transpose(2, 1, 0, 3, 4).reshape(1, NS, 2 * PAIRS, HD, HD)
    ckv, kpe = np.asarray(r["out_ckv"]), np.asarray(r["out_kpe"])
    return (y[None, 0:T], y[T:, None], np.asarray(r["out_wkv_p"])[None, None], sh[0][None, None],
            ckv[None, 0:T], kpe[None, 0:T], wkv_s, sh[1:][None], ckv[T:, None], kpe[T:, None])
```

```python
from contextlib import ExitStack

import numpy as np

import concourse.bass as bass
from concourse import mybir

F32 = mybir.dt.float32
I32 = mybir.dt.int32
ALU = mybir.AluOpType
ACT = mybir.ActivationFunctionType
AX_X = mybir.AxisListType.X

P = 128
D = 1024
KT = D // P
T = 512
NS = 8
N = T + NS
HALF = N // 2
HD = 64
PAIRS = D // P
C = 64
NCH = T // C
TT = T // P
BLK = 2 * TT
LEVELS = (2, 4, 8, 16, 32)
NLEV = len(LEVELS)
LORA = 64
GN_EPS = 64e-5
EPS = 1e-6
H = 8
NOPE = 128
ROPE = 64
QL = 384
QT = QL // P
KVL = 256
ROPE_THETA = 10000.0
SCALE = float(NOPE + ROPE) ** -0.5
PAGE = 128
NPAGES = 16
NPHYS = 160
PAST = NPAGES * PAGE
NEG = -1e30
(V_PRE0, V_PRE1, V_POST0, V_POST1, V_MU, V_W0, V_A0, V_KK, V_KA, V_RK, V_GNW, V_GNB, V_KVN) = (
    0, 1, 2, 3, 4, 10, 11, 12, 13, 14, 15, 16, 17)
NVEC = 18
ADA_COLS = 512
ADA_GROUPS = 8 * D // ADA_COLS
ADA_MT = ADA_COLS // P
MOD_TILES = 8 * KT
M_SH0, M_SC0, M_G0, M_SH1, M_SC1, M_G1, M_SHK, M_SCK = (KT * i for i in range(8))
E05 = float(np.exp(np.float32(-0.5)))
ADA_FIRST = 4
ADA_PAIRS = PAIRS
U_R, U_K, U_V, U_G, U_W, U_A, U_SS, U_BO, U_TV, U_TB = range(10)
NUSE = 10
ARENA = 9580


def build(nc, d, o):
    ctx = ExitStack()
    with ctx:
        def sb(name, shape, dt=F32):
            return ctx.enter_context(nc.sbuf_tensor(name, shape, dt))

        def sem(name):
            return ctx.enter_context(nc.semaphore(name))

        ring = sb("ring", [P, 3, 4096])
        R0 = sb("R0", [P, KT, N])
        R1 = sb("R1", [P, KT, N])
        R2 = sb("R2", [P, KT, N])
        XM = sb("XM", [P, 4, KT, N])
        vecs = sb("vecs", [P, NVEC, KT])
        ident = sb("ident", [P, P])
        ones = sb("ones", [P, P])
        cT = sb("cT", [P, KT, 1 + NS])
        adab = sb("adab", [P, MOD_TILES])
        mod = sb("mod", [P, MOD_TILES, 1 + NS])
        A0 = sb("A0", [P, KT, 1 + NS])
        decbuf = sb("decbuf", [P, 8, PAIRS, NS])
        arena = sb("arena", [P, ARENA])

        def cutter(flat, size):
            used = [0]

            def cut(n):
                a = flat[:, used[0]:used[0] + n]
                used[0] += n
                assert used[0] <= size, (used[0], size)
                return a
            return cut

        cutA = cutter(arena, ARENA)
        cutX = cutter(ring[:, 2, :], 4096)
        cut0 = cutter(R0[:, :, :].rearrange("p a b -> p (a b)"), KT * N)
        cut2 = cutter(R2[:, :, :].rearrange("p a b -> p (a b)"), KT * N)

        maskM = cutA(256)
        lowm = cutA(C)
        lv1 = cutA(2 * C).rearrange("p (a t) -> p a t", a=2)
        lvm = cutA(NLEV * C).rearrange("p (l t) -> p l t", l=NLEV)
        id64 = cutA(C)
        bones = cutA(P)
        scanm = cutA(N)
        omka, nw0, na0 = cutA(KT), cutA(KT), cutA(KT)
        lhid = cutA(N)
        lora2 = cutA(2 * P).rearrange("p (s e) -> p s e", s=2)
        stat = arena[:, ARENA - N:ARENA]
        SAx = cutA(192)
        rhs = cutA(P)
        S = cutA(P)
        stmp = cutA(P)
        Sout = rhs
        AR = [cutA(2 * T).rearrange("p (c a t) -> p c a t", c=NCH, a=2) for _ in range(2)]
        Vx = [cutA(TT * 192).rearrange("p (c x) -> p c x", c=TT) for _ in range(2)]
        BK = [cutA(2 * T).rearrange("p (a c j) -> p a c j", a=2, c=TT) for _ in range(2)]
        pc = cutA(2 * NCH).rearrange("p (s c) -> p s c", s=2)
        MM = cutX(BLK * 256).rearrange("p (b q t) -> p b q t", b=BLK, q=4)
        Mab, Tm, Tt, Zt = (cutX(BLK * C).rearrange("p (b t) -> p b t", b=BLK) for _ in range(4))
        adarow = Mab.rearrange("p b t -> p (b t)")[0:9]
        rT, kT, vT, bT, kmT = (cut0(N) for _ in range(5))
        wa = cut0(2 * N).rearrange("p (a n) -> p a n", a=2)
        sg, aT = wa[:, 0, :], wa[:, 1, :]
        cum, cumx = cut2(N), sg
        ecum, einv = cut0(N), cut2(N)
        kkT, sqk = cut2(N), cut2(N)
        tmb = sqk
        gT = [cut2(N) for _ in range(2)]
        bon = [cut2(N) for _ in range(2)]
        Bt, Kt_ = cutA(T), cutA(T)
        yc = Zt.rearrange("p b t -> p (b t)")
        ysq = Tm.rearrange("p b t -> p (b t)")
        lora1 = ring[:, 2, 0:KT * P].rearrange("p (k e) -> p k e", k=KT)
        shin = ring[:, 2, KT * P:KT * P + KT * NS].rearrange("p (k n) -> p k n", k=KT)
        shout = ring[:, 2, 1200:1200 + KT * (1 + NS)].rearrange("p (k n) -> p k n", k=KT)

        pj = ctx.enter_context(nc.psum_tensor("pj", [P, 2, 2, 512], F32))
        bk = ctx.enter_context(nc.psum_tensor("bk", [P, 4, 512], F32))
        pjs = [pj[:, s, :, 0:HALF] for s in range(2)]

        def two(ap):
            return ap.rearrange("p (a n) -> p a n", a=2)

        Sd = XM[:, 0, :, :].rearrange("p k n -> p (k n)")[:, 0:HD * HD].rearrange("p (i j) -> p i j", i=HD)
        Wd1 = XM[:, 1, :, :].rearrange("p k n -> p (k n)")[:, 0:HD * HD].rearrange("p (i j) -> p i j", i=HD)
        Wd2 = XM[:, 2, :, :].rearrange("p k n -> p (k n)")[:, 0:HD * HD].rearrange("p (i j) -> p i j", i=HD)
        cut0b = cutter(R2[:, :, :].rearrange("p a b -> p (a b)"), KT * N)
        dturn = cut0b(6 * P).rearrange("p (q j) -> p q j", q=6)
        dq = cut0b(6 * HD).rearrange("p (q j) -> p q j", q=6)
        sa = cut0b(HD)
        yd = cut0b(HD)
        bst, bag, rsd = cut0b(6), cut0b(2), cut0b(1)
        ydt = cut0b(P)
        Y = XM[:, 3, :, :]
        GATE = XM[:, 3, :, :]
        HN = XM[:, 1, :, :]
        HK = XM[:, 2, :, :]
        H1 = XM[:, 0, :, :]
        SQ = R2[:, :, :]
        QN = XM[:, 2, :, :]
        R2g = R2[:, :, :].rearrange("p a b -> p (a b)")
        QP = R2g[:, 0:4 * N].rearrange("p (i n) -> p i n", i=4)
        UV = R2g[:, 4 * N:4 * N + 2048].rearrange("p (a e) -> p a e", a=2)
        KN = XM[:, 1, :, :].rearrange("p k n -> p (k n)")[:, 0:H * T].rearrange("p (h t) -> p h t", h=H)
        VN = XM[:, 0, :, :].rearrange("p k n -> p (k n)")[:, 0:TT * D].rearrange("p (t e) -> p t e", t=TT)
        OG = QN
        cutB = cutter(arena, ARENA)
        shared = arena[:, 0:2 * N + 10 * ROPE + 4 * 384]
        cosT, sinT = cutB(N), cutB(N)
        cosN, sinN = cutB(5 * ROPE).rearrange("p (t e) -> p t e", t=5), cutB(5 * ROPE).rearrange("p (t e) -> p t e", t=5)
        kvn = cutB(5 * 384).rearrange("p (t e) -> p t e", t=5)
        ckvT = cutB(2 * N).rearrange("p (a n) -> p a n", a=2)
        kpeT = cutB(N)
        qa = cutB(QT * N).rearrange("p (a n) -> p a n", a=QT)
        kvg = cutB(KVL)
        qng = cutB(QT)
        st = cutB(N)
        kss = cutB(8)
        rtmp = cutB(N)
        qlat = cutB(2 * H * NS).rearrange("p (a h s) -> p a h s", a=2, h=H)
        A1 = cutB(KT * 9).rearrange("p (k n) -> p k n", k=KT)
        rt64 = cutB(ROPE)
        qpd = cutB(H * NS).rearrange("p (h s) -> p h s", h=H)
        olat = cutB(2 * H * NS).rearrange("p (a h s) -> p a h s", a=2, h=H)
        causal = cutB(P)
        mx, nmx, den = cutB(4), cutB(4), cutB(4)
        drow = shared[0:H, 0:PAST + 1]
        dval = shared[0:H, PAST + 4:PAST + 4 + KVL]
        dmx, dnm, dden, drc = (shared[0:H, PAST + 4 + KVL + i:PAST + 5 + KVL + i] for i in range(4))
        prT = cutB((NPAGES + 1) * H).rearrange("p (g h) -> p g h", g=NPAGES + 1)
        PN = rtmp[:, 0:T]
        PTb = st[:, 0:T].rearrange("p (b q) -> p b q", b=TT)
        ckr = kvg
        R1g = R1[:, :, :].rearrange("p a b -> p (a b)")
        CKg = [R1g[:, 0:4096], ring[:, 0, :], ring[:, 1, :]]
        CRg = [ring[:, 2, i * 1024:(i + 1) * 1024] for i in range(3)]
        CK = [x.rearrange("p (t c) -> p t c", t=NPAGES) for x in CKg]
        CR = [x.rearrange("p (t c) -> p t c", t=NPAGES) for x in CRg]
        qag = qa.rearrange("p a n -> p (a n)")
        KC = [x.rearrange("p (a k) -> p a k", a=2) for x in (ring[:, 2, 3072:4096], qag[:, 0:1024])]
        KR = [decbuf[:, :, :, :].rearrange("p a b c -> p (a b c)")[0:ROPE], qag[0:ROPE, 1024:1536]]
        WO = [ring[:, 1, :], R1g[:, 0:4096]]
        ptab = sb("ptab", [P, NS], I32)
        pidx = sb("pidx", [P, NS], I32)
        prow = sb("prow", [P, 1])

        s_const = sem("constants_loaded")
        s_mask = sem("masks_loaded")
        s_x = sem("x_loaded")
        s_ada = [sem("ada_group_loaded0"), sem("ada_group_loaded1")]
        s_adl = [sem("ada_group_between_pairs0"), sem("ada_group_between_pairs1")]
        s_adr, s_adt = sem("ada_rows_stored"), sem("ada_rows_turned")
        s_ada_mm = sem("ada_products_done")
        s_ada_out = sem("ada_tiles_stored")
        s_sq = sem("squares_ready")
        s_ss = sem("square_sums_done")
        s_ms = sem("mean_squares_ready")
        s_rstd = sem("rstd_ready")
        s_xm = sem("mixed_input_ready")
        s_l1 = sem("lora1_loaded")
        s_hid = sem("lora_hidden_products")
        s_hida = sem("lora_hidden_by_act")
        s_hidr = sem("lora_hidden_ready")
        s_shout = sem("shift_rows_ready")
        s_store = sem("outputs_stored")
        s_dve, s_act, s_pool = sem("dve_steps"), sem("act_steps"), sem("pool_steps")
        s_pw = [sem("pair_weights_loaded0"), sem("pair_weights_loaded1")]
        s_pjm = sem("projection_slot_filled")
        s_ra = sem("projection_slot_read_by_act")
        s_rd = sem("projection_slot_read_by_dve")
        s_pa = sem("pair_factors_by_act")
        s_pd = sem("pair_factors_by_dve")
        s_pp = sem("pair_factors_by_pool")
        s_M = sem("chunk_products_done")
        s_Me = sem("chunk_products_masked")
        s_Z = sem("inverse_z_product")
        s_Ze = sem("inverse_z_stored")
        s_T = sem("inverse_t_product")
        s_Te = sem("inverse_t_stored")
        s_sc = sem("scan_products")
        s_sce = sem("scan_operand_stored")
        s_Se = sem("state_updated")
        s_gna = sem("group_norm_by_act")
        s_gnd = sem("group_norm_centered")
        s_gnp = sem("group_norm_sums")
        s_yT = sem("mixer_tile_ready")
        s_So = sem("state_transposed")
        s_Soa = sem("state_out_ready")
        s_Sst = sem("state_out_stored")
        s_zero = sem("padding_cleared")
        s_zp = sem("pair_vectors_ready")

        s_xr = sem("x_loaded_again")
        s_w = [sem(f"weights_loaded{i}") for i in range(3)]
        s_wu = sem("weights_used")
        s_adb = sem("later_ada_tiles_stored")
        s_dt = sem("decode_factors_turned")
        s_dta = sem("decode_factors_stored")
        s_dq = sem("decode_factors_moved")
        s_sd = sem("decode_state_loaded")
        s_dd = sem("decode_step_by_dve")
        s_dp = sem("decode_step_by_pool")
        s_dso = sem("decode_state_stored")
        s_dr = sem("decode_rstd_ready")
        s_ydm = sem("decode_y_moved")
        s_ydt = sem("decode_y_turned")
        s_r1 = sem("decode_mixer_tile_ready")
        s_om = sem("output_tile_product")
        s_oa = sem("output_tile_stored")
        s_ns = sem("norm_sums_done")
        s_nd = sem("norm_mean_ready")
        s_na = sem("norm_rstd_ready")
        s_nq = sem("norm_squares_ready")
        s_res = sem("residual_ready")
        s_hh = sem("inputs_of_layer1_by_dve")
        s_hha = sem("inputs_of_layer1_by_act")
        s_cb = sem("second_half_constants_loaded")
        s_kvm = sem("kv_tile_product")
        s_kva = sem("kv_square_sums")
        s_kvd = sem("kv_mean_ready")
        s_kvr = sem("kv_rstd_ready")
        s_kvn = sem("kv_tile_ready")
        s_kvt = sem("kv_tile_turned")
        s_kvs = sem("kv_tile_turned_stored")
        s_kvo = sem("kv_outputs_stored")
        s_bm = sem("layer1_projection_product")
        s_ba = sem("layer1_projection_by_act")
        s_bd = sem("layer1_projection_by_dve")
        s_qn = sem("q_latent_normed")
        s_uv = sem("uv_loaded")
        s_pidx = sem("page_rows_ready")
        s_pt = sem("page_table_loaded")
        s_ck = [sem(f"cache_loaded{i}") for i in range(3)]
        s_bw = [sem("b_w_out_loaded0"), sem("b_w_out_loaded1")]
        s_sm = sem("attention_scores_done")
        s_sd1 = sem("attention_row_max")
        s_sa1 = sem("attention_exp_done")
        s_sd2 = sem("attention_rows_scaled")
        s_pt1 = sem("attention_rows_turned")
        s_pa1 = sem("attention_rows_turned_stored")
        s_po = sem("attention_output_done")
        s_pog = sem("attention_output_gated")
        s_kt = sem("cache_tiles_turned")
        s_kta = sem("cache_tiles_turned_by_act")
        s_ktd = sem("cache_tiles_turned_by_dve")
        s_ds = sem("decode_scores_done")
        s_dse = sem("decode_scores_stored")
        s_dsd = sem("decode_row_max")
        s_dsa = sem("decode_exp_done")
        s_dpt = sem("decode_weights_turned")
        s_dpa = sem("decode_weights_stored")
        s_dv = sem("decode_values_done")
        s_dvs = sem("decode_values_scaled")
        s_dot = sem("decode_values_turned")
        s_dvd = sem("decode_latent_ready")
        s_qpd = sem("decode_q_rope_moved")
        s_ckr = sem("decode_new_row_moved")
        s_do = sem("decode_output_done")
        s_y = sem("result_stored")

        stream = [("ada", g) for g in range(ADA_FIRST + ADA_PAIRS, ADA_GROUPS)] + [("w_out", 0), ("w_out", 1), ("kv_w_a", 0),
                  ("b_w_in", 0), ("b_w_in", 1), ("b_w_in", 2), ("w_q", 0), ("w_q", 1), ("uk", 0)]
        SI = {key: n for n, key in enumerate(stream)}
        NADA = SI[("w_out", 0)]
        B_Q, B_PE, B_K, B_V, B_L = 11, 19, 27, 35, 43

        NSTEP = TT * H

        def scored(n):
            return 5 * (n // TT) + n % TT + 1

        def used(n):
            name, g = stream[n]
            if name == "ada":
                return s_wu, n + 1
            return {"w_out": (s_om, 4 * g + 4), "kv_w_a": (s_kvm, 5), "b_w_in": (s_bm, QT + 4 * g),
                    "w_q": (s_bm, B_K if g else B_PE), "uk": (s_bm, B_L + 1)}[name]

        block = ctx.enter_context(nc.Block())

        def counter(eng, own):
            count = {}

            def mark(ins, s=None):
                s = own if s is None else s
                count[id(s)] = count.get(id(s), 0) + 1
                ins.then_inc(s, 1)
                return s, count[id(s)]

            def then(ins, s=None):
                eng.wait_ge(*mark(ins, s))
            return then, mark

        def store_state(sp, m):
            sp.wait_ge(s_Soa, m + 1)
            for h in range(2):
                sp.dma_start(o["wkv_p"][2 * m + h], Sout[h * HD:(h + 1) * HD, h * HD:(h + 1) * HD]).then_inc(s_Sst, 16)

        @block.sync
        def _(sp):
            for name, dst in (("ident", ident[:, :]), ("ones", ones[:, :]), ("vecs", vecs[:, :, :]),
                              ("adab", adab[:, :]), ("cT", cT[:, :, :])):
                sp.dma_start(dst, d[name]).then_inc(s_const, 16)
            sp.dma_start(R0[:, :, :], d["xT"]).then_inc(s_x, 16)
            for g in range(ADA_FIRST):
                if g >= 2:
                    sp.wait_ge(s_ada_mm, g - 1)
                sp.dma_start(ring[:, g % 2, :], d["ada"][g]).then_inc(s_ada[g % 2], 16)

            def pair_weights(m):
                sp.dma_start(ring[:, m % 2, :], d["w_in"][m]).then_inc(s_pw[m % 2], 16)
                sp.dma_start(lora2[:, m % 2, :], d["lora2"][m]).then_inc(s_pw[m % 2], 16)

            def ada_group(j):
                sp.dma_start(ring[:, (j + 1) % 2, :], d["ada"][ADA_FIRST + j]).then_inc(s_adl[(j + 1) % 2], 16)

            for m in range(2):
                sp.wait_ge(s_ada_mm, ADA_FIRST - 1 + m)
                pair_weights(m)
            sp.wait_ge(s_pjm, U_A + 1)
            pair_weights(2)
            for m in range(PAIRS):
                if m + 1 < PAIRS:
                    sp.wait_ge(s_pjm, NUSE * (m + 1) + U_G + 1)
                    ada_group(m)
                    sp.wait_ge(s_ada_mm, ADA_FIRST + m + 1)
                    if m + 3 < PAIRS:
                        pair_weights(m + 3)
                    if m + 1 == PAIRS - 1:
                        ada_group(PAIRS - 1)
                store_state(sp, m)
            sp.wait_ge(s_ada_mm, ADA_FIRST + ADA_PAIRS)
            sp.wait_ge(s_yT, PAIRS)
            sp.wait_ge(s_pp, 3 * PAIRS)
            sp.wait_ge(s_pa, 4 * PAIRS)
            sp.dma_start(R0[:, :, :], d["xT"]).then_inc(s_xr, 16)
            sp.dma_start(Sd, d["Sd"]).then_inc(s_sd, 16)
            for n, (name, g) in enumerate(stream):
                if n >= 3:
                    sp.wait_ge(*used(n - 3))
                src = d[name][g]
                sp.dma_start(ring[:, n % 3, 0:src.shape[1]], src).then_inc(s_w[n % 3], 16)
            sp.wait_ge(s_kvn, 5)
            for n in range(NS):
                if n >= 1:
                    sp.wait_ge(s_dv, n)
                sp.dma_start(ckr[0:1, :], kvn[n:n + 1, TT, 0:KVL]).then_inc(s_ckr, 16)
                if n >= NS - 2:
                    i = n - (NS - 2)
                    sp.dma_start(WO[i], d["b_w_out"][i]).then_inc(s_bw[i], 16)
            sp.wait_ge(s_res, 2)
            sp.dma_start(o["y"], R0[:, :, :]).then_inc(s_y, 16)
            sp.wait_ge(s_y, 16)
            sp.wait_ge(s_Sst, 32 * PAIRS)
            sp.wait_ge(s_store, 16)
            sp.wait_ge(s_dso, 16)
            sp.wait_ge(s_kvo, 160)

        @block.scalar
        def _(act):
            then, mark = counter(act, s_act)
            A = nc.scalar.activation
            nc.scalar.preload_act_table_set("natural_log_exp_and_others")
            for name, dst in (("scanm", scanm), ("maskM", maskM), ("lowm", lowm), ("lv1", lv1), ("lvm", lvm),
                              ("id64", id64), ("bones", bones)):
                act.dma_start(dst, d[name]).then_inc(s_mask, 16)
            act.dma_start(lora1, d["lora1"]).then_inc(s_l1, 16)
            act.dma_start(shin, d["shiftT"]).then_inc(s_l1, 16)
            act.wait_ge(s_x, 16)
            mark(A(R2[:, :, :], R0[:, :, :], ACT.Square), s_sq)
            act.wait_ge(s_ms, 1)
            then(A(stat, stat, ACT.Ln))
            mark(A(stat, stat, ACT.Exp, scale=-0.5), s_rstd)
            act.wait_ge(s_shout, 1)
            act.dma_start(o["shift"], shout).then_inc(s_store, 16)
            act.wait_ge(s_hid, 1)
            then(A(two(lhid)[0:LORA], pjs[0][0:LORA], ACT.Exp, scale=2.0))
            then(A(lhid[0:LORA], lhid[0:LORA], ACT.Ln, bias=1.0))
            mark(A(lhid[0:LORA], lhid[0:LORA], ACT.Exp, scale=-1.0), s_hida)
            act.wait_ge(s_hid, 2)
            mark(A(two(lhid)[LORA:P], pjs[1][LORA:P], ACT.Identity), s_hida)

            def prep(m, part):
                v = m % 2
                if part == "r":
                    act.wait_ge(s_pjm, NUSE * m + U_R + 1)
                    if m >= 1:
                        act.wait_ge(s_pd, 4 * m)
                        act.wait_ge(s_pp, 3 * m)
                    if m >= 2:
                        act.wait_ge(s_yT, m - 1)
                    mark(A(two(rT), pjs[0], ACT.Identity), s_ra)
                if part == "k":
                    act.wait_ge(s_pjm, NUSE * m + U_K + 1)
                    mark(A(two(kT), pjs[1], ACT.Identity))
                    mark(A(two(sqk), pjs[1], ACT.Square, scale=vecs[:, V_KK, m:m + 1]), s_ra)
                if part == "v":
                    act.wait_ge(s_pjm, NUSE * m + U_V + 1)
                    mark(A(two(vT), pjs[0], ACT.Identity), s_ra)
                if part == "g":
                    act.wait_ge(s_pjm, NUSE * m + U_G + 1)
                    then(A(two(gT[v]), pjs[1], ACT.Exp, scale=-1.0))
                    then(A(gT[v], gT[v], ACT.Ln, bias=1.0))
                    mark(A(gT[v], gT[v], ACT.Exp, scale=-1.0), s_pa)
                if part == "wa":
                    act.wait_ge(s_pjm, NUSE * m + U_W + 1)
                    if m == 0:
                        act.wait_ge(s_zp, 3)
                    mark(A(two(sg), pjs[0], ACT.Exp, scale=-1.0, bias=nw0[:, m:m + 1]), s_ra)
                    act.wait_ge(s_pjm, NUSE * m + U_A + 1)
                    then(A(two(aT), pjs[1], ACT.Exp, scale=-1.0, bias=na0[:, m:m + 1]), s_ra)
                    then(A(wa, wa, ACT.Ln, bias=1.0))
                    mark(A(wa, wa, ACT.Exp, scale=-1.0), s_pa)
                if part == "kk":
                    act.wait_ge(s_rd, 3 * m + 2)
                    then(A(sqk, sqk, ACT.Ln))
                    mark(A(sqk, sqk, ACT.Exp, scale=-0.5), s_pa)
                if part == "cum":
                    act.wait_ge(s_pd, 4 * m + 1)
                    mark(A(ecum, cum, ACT.Exp, scale=-E05))
                    mark(A(einv, cum, ACT.Exp, scale=E05))
                    mark(A(cumx, cumx, ACT.Exp, scale=-E05), s_pa)
                if part == "tv":
                    act.wait_ge(s_pjm, NUSE * m + U_TV + 1)
                    act.wait_ge(s_zero, 1)
                    mark(A(Vx[v].rearrange("p c (h x) -> p c h x", x=HD)[:, :, 0:3:2, :],
                           pj[:, 0, 0, :].rearrange("p (c h x) -> p c h x", c=TT, h=2), ACT.Identity), s_ra)
                if part == "tb":
                    act.wait_ge(s_pjm, NUSE * m + U_TB + 1)
                    mark(A(BK[v].rearrange("p a c j -> p a (c j)"), pj[:, 1, :, :], ACT.Identity), s_ra)

            def scan(m, ch):
                pr = slice((ch % 2) * C, (ch % 2) * C + C)
                n = 4 * (NCH * m + ch)
                act.wait_ge(s_sc, n + 1)
                if ch == 0 and m >= 1:
                    act.wait_ge(s_Sst, 32 * m)
                mark(A(rhs[pr], bk[pr, 3, 0:P], ACT.Copy, scale=-1.0), s_sce)
                act.wait_ge(s_sc, n + 2)
                mark(A(SAx[pr].rearrange("p (h x) -> p h x", x=HD)[:, 0:3:2, :],
                       bk[pr, 0, 0:P].rearrange("p (h x) -> p h x", h=2), ACT.Identity), s_sce)

            def norm(m):
                act.wait_ge(s_sc, 4 * NCH * (m + 1))
                mark(A(yc, bk[:, 2, :], ACT.Identity), s_gna)
                act.wait_ge(s_ada_mm, ADA_FIRST + m + 1)
                mark(A(adarow, pj[0:9, 0, 1, :], ACT.Identity), s_adr)
                act.wait_ge(s_So, m + 1)
                mark(A(Sout, bk[:, 3, 0:P], ACT.Identity), s_Soa)
                act.wait_ge(s_gnd, m + 1)
                mark(A(ysq, yc, ACT.Square), s_gna)
                act.wait_ge(s_gnp, 2 * m + 2)
                then(A(ysq, bk[:, 1, :], ACT.Ln, scale=1.0 / HD, bias=GN_EPS))
                mark(A(ysq, ysq, ACT.Exp, scale=-0.5), s_gna)

            for part in ("r", "k", "v", "g", "wa", "kk", "cum", "tv", "tb"):
                prep(0, part)
            for m in range(PAIRS):
                more = m + 1 < PAIRS
                if more:
                    for part in ("r", "k", "v", "g", "wa"):
                        prep(m + 1, part)
                for ch in range(NCH):
                    scan(m, ch)
                    if more and ch == 1:
                        prep(m + 1, "kk")
                    if more and ch == 2:
                        prep(m + 1, "cum")
                    if more and ch == 6:
                        prep(m + 1, "tv")
                norm(m)
                if more:
                    prep(m + 1, "tb")

            act.wait_ge(s_yT, PAIRS)
            act.wait_ge(s_pp, 3 * PAIRS)
            act.wait_ge(s_Sst, 32 * PAIRS)
            for name, dst in (("cosT", cosT), ("sinT", sinT), ("cosN", cosN), ("sinN", sinN), ("kvg", kvg),
                              ("qng", qng), ("causal", causal), ("prow", prow[:, :])):
                act.dma_start(dst, d[name]).then_inc(s_cb, 16)
            act.dma_start(ptab[:, :], d["page_table"]).then_inc(s_pt, 16)

            def ada(n):
                g = stream[n][1]
                act.wait_ge(s_wu, n + 1)
                for t in range(ADA_MT):
                    mark(A(mod[:, ADA_MT * g + t, :], bk[:, n % 2, 9 * t:9 * t + 9], ACT.Identity,
                           bias=adab[:, ADA_MT * g + t:ADA_MT * g + t + 1]), s_adb)

            def turn_factors():
                act.wait_ge(s_dt, 1)
                mark(A(dturn[0:HD, 0:4, :], pj[0:HD, 0, 0, :].rearrange("p (q j) -> p q j", q=4), ACT.Identity))
                then(A(dturn[0:HD, 4:6, :], pj[0:HD, 0, 1, 0:256].rearrange("p (q j) -> p q j", q=2), ACT.Identity))
                for hp in range(2):
                    act.dma_start(dq[hp * HD:(hp + 1) * HD], dturn[0:HD, :, hp * HD:(hp + 1) * HD]).then_inc(s_dq, 16)

            turn_factors()
            for n in range(NADA):
                ada(n)
            act.wait_ge(s_dd, 4)
            act.dma_start(o["wkv_s"], Sd).then_inc(s_dso, 16)
            act.wait_ge(s_dd, 5)
            then(A(rsd, bag[:, 1:2], ACT.Ln, bias=GN_EPS))
            mark(A(rsd, rsd, ACT.Exp, scale=-0.5), s_dr)
            act.wait_ge(s_dd, 6)
            for hp in range(2):
                act.dma_start(ydt[0:HD, hp * HD:(hp + 1) * HD], yd[hp * HD:(hp + 1) * HD]).then_inc(s_ydm, 16)

            def out_tiles(layer):
                for t in range(KT):
                    act.wait_ge(s_om, KT * layer + t + 1)
                    mark(A(two(SQ[:, t, :]), pjs[t % 2], ACT.Square), s_nq)
                    mark(A(two(Y[:, t, :]), pjs[t % 2], ACT.Identity), s_oa)

            nn = [0]

            def rstd(x):
                nn[0] += 1
                act.wait_ge(s_nd, nn[0])
                then(A(x, x, ACT.Ln))
                mark(A(x, x, ACT.Exp, scale=-0.5), s_na)

            out_tiles(0)
            rstd(st)
            act.wait_ge(s_res, 1)
            mark(A(SQ[:, :, :], R0[:, :, :], ACT.Square), s_nq)
            rstd(st)
            act.wait_ge(s_hh, 1)
            act.wait_ge(s_dso, 16)
            for k in range(KT):
                mark(A(H1[:, k, 0:T], HN[:, k, 0:T], ACT.Identity, scale=A0[:, k, 0:1], bias=mod[:, M_SH1 + k, 0:1]), s_hha)

            for t in range(5):
                n = P if t < TT else NS
                act.wait_ge(s_kvm, t + 1)
                then(A(rtmp[0:n, 0:KVL], pj[0:n, t % 2, 0, 0:KVL], ACT.Square, accum_out=kss[0:n, 0:1]), s_kva)
                act.wait_ge(s_kvd, t + 1)
                then(A(kss[0:n, 1:2], kss[0:n, 1:2], ACT.Ln))
                mark(A(kss[0:n, 1:2], kss[0:n, 1:2], ACT.Exp, scale=-0.5), s_kvr)
                act.wait_ge(s_kvt, t + 1)
                mark(A(ckvT[:, :, t * P:t * P + n], bk[:, 2, 0:2 * n].rearrange("p (a n) -> p a n", a=2), ACT.Identity))
                mark(A(kpeT[:, t * P:t * P + n], bk[:, 2, 2 * n:3 * n], ACT.Identity), s_kvs)
                act.wait_ge(s_kvn, t + 1)
                act.dma_start(o["ckv"][t * P:t * P + n, :], kvn[0:n, t, 0:KVL]).then_inc(s_kvo, 16)
                act.dma_start(o["kpe"][t * P:t * P + n, :], kvn[0:n, t, KVL:KVL + ROPE]).then_inc(s_kvo, 16)

            for t in range(QT + KT):
                act.wait_ge(s_bm, t + 1)
                if t < QT:
                    mark(A(two(SQ[:, t, :]), pjs[t % 2], ACT.Square), s_nq)
                    mark(A(two(qa[:, t, :]), pjs[t % 2], ACT.Identity), s_ba)
                else:
                    g = GATE[:, t - QT, :]
                    then(A(two(g), pjs[t % 2], ACT.Exp, scale=-1.0))
                    then(A(g, g, ACT.Ln, bias=1.0))
                    mark(A(g, g, ACT.Exp, scale=-1.0), s_ba)
                    if t == QT:
                        rstd(st)
                        act.dma_start(UV, d["uv"]).then_inc(s_uv, 16)
            for t in range(H):
                act.wait_ge(s_bm, B_Q + t + 1)
                mark(A(two(QN[:, t, :]), pjs[(B_Q + t) % 2], ACT.Identity), s_ba)
            act.wait_ge(s_bd, KT + 4)
            for hp in range(2):
                act.dma_start(qpd[0:ROPE, hp:H:2, :], QP[hp * ROPE:(hp + 1) * ROPE, :, T:N]).then_inc(s_qpd, 16)
            base = B_K
            for t in range(H):
                act.wait_ge(s_bm, base + t + 1)
                mark(A(KN[:, t, :], bk[:, t % 2, :], ACT.Identity), s_ba)
            for t in range(2 * TT):
                act.wait_ge(s_bm, base + H + t + 1)
                mark(A(VN[:, t // 2, (t % 2) * 512:(t % 2) * 512 + 512], bk[:, t % 2, :], ACT.Identity), s_ba)
            act.wait_ge(s_bm, base + H + 2 * TT + 1)
            mark(A(qlat, bk[:, 2, 0:2 * H * NS].rearrange("p (a h s) -> p a h s", a=2, h=H), ACT.Identity), s_ba)

            def row_exp(n):
                w = (n % TT + 1) * P
                act.wait_ge(s_sd1, n + 1)
                act.wait_ge(s_pt1, n)
                mark(A(PN[:, 0:w], bk[:, 0, 0:w], ACT.Exp, scale=SCALE, bias=nmx[:, 0:1], accum_out=den[:, 0:1]), s_sa1)

            def rows_turned(n):
                w = (n % TT + 1) * P
                act.wait_ge(s_pt1, n + 1)
                act.wait_ge(s_po, n)
                mark(A(PTb[:, 0:n % TT + 1, :], bk[:, 1, 0:w].rearrange("p (b q) -> p b q", q=P), ACT.Identity), s_pa1)

            def cache_turned(n):
                act.wait_ge(s_kt, n + 1)
                if n >= 2:
                    act.wait_ge(s_ds, scored(n - 2))
                mark(A(KC[n % 2], pj[:, 0, :, :], ACT.Identity), s_kta)

            def decode_exp(s):
                act.wait_ge(s_dsd, s + 1)
                mark(A(drow, drow, ACT.Exp, scale=SCALE, bias=dnm, accum_out=dden), s_dsa)

            def weights_turned(s):
                act.wait_ge(s_dpt, s + 1)
                act.wait_ge(s_dv, s)
                mark(A(prT[:, 0:NPAGES, :], bk[:, 3, 0:P].rearrange("p (g h) -> p g h", h=H), ACT.Identity))
                mark(A(prT[0:1, NPAGES, :], bk[0:1, 3, P:P + H], ACT.Identity), s_dpa)

            row_exp(0)
            for n in range(NSTEP):
                s, g = n // TT, n % TT
                cache_turned(n)
                rows_turned(n)
                if s >= 1 and g == 1:
                    decode_exp(s - 1)
                if n + 1 < NSTEP:
                    row_exp(n + 1)
                if s >= 1 and g == 2:
                    weights_turned(s - 1)
            decode_exp(NS - 1)
            weights_turned(NS - 1)
            out_tiles(1)
            rstd(st)

        @block.tensor
        def _(pe):
            mm, tr = nc.tensor.matmul, nc.tensor.transpose
            pe.wait_ge(s_const, 80)
            for g in range(ADA_FIRST):
                pe.wait_ge(s_ada[g % 2], 16 * (g // 2 + 1))
                if g >= 2:
                    pe.wait_ge(s_ada_out, g - 1)
                w = ring[:, g % 2, :].rearrange("p (k e) -> p k e", k=KT)
                for t in range(ADA_MT):
                    for k in range(KT):
                        last = mm(bk[:, g % 2, 9 * t:9 * t + 9], w[:, k, t * P:(t + 1) * P], cT[:, k, :],
                                  start=(k == 0), stop=(k == KT - 1))
                last.then_inc(s_ada_mm, 1)
                if g == 1:
                    pe.wait_ge(s_sq, 1)
                    for k in range(KT):
                        for a in range(2):
                            last = mm(pj[:, 0, a, 0:HALF], ones[:, :], R2[:, k, a * HALF:(a + 1) * HALF],
                                      start=(k == 0), stop=(k == KT - 1))
                    last.then_inc(s_ss, 1)
            pe.wait_ge(s_l1, 32)
            for e in range(2):
                pe.wait_ge(s_xm, e + 1)
                for k in range(KT):
                    for a in range(2):
                        last = mm(pj[e * LORA:(e + 1) * LORA, e, a, 0:HALF], lora1[:, k, e * LORA:(e + 1) * LORA],
                                  XM[:, e, k, a * HALF:(a + 1) * HALF], start=(k == 0), stop=(k == KT - 1))
                last.then_inc(s_hid, 1)

            def project(m, e):
                s = e % 2
                if m == 0:
                    pe.wait_ge(s_xm, (5, 6, 3, 4)[e])
                if e == U_R:
                    pe.wait_ge(s_pw[m % 2], 32 * (m // 2 + 1))
                    if m >= 2:
                        pe.wait_ge(s_ada_out, ADA_FIRST + m - 1)
                    if m >= 1:
                        pe.wait_ge(s_ra, 7 * m - 1)
                    else:
                        pe.wait_ge(s_hida, 2)
                if e == U_K and m >= 1:
                    pe.wait_ge(s_ra, 7 * m)
                if e == U_V:
                    pe.wait_ge(s_ra, 7 * m + 1)
                if e == U_G:
                    pe.wait_ge(s_ra, 7 * m + 2)
                w = ring[:, m % 2, :].rearrange("p (e k c) -> p e k c", e=4, k=KT)
                for k in range(KT):
                    for a in range(2):
                        last = mm(pj[:, s, a, 0:HALF], w[:, e, k, :], XM[:, e, k, a * HALF:(a + 1) * HALF],
                                  start=(k == 0), stop=(k == KT - 1))
                last.then_inc(s_pjm, 1)

            def lora(m, e):
                if m == 0:
                    pe.wait_ge(s_hidr, 1)
                    pe.wait_ge(s_hida, 2)
                if e == 0:
                    pe.wait_ge(s_ra, 7 * m + 3)
                else:
                    pe.wait_ge(s_rd, 3 * m + 1)
                r = slice(e * LORA, (e + 1) * LORA)
                for a in range(2):
                    last = mm(pj[:, e, a, 0:HALF], lora2[r, m % 2, :], lhid[r, a * HALF:(a + 1) * HALF],
                              start=True, stop=True)
                last.then_inc(s_pjm, 1)

            def head_sums(m, which):
                if which == 0:
                    pe.wait_ge(s_ra, 7 * m + 4)
                else:
                    pe.wait_ge(s_pd, 4 * m + 3)
                    pe.wait_ge(s_ra, 7 * m + 5)
                x = sqk if which == 0 else tmb
                for a in range(2):
                    last = mm(pj[:, which, a, 0:HALF], bones, x[:, a * HALF:(a + 1) * HALF], start=True, stop=True)
                last.then_inc(s_pjm, 1)

            def turn_v(m):
                pe.wait_ge(s_rd, 3 * m + 2)
                for t in range(TT):
                    last = tr(pj[:, 0, 0, t * P:(t + 1) * P], vT[:, t * P:(t + 1) * P], ident[:, :])
                last.then_inc(s_pjm, 1)

            def turn_bk(m):
                pe.wait_ge(s_pd, 4 * m + 4)
                pe.wait_ge(s_rd, 3 * m + 3)
                for a, x in ((0, cum), (1, sqk)):
                    for t in range(TT):
                        last = tr(pj[:, 1, a, t * P:(t + 1) * P], x[:, t * P:(t + 1) * P], ident[:, :])
                last.then_inc(s_pjm, 1)

            def chunk_products(m):
                v = m % 2
                pe.wait_ge(s_pd, 4 * m + 4)
                if m >= 1:
                    pe.wait_ge(s_yT, m)
                    pe.wait_ge(s_Soa, m)
                for half in range(2):
                    for h in range(2):
                        r = slice(h * HD, (h + 1) * HD)
                        for u in range(4):
                            t, cp = 2 * half + u // 2, u % 2
                            ch = 2 * t + cp
                            for a, x in ((0, Bt), (1, Kt_)):
                                c0 = (u // 2) * 256 + a * P
                                last = mm(bk[cp * C:(cp + 1) * C, 2 * half + h, c0:c0 + P], x[r, ch * C:(ch + 1) * C],
                                          AR[v][r, ch, :, :].rearrange("p a t -> p (a t)"), start=True, stop=True)
                        last.then_inc(s_M, 1)
                pe.wait_ge(s_Me, 5 * m + 2)
                for h in range(2):
                    r = slice(h * HD, (h + 1) * HD)
                    for ch in range(NCH):
                        t, cp = ch // 2, ch % 2
                        last = mm(bk[cp * C:(cp + 1) * C, h, t * C:(t + 1) * C], AR[v][r, ch, 0, :],
                                  Bt[r, ch * C:(ch + 1) * C], start=True, stop=True)
                last.then_inc(s_M, 1)

            def blocks(out, lhsT, rhs_):
                for b in range(BLK):
                    for cp in range(2):
                        r = slice(cp * C, (cp + 1) * C)
                        last = mm(bk[r, out, b * C:(b + 1) * C], lhsT[r, b, :], rhs_[r, b, :], start=True, stop=True)
                return last

            def level_z(m, l):
                pe.wait_ge(s_Te, (NLEV + 1) * m + l + 1)
                blocks(0, Mab, Tt).then_inc(s_Z, 1)

            def level_t(m, l):
                pe.wait_ge(s_Ze, NLEV * m + l + 1)
                blocks(2, Tm, Zt).then_inc(s_T, 1)
                if l < NLEV - 1:
                    blocks(1, Zt, Tm).then_inc(s_T, 1)

            def ada_slice(m, k):
                if k < 0:
                    return
                if k == 0:
                    pe.wait_ge(s_adl[(m + 1) % 2], 16 * (m // 2 + 1))
                    pe.wait_ge(s_rd, 3 * m + 5 if m + 1 < PAIRS else 3 * m + 3)
                    pe.wait_ge(s_ada_out, ADA_FIRST + m)
                w = ring[:, (m + 1) % 2, :].rearrange("p (k e) -> p k e", k=KT)
                last = mm(pj[0:9, 0, 1, :], cT[:, k, :], w[:, k, :], start=(k == 0), stop=(k == KT - 1))
                if k == KT - 1:
                    last.then_inc(s_ada_mm, 1)

            def ada_turn(m):
                pe.wait_ge(s_adr, m + 1)
                for t in range(ADA_MT):
                    last = tr(pj[:, 0, 1, 9 * t:9 * t + 9], adarow[:, t * P:(t + 1) * P], ident[0:9, 0:9])
                last.then_inc(s_adt, 1)

            def scan(m, ch):
                v = m % 2
                t, cp = ch // 2, ch % 2
                pr = slice(cp * C, (cp + 1) * C)
                n = NCH * m + ch
                both = lambda x: x.rearrange("p (h x) -> p h x", x=HD)[:, 0:3:2, :]
                pe.wait_ge(s_Se, n + m + 1)
                if ch == 0:
                    pe.wait_ge(s_Te, (NLEV + 1) * (m + 1))
                mm(bk[pr, 3, 0:P], AR[v][:, ch, 0, :], S, start=True, stop=False)
                for h in range(2):
                    last = mm(bk[pr, 3, h * HD:(h + 1) * HD], MM[pr, h * TT + t, 2, :],
                              Vx[v][pr, t, h * P:h * P + HD], start=False, stop=(h == 1))
                last.then_inc(s_sc, 1)
                ada_slice(m, ch - 2)
                pe.wait_ge(s_sce, 2 * n + 1)
                for h in range(2):
                    last = mm(bk[pr, 0, h * HD:(h + 1) * HD], Tt[pr, h * TT + t, :], rhs[pr, h * HD:(h + 1) * HD],
                              start=True, stop=True)
                last.then_inc(s_sc, 1)
                if ch >= 6:
                    ada_slice(m, ch)
                pe.wait_ge(s_sce, 2 * n + 2)
                mm(bk[:, 1, 0:P], BK[v][pr, 0, t, :], both(SAx[pr]), start=True, stop=False)
                mm(bk[:, 1, 0:P], BK[v][pr, 1, t, :], both(Vx[v][pr, t, :]), start=False, stop=True).then_inc(s_sc, 1)
                y = bk[:, 2, ch * C:(ch + 1) * C]
                mm(y, S, AR[v][:, ch, 1, :], start=True, stop=False)
                for h in range(2):
                    mm(y, SAx[pr, h * HD:h * HD + P], MM[pr, h * TT + t, 1, :], start=False, stop=False)
                    last = mm(y, Vx[v][pr, t, h * HD:h * HD + P], MM[pr, h * TT + t, 3, :],
                              start=False, stop=(h == 1))
                last.then_inc(s_sc, 1)

            def norm(m):
                pe.wait_ge(s_gna, 3 * m + 1)
                mm(bk[:, 0, :], bones, yc, start=True, stop=True).then_inc(s_gnp, 1)
                ada_turn(m)
                pe.wait_ge(s_Se, (NCH + 1) * (m + 1))
                tr(bk[:, 3, 0:P], S, ident[:, :]).then_inc(s_So, 1)
                pe.wait_ge(s_gna, 3 * m + 2)
                mm(bk[:, 1, :], bones, ysq, start=True, stop=True).then_inc(s_gnp, 1)

            pe.wait_ge(s_mask, 112)
            for e in range(4):
                project(0, e)
            lora(0, 0)
            lora(0, 1)
            head_sums(0, 0)
            head_sums(0, 1)
            turn_v(0)
            turn_bk(0)
            for m in range(PAIRS):
                more = m + 1 < PAIRS
                chunk_products(m)
                if more:
                    project(m + 1, 0)
                for l in range(NLEV):
                    level_z(m, l)
                    if more:
                        if l < 3:
                            project(m + 1, l + 1)
                        else:
                            lora(m + 1, l - 3)
                    level_t(m, l)
                for ch in range(NCH):
                    scan(m, ch)
                    if more and ch == 0:
                        head_sums(m + 1, 0)
                    if more and ch == 4:
                        head_sums(m + 1, 1)
                    if more and ch == 5:
                        turn_v(m + 1)
                norm(m)
                if more:
                    turn_bk(m + 1)

            def arrived(n):
                pe.wait_ge(s_w[n % 3], 16 * (n // 3 + 1))

            pe.wait_ge(s_yT, PAIRS)
            pe.wait_ge(s_Soa, PAIRS)
            pe.wait_ge(s_pp, 3 * PAIRS)
            for q in range(6):
                last = tr(pj[0:HD, 0, q // 4, (q % 4) * P:(q % 4 + 1) * P], decbuf[:, q, :, :].rearrange("p m s -> p (m s)"),
                          ident[:, :])
            last.then_inc(s_dt, 1)
            for n in range(NADA):
                arrived(n)
                if n >= 2:
                    pe.wait_ge(s_adb, ADA_MT * (n - 1))
                w = ring[:, n % 3, :].rearrange("p (k e) -> p k e", k=KT)
                for t in range(ADA_MT):
                    for k in range(KT):
                        last = mm(bk[:, n % 2, 9 * t:9 * t + 9], w[:, k, t * P:(t + 1) * P], cT[:, k, :],
                                  start=(k == 0), stop=(k == KT - 1))
                last.then_inc(s_wu, 1)
            pe.wait_ge(s_ydm, 32)
            tr(pj[:, 1, 0, 0:HD], ydt[0:HD, :], ident[0:HD, 0:HD]).then_inc(s_ydt, 1)

            def sums(src, k, last):
                for a in range(2):
                    i = mm(bk[:, 2 + a, 0:HALF], ones[:, :], src[:, k, a * HALF:(a + 1) * HALF], start=(k == 0), stop=last)
                return i

            def out_tiles(layer, src):
                for t in range(KT):
                    if layer == 0:
                        n = SI[("w_out", t // 4)]
                        arrived(n)
                        w = ring[:, n % 3, :]
                        if t == 0:
                            pe.wait_ge(s_r1, 1)
                    else:
                        w = WO[t // 4]
                        pe.wait_ge(s_bw[t // 4], 16)
                        if t == 0:
                            pe.wait_ge(s_pog, H + 1)
                    w = w.rearrange("p (k e) -> p k e", k=KT)
                    if t >= 2:
                        pe.wait_ge(s_oa, KT * layer + t - 1)
                    for k in range(KT):
                        for a in range(2):
                            last = mm(pj[:, t % 2, a, 0:HALF], w[:, k, (t % 4) * P:(t % 4 + 1) * P],
                                      src[:, k, a * HALF:(a + 1) * HALF], start=(k == 0), stop=(k == KT - 1))
                    last.then_inc(s_om, 1)
                for t in range(KT):
                    pe.wait_ge(s_nq, (0, 12)[layer] + t + 1)
                    last = sums(SQ, t, t == KT - 1)
                last.then_inc(s_ns, 1)

            out_tiles(0, R1)
            pe.wait_ge(s_nq, KT + 1)
            pe.wait_ge(s_nd, 1)
            for k in range(KT):
                last = sums(SQ, k, k == KT - 1)
            last.then_inc(s_ns, 1)

            n = SI[("kv_w_a", 0)]
            arrived(n)
            kw = ring[:, n % 3, 0:KT * 384].rearrange("p (k e) -> p k e", k=KT)
            pe.wait_ge(s_hh, 2)
            pe.wait_ge(s_oa, KT)

            def kv_turn(t):
                c = P if t < TT else NS
                pe.wait_ge(s_kvn, t + 1)
                pe.wait_ge(s_kvs, t)
                pe.wait_ge(s_nd, 2)
                for a in range(3):
                    last = tr(bk[:, 2, a * c:(a + 1) * c], kvn[0:c, t, a * P:(a + 1) * P], ident[0:c, 0:c])
                last.then_inc(s_kvt, 1)

            for t in range(5):
                c = P if t < TT else NS
                if t >= 2:
                    pe.wait_ge(s_kvn, t - 1)
                for k in range(KT):
                    last = mm(pj[0:c, t % 2, 0, 0:384], HK[:, k, t * P:t * P + c], kw[:, k, :],
                              start=(k == 0), stop=(k == KT - 1))
                last.then_inc(s_kvm, 1)
                if t >= 1:
                    kv_turn(t - 1)
            kv_turn(TT)

            pe.wait_ge(s_hha, KT)
            pe.wait_ge(s_kvn, 5)
            for t in range(QT + KT):
                g = 0 if t < QT else 1 + (t - QT) // 4
                n = SI[("b_w_in", g)]
                arrived(n)
                wid = 384 if g == 0 else 512
                e = t if g == 0 else (t - QT) % 4
                w = ring[:, n % 3, 0:KT * wid].rearrange("p (k e) -> p k e", k=KT)
                if 2 <= t < QT + 2:
                    pe.wait_ge(s_ba, t - 1)
                if t >= QT + 2:
                    pe.wait_ge(s_bd, t - 2 - QT + 1)
                for k in range(KT):
                    for a in range(2):
                        last = mm(pj[:, t % 2, a, 0:HALF], w[:, k, e * P:(e + 1) * P], H1[:, k, a * HALF:(a + 1) * HALF],
                                  start=(k == 0), stop=(k == KT - 1))
                last.then_inc(s_bm, 1)
                if t == QT:
                    pe.wait_ge(s_nq, KT + 1 + QT)
                    pe.wait_ge(s_kvs, 5)
                    for k in range(QT):
                        last = sums(SQ, k, k == QT - 1)
                    last.then_inc(s_ns, 1)
            pe.wait_ge(s_qn, 1)
            for u in range(16):
                n = SI[("w_q", u // 8)]
                arrived(n)
                w = ring[:, n % 3, 0:QT * D].rearrange("p (k e) -> p k e", k=QT)
                slot = (B_Q + u) % 2 if u < 8 else u % 2
                if u < 2:
                    pe.wait_ge(s_bd, KT - 1 + u)
                elif u < 8:
                    pe.wait_ge(s_ba, B_Q + u - 1)
                elif u < 10:
                    pe.wait_ge(s_ba, B_PE)
                else:
                    pe.wait_ge(s_bd, KT + (u - 8) // 2)
                e = u if u < 8 else (u - 8) // 2 + 4 * (u % 2)
                for k in range(QT):
                    for a in range(2):
                        last = mm(pj[:, slot, a, 0:HALF], w[:, k, e * P:(e + 1) * P], qa[:, k, a * HALF:(a + 1) * HALF],
                                  start=(k == 0), stop=(k == QT - 1))
                last.then_inc(s_bm, 1)
            n = SI[("uk", 0)]
            arrived(n)
            uk = ring[:, n % 3, 0:2048].rearrange("p (a e) -> p a e", a=2)
            ukT = ring[:, n % 3, 2048:4096].rearrange("p (h c) -> p h c", h=H)
            for h in range(H):
                if h >= 2:
                    pe.wait_ge(s_ba, B_PE + h - 1)
                for a in range(2):
                    last = mm(bk[:, h % 2, :], uk[:, a, h * P:(h + 1) * P], ckvT[:, a, 0:T], start=(a == 0), stop=(a == 1))
                last.then_inc(s_bm, 1)
            pe.wait_ge(s_uv, 16)
            for t in range(2 * TT):
                pe.wait_ge(s_ba, B_PE + H + t - 1)
                for a in range(2):
                    last = mm(bk[:, t % 2, :], ckvT[:, a, (t // 2) * P:(t // 2 + 1) * P],
                              UV[:, a, (t % 2) * 512:(t % 2) * 512 + 512], start=(a == 0), stop=(a == 1))
                last.then_inc(s_bm, 1)
            pe.wait_ge(s_nd, 3)
            for a in range(2):
                for h in range(H):
                    c0 = (a * H + h) * NS
                    last = mm(bk[:, 2, c0:c0 + NS], ukT[:, h, a * P:(a + 1) * P], QN[:, h, T:N], start=True, stop=True)
            last.then_inc(s_bm, 1)

            def scores(n):
                h, q = n // TT, n % TT
                r = slice((h % 2) * ROPE, (h % 2 + 1) * ROPE)
                w = (q + 1) * P
                qs = slice(q * P, (q + 1) * P)
                pe.wait_ge(s_sa1, n)
                mm(bk[:, 0, 0:w], QN[:, h, qs], KN[:, h, 0:w], start=True, stop=False)
                mm(bk[:, 0, 0:w], QP[r, h // 2, qs], kpeT[r, 0:w], start=False, stop=True).then_inc(s_sm, 1)

            def turn_rows(n):
                pe.wait_ge(s_sd2, n + 1)
                pe.wait_ge(s_pa1, n)
                for b in range(n % TT + 1):
                    last = tr(bk[:, 1, b * P:(b + 1) * P], PN[:, b * P:(b + 1) * P], ident[:, :])
                last.then_inc(s_pt1, 1)

            def row_values(n):
                h, q = n // TT, n % TT
                pe.wait_ge(s_pa1, n + 1)
                if q == 0:
                    pe.wait_ge(s_pog, h)
                for b in range(q + 1):
                    last = mm(bk[:, 2, q * P:(q + 1) * P], VN[:, b, h * P:(h + 1) * P], PTb[:, b, :], start=(b == 0), stop=(b == q))
                last.then_inc(s_po, 1)

            def turn_cache(n):
                s, g = n // TT, n % TT
                v = s % 3
                if g == 0:
                    pe.wait_ge(s_ck[v], 32 * (s // 3 + 1))
                pe.wait_ge(s_kta, n)
                pe.wait_ge(s_ktd, n)
                for k in range(4):
                    ks = slice(k * P, (k + 1) * P)
                    for a in range(2):
                        tr(pj[:, 0, a, ks], CK[v][:, 4 * g + k, a * P:(a + 1) * P], ident[:, :])
                    last = tr(pj[0:ROPE, 1, 0, ks], CR[v][:, 4 * g + k, :], ident[:, :])
                last.then_inc(s_kt, 1)

            def cache_scores(n):
                s, g = n // TT, n % TT
                pe.wait_ge(s_kta, n + 1)
                pe.wait_ge(s_ktd, n + 1)
                pe.wait_ge(s_dse, n)
                out = pj[0:H, 1, 1, :]
                mm(out, qlat[:, 0, :, s], KC[n % 2][:, 0, :], start=True, stop=False)
                mm(out, qlat[:, 1, :, s], KC[n % 2][:, 1, :], start=False, stop=False)
                mm(out, qpd[0:ROPE, :, s], KR[n % 2], start=False, stop=True).then_inc(s_ds, 1)
                if g == TT - 1:
                    out = bk[0:H, 3, 0:1]
                    me = slice(T + s, T + s + 1)
                    pe.wait_ge(s_dvs, s)
                    mm(out, qlat[:, 0, :, s], ckvT[:, 0, me], start=True, stop=False)
                    mm(out, qlat[:, 1, :, s], ckvT[:, 1, me], start=False, stop=False)
                    mm(out, qpd[0:ROPE, :, s], kpeT[0:ROPE, me], start=False, stop=True).then_inc(s_ds, 1)

            def turn_weights(s):
                pe.wait_ge(s_dsa, s + 1)
                pe.wait_ge(s_dvd, s)
                for g in range(NPAGES):
                    tr(bk[:, 3, g * H:(g + 1) * H], drow[:, g * P:(g + 1) * P], ident[0:H, 0:H])
                tr(bk[0:1, 3, P:P + H], drow[:, PAST:PAST + 1], ident[0:H, 0:H]).then_inc(s_dpt, 1)

            def decode_values(s):
                v = s % 3
                pe.wait_ge(s_dpa, s + 1)
                pe.wait_ge(s_ckr, 16 * (s + 1))
                out = bk[0:H, 3, 0:KVL]
                for g in range(NPAGES):
                    mm(out, prT[:, g, :], CK[v][:, g, :], start=(g == 0), stop=False)
                mm(out, prT[0:1, NPAGES, :], ckr[0:1, :], start=False, stop=True).then_inc(s_dv, 1)

            def turn_values(s):
                pe.wait_ge(s_dvs, s + 1)
                if s + 1 < NS:
                    pe.wait_ge(s_dsd, s + 2)
                for a in range(2):
                    last = tr(bk[:, 3, a * H:(a + 1) * H], dval[:, a * P:(a + 1) * P], ident[0:H, 0:H])
                last.then_inc(s_dot, 1)

            pe.wait_ge(s_ba, B_L + 1 - 8)
            pe.wait_ge(s_qpd, 32)
            scores(0)
            for n in range(NSTEP):
                s, g = n // TT, n % TT
                turn_cache(n)
                turn_rows(n)
                if s >= 2 and g == 1:
                    turn_values(s - 2)
                if n + 1 < NSTEP:
                    scores(n + 1)
                if s >= 1 and g == 2:
                    turn_weights(s - 1)
                    row_values(n)
                if n >= 1:
                    cache_scores(n - 1)
                if s >= 1 and g == 3:
                    decode_values(s - 1)
                if s == 0 or g != 2:
                    row_values(n)
            cache_scores(NSTEP - 1)
            turn_values(NS - 2)
            turn_weights(NS - 1)
            decode_values(NS - 1)
            turn_values(NS - 1)
            pe.wait_ge(s_dvd, NS)
            for h in range(H):
                for a in range(2):
                    last = mm(bk[:, 3, P + h * NS:P + (h + 1) * NS], UV[:, a, h * P:(h + 1) * P], olat[:, a, h, :],
                              start=(a == 0), stop=(a == 1))
            last.then_inc(s_do, 1)
            out_tiles(1, OG)

        @block.gpsimd
        def _(pool):
            then, mark = counter(pool, s_pool)
            G = nc.gpsimd
            pool.wait_ge(s_const, 80)
            then(G.tensor_scalar(nw0, vecs[:, V_W0, :], -1.0, None, ALU.mult), s_zp)
            then(G.tensor_scalar(na0, vecs[:, V_A0, :], -1.0, None, ALU.mult), s_zp)
            then(G.tensor_scalar(omka, vecs[:, V_KA, :], -1.0, 1.0, ALU.mult, ALU.add), s_zp)
            then(G.memset(SAx[:, HD:2 * HD], 0.0), s_zero)
            then(G.memset(Vx[0][:, :, HD:2 * HD], 0.0), s_zero)
            then(G.memset(Vx[1][:, :, HD:2 * HD], 0.0), s_zero)
            for m in range(PAIRS):
                v = m % 2
                col = lambda n: vecs[:, n, m:m + 1]
                pool.wait_ge(s_pa, 4 * m + 2)
                if m >= 1:
                    pool.wait_ge(s_pd, 4 * m)
                    pool.wait_ge(s_rd, 3 * m)
                then(G.tensor_scalar(kmT, aT, col(V_KA), omka[:, m:m + 1], ALU.mult, ALU.add))
                pool.wait_ge(s_ra, 7 * m + 2)
                then(G.tensor_tensor(kmT, kmT, kT, ALU.mult), s_pp)
                pool.wait_ge(s_pd, 4 * m + 2)
                then(G.tensor_tensor(bT, kkT, aT, ALU.mult), s_pp)
                pool.wait_ge(s_pa, 4 * m + 4)
                pool.wait_ge(s_rd, 3 * m + 3)
                for q, x in enumerate((rT, kmT, vT, kkT, bT, ecum, bon[v], gT[v])):
                    last = G.tensor_copy(decbuf[:, q, m, :], x[:, T:N])
                    if q < 7:
                        mark(last)
                then(last, s_pp)
            bi = lambda q: dq[:, q, :].unsqueeze(1).to_broadcast([P, HD, HD])
            bj = lambda x: x.unsqueeze(2).to_broadcast([P, HD, HD])
            pool.wait_ge(s_dq, 32)
            mark(G.tensor_tensor(Wd2, bj(dq[:, 2, :]), bi(1), ALU.mult), s_dp)
            pool.wait_ge(s_dd, 1)
            mark(G.tensor_tensor(Sd, Sd, bi(5), ALU.mult), s_dp)
            pool.wait_ge(s_pidx, 1)
            pool.wait_ge(s_bm, B_L + 1)

            def gather(s_):
                off = bass.IndirectOffsetOnAxis(ap=pidx[:, s_:s_ + 1], axis=0)
                G.indirect_dma_start(CKg[s_ % 3], None, d["cache_c"], off).then_inc(s_ck[s_ % 3], 16)
                G.indirect_dma_start(CRg[s_ % 3], None, d["cache_r"], off).then_inc(s_ck[s_ % 3], 16)

            for s_ in range(NS):
                if s_ >= 3:
                    pool.wait_ge(s_dv, s_ - 2)
                gather(s_)

        @block.vector
        def _(dve):
            then, mark = counter(dve, s_dve)
            V = nc.vector
            dve.wait_ge(s_const, 80)

            def ada(g):
                dve.wait_ge(s_ada_mm, g + 1)
                mark(V.tensor_tensor(mod[:, ADA_MT * g:ADA_MT * (g + 1), :],
                                     bk[:, g % 2, 0:36].rearrange("p (t n) -> p t n", n=9),
                                     adab[:, ADA_MT * g:ADA_MT * (g + 1)].unsqueeze(2).to_broadcast([P, ADA_MT, 9]),
                                     ALU.add), s_ada_out)
            ada(0)
            ada(1)
            dve.wait_ge(s_ss, 1)
            then(V.tensor_scalar(two(stat), pjs[0], 1.0 / D, EPS, ALU.mult, ALU.add), s_ms)
            dve.wait_ge(s_rstd, 1)
            dve.wait_ge(s_x, 16)
            then(V.tensor_tensor(R1[:, :, :], R0[:, :, :], stat.unsqueeze(1).to_broadcast([P, KT, N]), ALU.mult))
            for g in range(2, ADA_FIRST):
                ada(g)
            dve.wait_ge(s_ada_out, ADA_FIRST)
            then(V.tensor_scalar(A0[:, :, :], mod[:, M_SC0:M_SC0 + KT, :], 1.0, None, ALU.add))
            then(V.tensor_tensor(A0[:, :, :], A0[:, :, :],
                                 vecs[:, V_PRE0, :].unsqueeze(2).to_broadcast([P, KT, 9]), ALU.mult))
            for k in range(KT):
                mark(V.tensor_scalar(R1[:, k, 0:T], R1[:, k, 0:T], A0[:, k, 0:1], mod[:, M_SH0 + k, 0:1],
                                     ALU.mult, ALU.add))
            then(V.tensor_tensor(R1[:, :, T:N], R1[:, :, T:N], A0[:, :, 1:9], ALU.mult))
            then(V.tensor_tensor(R1[:, :, T:N], R1[:, :, T:N], mod[:, M_SH0:M_SH0 + KT, 1:9], ALU.add))
            then(V.tensor_copy(shout, R1[:, :, T - 1:N]), s_shout)
            mark(V.tensor_tensor(R2[:, :, 1:T], R1[:, :, 0:T - 1], R1[:, :, 1:T], ALU.subtract))
            mark(V.tensor_scalar(R2[:, :, 0:1], R1[:, :, 0:1], -1.0, None, ALU.mult))
            dve.wait_ge(s_l1, 32)
            then(V.tensor_tensor(R2[:, :, T:N], shin, R1[:, :, T:N], ALU.subtract))
            for n, (e, dst) in enumerate(((4, 0), (5, 1), (2, 2), (3, 3), (0, 0), (1, 1))):
                if n >= 4:
                    dve.wait_ge(s_hid, n - 3)
                for k in range(KT):
                    last = V.scalar_tensor_tensor(XM[:, dst, k, :], R2[:, k, :], vecs[:, V_MU + e, k:k + 1],
                                                  R1[:, k, :], ALU.mult, ALU.add)
                    if k < KT - 1:
                        mark(last)
                then(last, s_xm)
            dve.wait_ge(s_hida, 1)
            then(V.tensor_scalar(lhid[0:LORA], lhid[0:LORA], -2.0, 1.0, ALU.mult, ALU.add), s_hidr)

            def chunk(x, t0=0):
                return x[:, 0:T].rearrange("p (c t) -> p c t", c=NCH)

            def prep(m, part):
                v = m % 2
                col = lambda n: vecs[:, n, m:m + 1]
                if part == "g":
                    dve.wait_ge(s_pa, 4 * m + 1)
                    if m >= 1:
                        dve.wait_ge(s_pp, 3 * m)
                        dve.wait_ge(s_pjm, NUSE * m)
                    then(V.tensor_tensor(two(gT[v]), pjs[1], two(gT[v]), ALU.mult), s_rd)
                if part == "cum":
                    dve.wait_ge(s_pa, 4 * m + 2)
                    dve.wait_ge(s_mask, 112)
                    then(V.tensor_tensor_scan(cum, scanm, sg, 0.0, ALU.mult, ALU.add))
                    then(V.tensor_tensor(cumx, cum, sg, ALU.subtract), s_pd)
                if part == "ss":
                    dve.wait_ge(s_pjm, NUSE * m + U_SS + 1)
                    then(V.tensor_scalar(two(sqk), pjs[0], 1e-24, None, ALU.max), s_rd)
                if part == "kk":
                    dve.wait_ge(s_pa, 4 * m + 3)
                    then(V.scalar_tensor_tensor(kkT, kT, col(V_KK), sqk, ALU.mult, ALU.mult), s_pd)
                if part == "rk":
                    dve.wait_ge(s_pp, 3 * m + 1)
                    then(V.scalar_tensor_tensor(tmb, rT, col(V_RK), kmT, ALU.mult, ALU.mult), s_pd)
                if part == "bon":
                    dve.wait_ge(s_pjm, NUSE * m + U_BO + 1)
                    then(V.tensor_tensor(two(bon[v]), pjs[1], two(vT), ALU.mult), s_rd)
                if part == "ar":
                    dve.wait_ge(s_pa, 4 * m + 4)
                    then(V.tensor_tensor(AR[v][:, :, 0, :], chunk(kkT), chunk(cumx), ALU.mult))
                    then(V.tensor_tensor(AR[v][:, :, 1, :], chunk(rT), chunk(ecum), ALU.mult))
                    then(V.tensor_copy(pc[:, v, :], ecum[:, C - 1:T:C]))
                if part == "bt":
                    dve.wait_ge(s_pp, 3 * m + 2)
                    then(V.tensor_tensor(Bt, bT[:, 0:T], einv[:, 0:T], ALU.mult))
                    then(V.tensor_tensor(Kt_, kmT[:, 0:T], einv[:, 0:T], ALU.mult))
                if part == "bh":
                    pcb = pc[:, v, :].unsqueeze(2).to_broadcast([P, NCH, C])
                    then(V.tensor_tensor(chunk(cum), chunk(Bt), pcb, ALU.mult))
                    then(V.tensor_tensor(chunk(sqk), chunk(Kt_), pcb, ALU.mult), s_pd)

            def masks(m):
                if m == 0:
                    dve.wait_ge(s_store, 16)
                for n in range(4):
                    half, h = n // 2, n % 2
                    dve.wait_ge(s_M, 5 * m + n + 1)
                    b0 = h * TT + 2 * half
                    then(V.tensor_tensor(MM[:, b0:b0 + 2, :, :].rearrange("p b q t -> p b (q t)"),
                                         bk[:, n, :].rearrange("p (b x) -> p b x", b=2),
                                         maskM.unsqueeze(1).to_broadcast([P, 2, 256]), ALU.mult), s_Me)
                dve.wait_ge(s_M, 5 * m + 5)
                then(V.tensor_tensor(Mab.rearrange("p (h b) t -> p h b t", h=2),
                                     bk[:, 0:2, 0:256].rearrange("p h (b t) -> p h b t", b=TT),
                                     lowm.unsqueeze(1).unsqueeze(1).to_broadcast([P, 2, TT, C]), ALU.mult), s_Me)
                idb = id64.unsqueeze(1).to_broadcast([P, BLK, C])
                for x, dst, a in ((MM[:, :, 0, :], Tt, 1), (Mab, Tm, 0)):
                    then(V.scalar_tensor_tensor(dst, x, -1.0, lv1[:, a, :].unsqueeze(1).to_broadcast([P, BLK, C]),
                                                ALU.mult, ALU.mult))
                    then(V.tensor_tensor(dst, dst, idb, ALU.add), s_Te if a else None)

            def level_z(m, l):
                dve.wait_ge(s_Z, NLEV * m + l + 1)
                then(V.tensor_tensor(Zt, bk[:, 0, :].rearrange("p (b t) -> p b t", b=BLK),
                                     lvm[:, l, :].unsqueeze(1).to_broadcast([P, BLK, C]), ALU.mult), s_Ze)

            def level_t(m, l):
                n = (2 * NLEV - 1) * m + 2 * l
                dve.wait_ge(s_T, n + 1)
                mark(V.tensor_tensor(Tt, Tt, bk[:, 2, :].rearrange("p (b t) -> p b t", b=BLK), ALU.subtract), s_Te)
                if l < NLEV - 1:
                    dve.wait_ge(s_T, n + 2)
                    mark(V.tensor_tensor(Tm, Tm, bk[:, 1, :].rearrange("p (b t) -> p b t", b=BLK), ALU.subtract))

            def scan(m, ch):
                v = m % 2
                n = 4 * (NCH * m + ch)
                dve.wait_ge(s_sc, n + 3)
                then(V.tensor_tensor(stmp, bk[:, 1, 0:P], bones, ALU.mult))
                dve.wait_ge(s_sc, n + 4)
                then(V.scalar_tensor_tensor(S, S, pc[:, v, ch:ch + 1], stmp, ALU.mult, ALU.add), s_Se)

            def ada_between(j):
                g = ADA_FIRST + j
                dve.wait_ge(s_adt, j + 1)
                mark(V.tensor_tensor(mod[:, ADA_MT * g:ADA_MT * (g + 1), :],
                                     pj[:, 0, 1, 0:36].rearrange("p (t n) -> p t n", n=9),
                                     adab[:, ADA_MT * g:ADA_MT * (g + 1)].unsqueeze(2).to_broadcast([P, ADA_MT, 9]),
                                     ALU.add), s_ada_out)

            def norm(m):
                v = m % 2
                dve.wait_ge(s_gnp, 2 * m + 1)
                then(V.scalar_tensor_tensor(yc, bk[:, 0, :], -1.0 / HD, yc, ALU.mult, ALU.add), s_gnd)
                ada_between(m)
                dve.wait_ge(s_gna, 3 * m + 3)
                then(V.tensor_tensor(yc, yc, ysq, ALU.mult))
                then(V.tensor_scalar(yc, yc, vecs[:, V_GNW, m:m + 1], vecs[:, V_GNB, m:m + 1], ALU.mult, ALU.add))
                then(V.tensor_tensor(yc, yc, bon[v][:, 0:T], ALU.add))
                then(V.tensor_tensor(R1[:, m, 0:T], yc, gT[v][:, 0:T], ALU.mult), s_yT)

            for part in ("g", "cum", "ss", "kk", "rk", "bon", "ar", "bt", "bh"):
                prep(0, part)
            for m in range(PAIRS):
                more = m + 1 < PAIRS
                if m >= 1:
                    dve.wait_ge(s_So, m)
                then(V.memset(S, 0.0), s_Se)
                masks(m)
                for l in range(NLEV):
                    level_z(m, l)
                    if more and l == 3:
                        prep(m + 1, "g")
                    level_t(m, l)
                if more:
                    prep(m + 1, "cum")
                for ch in range(NCH):
                    scan(m, ch)
                    if more and 1 <= ch <= 7:
                        prep(m + 1, (None, "ss", "kk", "rk", "bon", "ar", None, "bt")[ch])
                if more:
                    prep(m + 1, "bh")
                norm(m)

            bi = lambda q: dq[:, q, :].unsqueeze(1).to_broadcast([P, HD, HD])
            bj = lambda x: x.unsqueeze(2).to_broadcast([P, HD, HD])
            dve.wait_ge(s_pt, 16)
            dve.wait_ge(s_cb, 128)
            then(V.tensor_scalar(pidx[:, :], ptab[:, :], 8.0, prow[:, 0:1], ALU.mult, ALU.add), s_pidx)
            dve.wait_ge(s_dq, 32)
            dve.wait_ge(s_sd, 16)
            then(V.tensor_tensor(Wd1, Sd, bi(3), ALU.mult), s_dd)
            then(V.tensor_reduce(sa, Wd1, AX_X, ALU.add))
            then(V.tensor_tensor(Wd1, bj(sa), bi(4), ALU.mult), s_dd)
            dve.wait_ge(s_dp, 1)
            then(V.tensor_tensor(Wd2, Wd2, Wd1, ALU.subtract), s_dd)
            dve.wait_ge(s_dp, 2)
            then(V.tensor_tensor(Sd, Sd, Wd2, ALU.add), s_dd)
            then(V.tensor_tensor(Wd1, Sd, bi(0), ALU.mult))
            then(V.tensor_reduce(yd, Wd1, AX_X, ALU.add))
            then(V.bn_stats(bst, yd))
            then(V.bn_aggr(bag, bst), s_dd)
            dve.wait_ge(s_dr, 1)
            then(V.tensor_scalar(yd, yd, bag[:, 0:1], rsd, ALU.subtract, ALU.mult), s_dd)
            dve.wait_ge(s_ydt, 1)
            r1d = R1[:, :, T:N]
            bc = lambda x: x.unsqueeze(2).to_broadcast([P, KT, NS])
            then(V.tensor_tensor(r1d, pj[:, 1, 0, 0:HD].rearrange("p (m s) -> p m s", m=PAIRS), bc(vecs[:, V_GNW, :]), ALU.mult))
            then(V.tensor_tensor(r1d, r1d, bc(vecs[:, V_GNB, :]), ALU.add))
            then(V.tensor_tensor(r1d, r1d, decbuf[:, 6, :, :], ALU.add))
            then(V.tensor_tensor(r1d, r1d, decbuf[:, 7, :, :], ALU.mult), s_r1)

            nn = [0]

            def mean(width):
                nn[0] += 1
                dve.wait_ge(s_ns, nn[0])
                then(V.tensor_scalar(two(st), bk[:, 2:4, 0:HALF], 1.0 / width, EPS, ALU.mult, ALU.add), s_nd)
                return nn[0]

            all_k = lambda x: x.unsqueeze(1).to_broadcast([P, KT, N])
            b9 = lambda x: x.unsqueeze(2).to_broadcast([P, KT, 9])

            def residual(layer, gate, post):
                n = mean(D)
                then(V.tensor_tensor(A0[:, :, :], mod[:, gate:gate + KT, :], b9(vecs[:, post, :]), ALU.mult))
                dve.wait_ge(s_na, n)
                dve.wait_ge(s_oa, KT * (layer + 1))
                then(V.tensor_tensor(Y, Y, all_k(st), ALU.mult))
                dve.wait_ge(s_xr, 16)
                for k in range(KT):
                    mark(V.scalar_tensor_tensor(R0[:, k, 0:T], Y[:, k, 0:T], A0[:, k, 0:1], R0[:, k, 0:T], ALU.mult, ALU.add))
                then(V.tensor_tensor(Y[:, :, T:N], Y[:, :, T:N], A0[:, :, 1:9], ALU.mult))
                then(V.tensor_tensor(R0[:, :, T:N], R0[:, :, T:N], Y[:, :, T:N], ALU.add), s_res)

            dve.wait_ge(s_adb, ADA_MT * NADA)
            residual(0, M_G0, V_POST0)
            n = mean(D)
            for a, sc, g in ((A0, M_SC1, V_PRE1), (A1, M_SCK, V_KVN)):
                then(V.tensor_scalar(a[:, :, :], mod[:, sc:sc + KT, :], 1.0, None, ALU.add))
                then(V.tensor_tensor(a[:, :, :], a[:, :, :], b9(vecs[:, g, :]), ALU.mult))
            dve.wait_ge(s_na, n)
            then(V.tensor_tensor(HN, R0[:, :, :], all_k(st), ALU.mult), s_hh)
            for k in range(KT):
                mark(V.tensor_scalar(HK[:, k, 0:T], HN[:, k, 0:T], A1[:, k, 0:1], mod[:, M_SHK + k, 0:1], ALU.mult, ALU.add))
            dve.wait_ge(s_dso, 16)
            for x, a, sh, nm in ((H1, A0, M_SH1, None), (HK, A1, M_SHK, s_hh)):
                then(V.tensor_tensor(x[:, :, T:N], HN[:, :, T:N], a[:, :, 1:9], ALU.mult))
                then(V.tensor_tensor(x[:, :, T:N], x[:, :, T:N], mod[:, sh:sh + KT, 1:9], ALU.add), nm)

            for t in range(5):
                c = P if t < TT else NS
                ps = pj[0:c, t % 2, 0, :]
                dve.wait_ge(s_kva, t + 1)
                then(V.tensor_scalar(kss[0:c, 1:2], kss[0:c, 0:1], 1.0 / KVL, EPS, ALU.mult, ALU.add), s_kvd)
                mark(V.tensor_tensor(kvn[0:c, t, 256:320], ps[:, 256:320], cosN[0:c, t, :], ALU.mult))
                then(V.tensor_tensor(rt64[0:c], ps[:, 320:384], sinN[0:c, t, :], ALU.mult))
                then(V.tensor_tensor(kvn[0:c, t, 256:320], kvn[0:c, t, 256:320], rt64[0:c], ALU.add))
                mark(V.tensor_copy(kvn[0:c, t, 320:384], kvn[0:c, t, 256:320]))
                dve.wait_ge(s_kvr, t + 1)
                then(V.scalar_tensor_tensor(kvn[0:c, t, 0:KVL], ps[:, 0:KVL], kss[0:c, 1:2], kvg[0:c], ALU.mult, ALU.mult), s_kvn)

            n = mean(QL)
            for t in range(KT):
                dve.wait_ge(s_ba, QT + t + 1)
                then(V.tensor_tensor(two(GATE[:, t, :]), two(GATE[:, t, :]), pjs[(QT + t) % 2], ALU.mult), s_bd)
                if t == 0:
                    dve.wait_ge(s_na, n)
                    then(V.tensor_tensor(qa, qa, st.unsqueeze(1).to_broadcast([P, QT, N]), ALU.mult))
                    for k in range(QT):
                        last = V.tensor_scalar(qa[:, k, :], qa[:, k, :], qng[:, k:k + 1], None, ALU.mult)
                        if k < QT - 1:
                            mark(last)
                    then(last, s_qn)
            for i in range(4):
                dve.wait_ge(s_bm, B_PE + 2 * i + 2)
                then(V.tensor_tensor(two(QP[:, i, :]), pjs[0], two(cosT), ALU.mult))
                then(V.tensor_tensor(two(rtmp), pjs[1], two(sinT), ALU.mult))
                then(V.tensor_tensor(QP[:, i, :], QP[:, i, :], rtmp, ALU.add), s_bd)

            def rows(n):
                w = (n % TT + 1) * P
                dve.wait_ge(s_sm, n + 1)
                dve.wait_ge(s_sa1, n)
                then(V.tensor_tensor(bk[:, 0, w - P:w], bk[:, 0, w - P:w], causal, ALU.add))
                then(V.tensor_reduce(mx[:, 0:1], bk[:, 0, 0:w], AX_X, ALU.max))
                then(V.tensor_scalar(nmx[:, 0:1], mx[:, 0:1], -SCALE, None, ALU.mult), s_sd1)
                dve.wait_ge(s_sa1, n + 1)
                then(V.reciprocal(mx[:, 1:2], den[:, 0:1]))
                then(V.tensor_scalar(PN[:, 0:w], PN[:, 0:w], mx[:, 1:2], None, ALU.mult), s_sd2)

            def gate_head(h):
                dve.wait_ge(s_po, TT * (h + 1))
                then(V.tensor_tensor(OG[:, h, 0:T], bk[:, 2, :], GATE[:, h, 0:T], ALU.mult), s_pog)

            def cache_turned(n):
                dve.wait_ge(s_kt, n + 1)
                if n >= 2:
                    dve.wait_ge(s_ds, scored(n - 2))
                mark(V.tensor_copy(KR[n % 2], pj[0:ROPE, 1, 0, :]), s_ktd)

            def scores_stored(n):
                s, g = n // TT, n % TT
                dve.wait_ge(s_ds, scored(n))
                if g == 0:
                    dve.wait_ge(s_dpt, s)
                mark(V.tensor_copy(drow[:, g * 512:(g + 1) * 512], pj[0:H, 1, 1, :]), s_dse)

            def decode_max(s):
                dve.wait_ge(s_ds, 5 * s + 5)
                then(V.tensor_copy(drow[:, PAST:PAST + 1], bk[0:H, 3, 0:1]))
                dve.wait_ge(s_dse, TT * (s + 1))
                then(V.tensor_reduce(dmx, drow, AX_X, ALU.max))
                then(V.tensor_scalar(dnm, dmx, -SCALE, None, ALU.mult), s_dsd)

            def scale_values(s):
                dve.wait_ge(s_dv, s + 1)
                dve.wait_ge(s_dot, s)
                then(V.reciprocal(drc, dden))
                then(V.tensor_scalar(dval, bk[0:H, 3, 0:KVL], drc, None, ALU.mult), s_dvs)

            def decode_latent(s):
                dve.wait_ge(s_dot, s + 1)
                then(V.tensor_copy(olat[:, :, :, s], bk[:, 3, 0:2 * H].rearrange("p (a h) -> p a h", a=2)), s_dvd)

            dve.wait_ge(s_kvo, 160)
            rows(0)
            for n in range(NSTEP):
                s, g = n // TT, n % TT
                if s >= 1 and g == 0:
                    gate_head(s - 1)
                cache_turned(n)
                if s >= 2 and g == 0:
                    scale_values(s - 2)
                if n >= 2 and g != 1:
                    scores_stored(n - 2)
                if n + 1 < NSTEP:
                    rows(n + 1)
                if s >= 1 and g == 0:
                    scores_stored(n - 1)
                    decode_max(s - 1)
                if s >= 2 and g == 1:
                    decode_latent(s - 2)
            gate_head(H - 1)
            scale_values(NS - 2)
            scores_stored(NSTEP - 2)
            scores_stored(NSTEP - 1)
            decode_max(NS - 1)
            decode_latent(NS - 2)
            scale_values(NS - 1)
            decode_latent(NS - 1)
            dve.wait_ge(s_do, 1)
            then(V.tensor_tensor(OG[:, :, T:N], bk[:, 3, P:P + H * NS].rearrange("p (h s) -> p h s", h=H),
                                 GATE[:, :, T:N], ALU.mult), s_pog)
            residual(1, M_G1, V_POST1)


def host_layout(i):
    f = np.float32

    def feat(a):
        a = np.asarray(a)
        lead = a.shape[:-1]
        a = a.reshape(*lead, KT, P)
        return np.moveaxis(a, -1, 0)

    def cols(a, width):
        k, n = a.shape
        return np.ascontiguousarray(a.reshape(k // P, P, n // width, width).transpose(2, 1, 0, 3))

    r = {}
    x = np.concatenate([i["x_prompt"][0], i["x_sample"][:, 0]], 0)
    r["xT"] = np.ascontiguousarray(x.T.reshape(KT, P, N).transpose(1, 0, 2))
    c = np.concatenate([i["c_prompt"], i["c_sample"]], 0)
    r["cT"] = np.ascontiguousarray(c.T.reshape(KT, P, 1 + NS).transpose(1, 0, 2))
    r["shiftT"] = np.ascontiguousarray(i["state_shift"][0].T.reshape(KT, P, NS).transpose(1, 0, 2))
    ada = np.concatenate([i["ada_w"][0], i["ada_w"][1], i["kv_ada_w"]], 1)
    r["ada"] = cols(ada, ADA_COLS).reshape(ADA_GROUPS, P, 4096)
    r["adab"] = np.ascontiguousarray(np.concatenate([i["ada_b"][0], i["ada_b"][1], i["kv_ada_b"]]).reshape(MOD_TILES, P).T)
    vs = [i["norm_pre"][0], i["norm_pre"][1], i["norm_post"][0], i["norm_post"][1], *i["a_mu"][0],
          i["a_w0"][0], i["a_a0"][0], i["a_k_k"][0], i["a_k_a"][0], i["a_r_k"][0].reshape(-1),
          i["a_gn_w"][0], i["a_gn_b"][0], i["kv_norm"]]
    r["vecs"] = np.ascontiguousarray(np.stack([v.reshape(KT, P).T for v in vs], 1))
    w = i["a_w_in"][0]
    r["w_in"] = np.ascontiguousarray(w.reshape(4, KT, P, PAIRS, P).transpose(3, 2, 0, 1, 4)).reshape(PAIRS, P, 4096)
    l1 = np.concatenate([i["a_w1"][0], i["a_a1"][0]], 1)
    r["lora1"] = np.ascontiguousarray(l1.reshape(KT, P, P).transpose(1, 0, 2))
    l2 = np.concatenate([i["a_w2"][0], i["a_a2"][0]], 0)
    r["lora2"] = np.ascontiguousarray(l2.reshape(P, PAIRS, P).transpose(1, 0, 2))
    st = i["state_wkv"][0].reshape(NS, PAIRS, 2, HD, HD).transpose(2, 1, 0, 3, 4)
    r["Sd"] = np.ascontiguousarray(st.reshape(P, HD, HD))
    r["w_out"] = cols(i["a_w_out"][0], 512).reshape(2, P, 4096)
    r["b_w_out"] = cols(i["b_w_out"][0], 512).reshape(2, P, 4096)
    swap = np.r_[ROPE // 2:ROPE, 0:ROPE // 2]
    kva = i["kv_w_a"]
    r["kv_w_a"] = cols(np.concatenate([kva, kva[:, KVL + swap]], 1), 384).reshape(1, P, KT * 384)
    bw = i["b_w_in"][0]
    pad = np.zeros((P, KT * 128), f)
    r["b_w_in"] = np.stack([np.concatenate([cols(bw[:, 0:QL], QL).reshape(P, KT * QL), pad], 1),
                            *cols(bw[:, QL:], 512).reshape(2, P, 4096)])
    wq = i["b_w_q"][0]
    pe = wq[:, :, NOPE:]
    r["w_q"] = np.stack([cols(wq[:, :, 0:NOPE].reshape(QL, H * NOPE), H * NOPE).reshape(P, QT * D),
                         cols(np.concatenate([pe.reshape(QL, -1), pe[:, :, swap].reshape(QL, -1)], 1), D).reshape(P, QT * D)])
    kvb = i["kv_w_b"]
    uk = kvb[:, :, 0:NOPE]
    r["uk"] = np.concatenate([uk.reshape(2, P, H * NOPE).transpose(1, 0, 2).reshape(P, -1),
                              uk.transpose(2, 1, 0).reshape(P, -1)], 1)[None]
    r["uv"] = np.ascontiguousarray(kvb[:, :, NOPE:].reshape(2, P, H * P).transpose(1, 0, 2))
    r["kvg"] = np.broadcast_to(i["kv_a_norm"], (P, KVL)).copy()
    r["qng"] = np.ascontiguousarray(i["b_q_norm"][0].reshape(QT, P).T)
    r["page_table"] = np.ascontiguousarray(np.repeat(i["page_table"].T, PAGE // 16, axis=0))
    r["cache_c"] = i["cache_kv_latent"].reshape(-1, NPAGES * KVL)
    r["cache_r"] = i["cache_k_rope"].reshape(-1, NPAGES * ROPE)
    inv = f(ROPE_THETA) ** (-np.arange(ROPE // 2, dtype=f) / f(ROPE // 2))
    pos = np.concatenate([np.arange(T), np.full(NS, PAST)]).astype(f)
    ang = pos[:, None] * inv[None, :]
    cs = np.concatenate([np.cos(ang), np.cos(ang)], 1).astype(f)
    sn = np.concatenate([-np.sin(ang), np.sin(ang)], 1).astype(f)
    r["cosT"], r["sinT"] = (np.concatenate([a.T, a.T], 0).copy() for a in (cs, sn))
    r["cosN"], r["sinN"] = (np.ascontiguousarray(np.concatenate([a, np.zeros((5 * P - N, ROPE), f)], 0)
                            .reshape(5, P, ROPE).transpose(1, 0, 2)) for a in (cs, sn))
    r["causal"] = np.where(np.arange(P)[None, :] <= np.arange(P)[:, None], 0, NEG).astype(f)
    r["prow"] = (np.arange(P) % 8).astype(f)[:, None]
    r["ident"] = np.eye(P, dtype=f)
    r["ones"] = np.ones((P, P), f)
    s, t = np.meshgrid(np.arange(P) % C, np.arange(C), indexing="ij")
    r["maskM"] = np.concatenate([t > s, t >= s, t > s, t >= s], 1).astype(f)
    r["lowm"] = (t < s).astype(f)
    off = lambda a, b, m: (a // (2 * m) == b // (2 * m)) & (a % (2 * m) >= m) & (b % (2 * m) < m)
    r["lv1"] = np.stack([off(s, t, 1), off(t, s, 1)], 1).astype(f)
    r["lvm"] = np.stack([off(t, s, m) for m in LEVELS], 1).astype(f)
    r["id64"] = (s == t).astype(f)
    hb = np.arange(P) // HD
    r["bones"] = (hb[:, None] == hb[None, :]).astype(f)
    r["scanm"] = np.broadcast_to(np.where(np.arange(N) < T, np.arange(N) % C != 0, False).astype(f), (P, N)).copy()
    return r


OUTS = {"shift": (P, KT, 1 + NS), "wkv_p": (2 * PAIRS, HD, HD), "wkv_s": (P, HD, HD), "ckv": (N, KVL),
        "kpe": (N, ROPE), "y": (P, KT, N)}


def kernel(**inputs):
    import concourse.bacc as bacc
    from concourse.bass_utils import run_bass_kernel_spmd

    nc = bacc.Bacc("TRN2", target_bir_lowering=False, num_devices=1)
    arrays = host_layout({k: np.asarray(v) for k, v in inputs.items()})
    d = {k: nc.dram_tensor(f"in_{k}", a.shape, mybir.dt.from_np(a.dtype), kind="ExternalInput").ap()
         for k, a in arrays.items()}
    o = {k: nc.dram_tensor(f"out_{k}", s, F32, kind="ExternalOutput").ap() for k, s in OUTS.items()}
    build(nc, d, o)
    r = run_bass_kernel_spmd(nc, [{f"in_{k}": a for k, a in arrays.items()}], core_ids=[0]).results[0]
    sh = np.asarray(r["out_shift"]).transpose(2, 1, 0).reshape(1 + NS, D)
    y = np.asarray(r["out_y"]).transpose(2, 1, 0).reshape(N, D)
    wkv_s = np.asarray(r["out_wkv_s"]).reshape(2, PAIRS, NS, HD, HD).transpose(2, 1, 0, 3, 4).reshape(1, NS, 2 * PAIRS, HD, HD)
    ckv, kpe = np.asarray(r["out_ckv"]), np.asarray(r["out_kpe"])
    return (y[None, 0:T], y[T:, None], np.asarray(r["out_wkv_p"])[None, None], sh[0][None, None],
            ckv[None, 0:T], kpe[None, 0:T], wkv_s, sh[1:][None], ckv[T:, None], kpe[T:, None])
```

```python
from contextlib import ExitStack

import numpy as np

import concourse.bass as bass
from concourse import mybir

F32 = mybir.dt.float32
I32 = mybir.dt.int32
ALU = mybir.AluOpType
ACT = mybir.ActivationFunctionType
AX_X = mybir.AxisListType.X

P = 128
D = 1024
KT = D // P
T = 512
NS = 8
N = T + NS
HALF = N // 2
HD = 64
PAIRS = D // P
C = 64
NCH = T // C
TT = T // P
BLK = 2 * TT
LEVELS = (2, 4, 8, 16, 32)
NLEV = len(LEVELS)
LORA = 64
GN_EPS = 64e-5
EPS = 1e-6
H = 8
NOPE = 128
ROPE = 64
QL = 384
QT = QL // P
KVL = 256
ROPE_THETA = 10000.0
SCALE = float(NOPE + ROPE) ** -0.5
PAGE = 128
NPAGES = 16
PAST = NPAGES * PAGE
NEG = -1e30
(V_PRE0, V_PRE1, V_POST0, V_POST1, V_MU, V_W0, V_A0, V_KK, V_KA, V_RK, V_GNW, V_GNB, V_KVN) = (
    0, 1, 2, 3, 4, 10, 11, 12, 13, 14, 15, 16, 17)
NVEC = 18
ADA_COLS = 512
ADA_GROUPS = 8 * D // ADA_COLS
ADA_MT = ADA_COLS // P
MOD_TILES = 8 * KT
M_SH0, M_SC0, M_G0, M_SH1, M_SC1, M_G1, M_SHK, M_SCK = (KT * i for i in range(8))
E05 = float(np.exp(np.float32(-0.5)))
ADA_FIRST = 4
ADA_PAIRS = PAIRS
U_R, U_K, U_W, U_A, U_V, U_SS, U_G, U_TV, U_BO, U_TB = range(10)
NUSE = 10
ARENA = 9580


def build(nc, d, o):
    ctx = ExitStack()
    with ctx:
        def sb(name, shape, dt=F32):
            return ctx.enter_context(nc.sbuf_tensor(name, shape, dt))

        def sem(name):
            return ctx.enter_context(nc.semaphore(name))

        ring = sb("ring", [P, 3, 4096])
        R0 = sb("R0", [P, KT, N])
        R1 = sb("R1", [P, KT, N])
        R2 = sb("R2", [P, KT, N])
        XM = sb("XM", [P, 4, KT, N])
        vecs = sb("vecs", [P, NVEC, KT])
        ident = sb("ident", [P, P])
        ones = sb("ones", [P, P])
        cT = sb("cT", [P, KT, 1 + NS])
        adab = sb("adab", [P, MOD_TILES])
        mod = sb("mod", [P, MOD_TILES, 1 + NS])
        A0 = sb("A0", [P, KT, 1 + NS])
        decbuf = sb("decbuf", [P, 8, PAIRS, NS])
        arena = sb("arena", [P, ARENA])

        def cutter(flat, size):
            used = [0]

            def cut(n):
                a = flat[:, used[0]:used[0] + n]
                used[0] += n
                assert used[0] <= size, (used[0], size)
                return a
            return cut

        cutA = cutter(arena, ARENA)
        cutX = cutter(ring[:, 2, :], 4096)
        cut0 = cutter(R0[:, :, :].rearrange("p a b -> p (a b)"), KT * N)
        cut2 = cutter(R2[:, :, :].rearrange("p a b -> p (a b)"), KT * N)

        maskM = cutA(256)
        lowm = cutA(C)
        lv1 = cutA(2 * C).rearrange("p (a t) -> p a t", a=2)
        lvm = cutA(NLEV * C).rearrange("p (l t) -> p l t", l=NLEV)
        id64 = cutA(C)
        bones = cutA(P)
        scanm = cutA(N)
        omka, nw0, na0 = cutA(KT), cutA(KT), cutA(KT)
        lhid = cutA(N)
        lora2 = cutA(2 * P).rearrange("p (s e) -> p s e", s=2)
        stat = arena[:, ARENA - N:ARENA]
        SAx = cutA(192)
        rhs = cutA(P)
        SS = [cutA(P) for _ in range(2)]
        Sout = rhs
        AR = [cutA(2 * T).rearrange("p (c a t) -> p c a t", c=NCH, a=2) for _ in range(2)]
        Vx = [cutA(TT * 192).rearrange("p (c x) -> p c x", c=TT) for _ in range(2)]
        BK = [cutA(2 * T).rearrange("p (a c j) -> p a c j", a=2, c=TT) for _ in range(2)]
        pc = cutA(2 * NCH).rearrange("p (s c) -> p s c", s=2)
        MM = cutX(BLK * 256).rearrange("p (b q t) -> p b q t", b=BLK, q=4)
        Mab, Tm, Tt, Zt = (cutX(BLK * C).rearrange("p (b t) -> p b t", b=BLK) for _ in range(4))
        adarow = Mab.rearrange("p b t -> p (b t)")[0:9]
        rT, kT, vT, bT, kmT = (cut0(N) for _ in range(5))
        wa = cut0(2 * N).rearrange("p (a n) -> p a n", a=2)
        sg, aT = wa[:, 0, :], wa[:, 1, :]
        cum, cumx = cut2(N), sg
        ecum, einv = cut0(N), cut2(N)
        kkT, sqk = cut2(N), cut2(N)
        tmb = sqk
        gT = [cut2(N) for _ in range(2)]
        bon = [cut2(N) for _ in range(2)]
        Bt, Kt_ = cutA(T), cutA(T)
        arow = [ring[0:9, 2, 2048 + 512 * i:2560 + 512 * i] for i in range(2)]
        yc = Zt.rearrange("p b t -> p (b t)")
        ysq = Tm.rearrange("p b t -> p (b t)")
        lora1 = ring[:, 2, 0:KT * P].rearrange("p (k e) -> p k e", k=KT)
        shin = ring[:, 2, KT * P:KT * P + KT * NS].rearrange("p (k n) -> p k n", k=KT)
        shout = ring[:, 2, 1200:1200 + KT * (1 + NS)].rearrange("p (k n) -> p k n", k=KT)

        pj = ctx.enter_context(nc.psum_tensor("pj", [P, 2, 2, 512], F32))
        bk = ctx.enter_context(nc.psum_tensor("bk", [P, 4, 512], F32))
        pjs = [pj[:, s, :, 0:HALF] for s in range(2)]

        def two(ap):
            return ap.rearrange("p (a n) -> p a n", a=2)

        Sd = XM[:, 0, :, :].rearrange("p k n -> p (k n)")[:, 0:HD * HD].rearrange("p (i j) -> p i j", i=HD)
        Wd1 = XM[:, 1, :, :].rearrange("p k n -> p (k n)")[:, 0:HD * HD].rearrange("p (i j) -> p i j", i=HD)
        Wd2 = XM[:, 2, :, :].rearrange("p k n -> p (k n)")[:, 0:HD * HD].rearrange("p (i j) -> p i j", i=HD)
        Y = XM[:, 3, :, :]
        GATE = XM[:, 3, :, :]
        HN = XM[:, 1, :, :]
        HK = XM[:, 2, :, :]
        H1 = XM[:, 0, :, :]
        SQ = R2[:, :, :]
        QN = XM[:, 2, :, :]
        R2g = R2[:, :, :].rearrange("p a b -> p (a b)")
        QP = R2g[:, 0:4 * N].rearrange("p (i n) -> p i n", i=4)
        UV = R2g[:, 4 * N:4 * N + 2048].rearrange("p (a e) -> p a e", a=2)
        KN = XM[:, 1, :, :].rearrange("p k n -> p (k n)")[:, 0:H * T].rearrange("p (h t) -> p h t", h=H)
        VN = XM[:, 0, :, :].rearrange("p k n -> p (k n)")[:, 0:TT * D].rearrange("p (t e) -> p t e", t=TT)
        OG = QN
        cutB = cutter(arena, ARENA)
        shared = arena[:, 0:2 * N + 10 * ROPE + 4 * 384]
        cosT, sinT = cutB(N), cutB(N)
        cosN, sinN = cutB(5 * ROPE).rearrange("p (t e) -> p t e", t=5), cutB(5 * ROPE).rearrange("p (t e) -> p t e", t=5)
        kvn = cutB(5 * 384).rearrange("p (t e) -> p t e", t=5)
        ckvT = cutB(2 * N).rearrange("p (a n) -> p a n", a=2)
        kpeT = cutB(N)
        qa = cutB(QT * N).rearrange("p (a n) -> p a n", a=QT)
        kvg = cutB(KVL)
        qng = cutB(QT)
        st = cutB(N)
        kss = cutB(8)
        rtmp = cutB(N)
        qlat = cutB(2 * H * NS).rearrange("p (a h s) -> p a h s", a=2, h=H)
        A1 = cutB(KT * 9).rearrange("p (k n) -> p k n", k=KT)
        rt64 = cutB(ROPE)
        qpd = cutB(H * NS).rearrange("p (h s) -> p h s", h=H)
        olat = cutB(2 * H * NS).rearrange("p (a h s) -> p a h s", a=2, h=H)
        causal = cutB(P)
        mx, nmx, den = cutB(4), cutB(4), cutB(4)
        drow = shared[0:H, 0:PAST + 1]
        dval = shared[0:H, PAST + 4:PAST + 4 + KVL]
        dmx, dnm, dden, drc = (shared[0:H, PAST + 4 + KVL + i:PAST + 5 + KVL + i] for i in range(4))
        prT = cutB((NPAGES + 1) * H).rearrange("p (g h) -> p g h", g=NPAGES + 1)
        PN = rtmp[:, 0:T]
        PTb = st[:, 0:T].rearrange("p (b q) -> p b q", b=TT)
        ckr = kvg
        cutD = cutter(qa.rearrange("p a n -> p (a n)"), QT * N)
        dturn = cutD(6 * P).rearrange("p (q j) -> p q j", q=6)
        dq = cutD(6 * HD).rearrange("p (q j) -> p q j", q=6)
        sa = cutD(HD)
        yd = cutD(HD)
        wr, dot = cutD(HD), cutD(1)
        bst, bag, rsd = cutD(6), cutD(2), cutD(1)
        ydt = cutD(P)
        orow = shared[0:NS, 1680:1680 + 512]
        laterow = shared[0:9, 2192:2192 + 512]
        R1g = R1[:, :, :].rearrange("p a b -> p (a b)")
        CKg = [R1g[:, 0:4096], ring[:, 1, :], ring[:, 0, :]]
        CRg = [ring[:, 2, i * 1024:(i + 1) * 1024] for i in range(3)]
        CK = [x.rearrange("p (t c) -> p t c", t=NPAGES) for x in CKg]
        CR = [x.rearrange("p (t c) -> p t c", t=NPAGES) for x in CRg]
        qag = qa.rearrange("p a n -> p (a n)")
        KC = [x.rearrange("p (a k) -> p a k", a=2) for x in (ring[:, 2, 3072:4096], qag[:, 0:1024])]
        KR = [decbuf[:, :, :, :].rearrange("p a b c -> p (a b c)")[0:ROPE], qag[0:ROPE, 1024:1536]]
        WO = [ring[:, 0, :], R1g[:, 0:4096]]
        ptab = sb("ptab", [P, NS], I32)
        pidx = sb("pidx", [P, NS], I32)
        prow = sb("prow", [P, 1])

        s_const = sem("constants_loaded")
        s_mask = sem("masks_loaded")
        s_x = sem("x_loaded")
        s_ada = [sem("ada_group_loaded0"), sem("ada_group_loaded1")]
        s_adl = [sem("ada_group_between_pairs0"), sem("ada_group_between_pairs1")]
        s_a0 = sem("input_scale_ready")
        s_ha = sem("input_tiles_by_act")
        s_r2 = sem("shift_difference_ready")
        s_xmp = sem("mixed_input_by_pool")
        s_adr, s_adt = sem("ada_rows_stored"), sem("ada_rows_turned")
        s_ada_mm = sem("ada_products_done")
        s_ada_out = sem("ada_tiles_stored")
        s_sq = sem("squares_ready")
        s_ss = sem("square_sums_done")
        s_ms = sem("mean_squares_ready")
        s_rstd = sem("rstd_ready")
        s_xm = sem("mixed_input_ready")
        s_l1 = sem("lora1_loaded")
        s_hid = sem("lora_hidden_products")
        s_hida = sem("lora_hidden_by_act")
        s_hidr = sem("lora_hidden_ready")
        s_shout = sem("shift_rows_ready")
        s_store = sem("outputs_stored")
        s_dve, s_act, s_pool = sem("dve_steps"), sem("act_steps"), sem("pool_steps")
        s_pw = [sem("pair_weights_loaded0"), sem("pair_weights_loaded1")]
        s_pjm = sem("projection_slot_filled")
        s_ra = sem("projection_slot_read_by_act")
        s_rd = sem("projection_slot_read_by_dve")
        s_pa = sem("pair_factors_by_act")
        s_pd = sem("pair_factors_by_dve")
        s_pp = sem("pair_factors_by_pool")
        s_M = sem("chunk_products_done")
        s_Me = sem("chunk_products_masked")
        s_Z = sem("inverse_z_product")
        s_Ze = sem("inverse_z_stored")
        s_T = sem("inverse_t_product")
        s_Te = sem("inverse_t_stored")
        s_sc = sem("scan_products")
        s_sce = sem("scan_operand_stored")
        s_Se = sem("state_updated")
        s_gna = sem("group_norm_by_act")
        s_gnd = sem("group_norm_centered")
        s_gnp = sem("group_norm_sums")
        s_yT = sem("mixer_tile_ready")
        s_So = sem("state_transposed")
        s_Soa = sem("state_out_ready")
        s_Sst = sem("state_out_stored")
        s_zero = sem("padding_cleared")
        s_zp = sem("pair_vectors_ready")

        s_xr = sem("x_loaded_again")
        s_w = [sem(f"weights_loaded{i}") for i in range(3)]
        s_wu = sem("weights_used")
        s_adb = sem("later_ada_tiles_stored")
        s_dt = sem("decode_factors_turned")
        s_dta = sem("decode_factors_stored")
        s_dq = sem("decode_factors_moved")
        s_sd = sem("decode_state_loaded")
        s_dd = sem("decode_step_by_dve")
        s_dp = sem("decode_step_by_pool")
        s_dso = sem("decode_state_stored")
        s_dr = sem("decode_rstd_ready")
        s_ydm = sem("decode_y_moved")
        s_ydt = sem("decode_y_turned")
        s_r1 = sem("decode_mixer_tile_ready")
        s_om = sem("output_tile_product")
        s_ow = sem("output_rows_product")
        s_owa = sem("output_rows_stored")
        s_odt = sem("output_rows_turned")
        s_lr = sem("late_ada_rows_stored")
        s_lt = sem("late_ada_rows_turned")
        s_oa = sem("output_tile_stored")
        s_ns = sem("norm_sums_done")
        s_nd = sem("norm_mean_ready")
        s_na = sem("norm_rstd_ready")
        s_acc = sem("squares_added")
        s_nq = sem("norm_squares_ready")
        s_res = sem("residual_ready")
        s_hh = sem("inputs_of_layer1_by_dve")
        s_hha = sem("inputs_of_layer1_by_act")
        s_cb = sem("second_half_constants_loaded")
        s_kvm = sem("kv_tile_product")
        s_kva = sem("kv_square_sums")
        s_kvd = sem("kv_mean_ready")
        s_kvr = sem("kv_rstd_ready")
        s_kvn = sem("kv_tile_ready")
        s_kvt = sem("kv_tile_turned")
        s_kvs = sem("kv_tile_turned_stored")
        s_kvo = sem("kv_outputs_stored")
        s_bm = sem("layer1_projection_product")
        s_ba = sem("layer1_projection_by_act")
        s_bd = sem("layer1_projection_by_dve")
        s_qn = sem("q_latent_normed")
        s_uv = sem("uv_loaded")
        s_pidx = sem("page_rows_ready")
        s_pt = sem("page_table_loaded")
        s_ck = [sem(f"cache_loaded{i}") for i in range(3)]
        s_bw = [sem("b_w_out_loaded0"), sem("b_w_out_loaded1")]
        s_sm = sem("attention_scores_done")
        s_sd1 = sem("attention_row_max")
        s_sa1 = sem("attention_exp_done")
        s_sd2 = sem("attention_rows_scaled")
        s_pt1 = sem("attention_rows_turned")
        s_pa1 = sem("attention_rows_turned_stored")
        s_po = sem("attention_output_done")
        s_pog = sem("attention_output_gated")
        s_kt = sem("cache_tiles_turned")
        s_kta = sem("cache_tiles_turned_by_act")
        s_ktd = sem("cache_tiles_turned_by_dve")
        s_ds = sem("decode_scores_done")
        s_dse = sem("decode_scores_stored")
        s_dsd = sem("decode_row_max")
        s_dsa = sem("decode_exp_done")
        s_dpt = sem("decode_weights_turned")
        s_dpa = sem("decode_weights_stored")
        s_dv = sem("decode_values_done")
        s_dvs = sem("decode_values_scaled")
        s_dot = sem("decode_values_turned")
        s_dvd = sem("decode_latent_ready")
        s_qpd = sem("decode_q_rope_moved")
        s_ckr = sem("decode_new_row_moved")
        s_do = sem("decode_output_done")
        s_y = sem("result_stored")

        LATE = ADA_FIRST + ADA_PAIRS
        stream = [("ada", LATE), ("w_out", 0), ("w_out", 1), ("ada", LATE + 1), ("ada", LATE + 2), ("ada", LATE + 3),
                  ("b_w_in", 0), ("b_w_in", 1), ("b_w_in", 2), ("kv_w_a", 0), ("w_q", 0), ("w_q", 1), ("uk", 0)]
        SI = {key: n for n, key in enumerate(stream)}
        NADA = ADA_GROUPS - LATE
        SPL = 4
        NQ_O, NQ_R, NQ_A = 0, KT + 1, 2 * KT + 1
        NQ_O1 = NQ_A + QT
        B_Q, B_PE, B_K, B_V, B_L = 11, 19, 27, 35, 43

        def late_rows(i):
            return pj[0:9, 1, 0, :] if i == 0 else bk[0:9, 0, :]

        def rope_slot(u):
            return pjs[u % 2] if (u - 8) // 2 % 2 == 0 else bk[:, 2 * (u % 2):2 * (u % 2) + 2, 0:HALF]

        NSTEP = TT * H

        def scored(n):
            return 5 * (n // TT) + n % TT + 1

        def used(n):
            name, g = stream[n]
            if name == "ada":
                return s_wu, g - LATE + 1
            return {"w_out": (s_om, KT) if g else (s_ow, 1), "kv_w_a": (s_kvm, 5), "b_w_in": (s_bm, QT + 4 * g),
                    "w_q": (s_bm, B_K if g else B_PE), "uk": (s_bm, B_L + 1)}[name]

        block = ctx.enter_context(nc.Block())

        def counter(eng, own):
            count = {}

            def mark(ins, s=None):
                s = own if s is None else s
                count[id(s)] = count.get(id(s), 0) + 1
                ins.then_inc(s, 1)
                return s, count[id(s)]

            def then(ins, s=None):
                eng.wait_ge(*mark(ins, s))
            return then, mark

        def store_state(sp, m):
            sp.wait_ge(s_Soa, m + 1)
            for h in range(2):
                sp.dma_start(o["wkv_p"][2 * m + h], Sout[h * HD:(h + 1) * HD, h * HD:(h + 1) * HD]).then_inc(s_Sst, 16)

        @block.sync
        def _(sp):
            for name, dst in (("cT", cT[:, :, :]), ("ident", ident[:, :]), ("ones", ones[:, :]),
                              ("vecs", vecs[:, :, :]), ("adab", adab[:, :])):
                sp.dma_start(dst, d[name]).then_inc(s_const, 16)
            for g in range(ADA_FIRST):
                if g == 1:
                    sp.dma_start(R0[:, :, :], d["xT"]).then_inc(s_x, 16)
                if g >= 2:
                    sp.wait_ge(s_ada_mm, g - 1)
                sp.dma_start(ring[:, g % 2, :], d["ada"][g]).then_inc(s_ada[g % 2], 16)

            def pair_weights(m):
                sp.dma_start(ring[:, m % 2, :], d["w_in"][m]).then_inc(s_pw[m % 2], 16)
                sp.dma_start(lora2[:, m % 2, :], d["lora2"][m]).then_inc(s_pw[m % 2], 16)

            def ada_group(j):
                sp.dma_start(ring[:, j % 2, :], d["ada"][ADA_FIRST + j]).then_inc(s_adl[j % 2], 16)

            def load(n):
                name, g = stream[n]
                src = d[name][g]
                sp.dma_start(ring[:, n % 3, 0:src.shape[1]], src).then_inc(s_w[n % 3], 16)

            for m in range(2):
                sp.wait_ge(s_ada_mm, ADA_FIRST - 1 + m)
                pair_weights(m)
            for m in range(PAIRS):
                if m == PAIRS - 1:
                    load(0)
                sp.wait_ge(s_pjm, NUSE * m + U_G + 1)
                ada_group(m)
                if m == PAIRS - 1:
                    sp.dma_start(Sd, d["Sd"]).then_inc(s_sd, 16)
                sp.wait_ge(s_ada_mm, ADA_FIRST + m + 1)
                if m + 2 < PAIRS:
                    pair_weights(m + 2)
                if m == PAIRS - 1:
                    load(1)
                store_state(sp, m)
            sp.wait_ge(s_yT, PAIRS)
            sp.wait_ge(s_pp, 3 * PAIRS)
            sp.wait_ge(s_pa, 4 * PAIRS)
            sp.wait_ge(s_dq, 32)
            load(2)
            sp.dma_start(R0[:, :, :], d["xT"]).then_inc(s_xr, 16)
            for name, dst in (("cosT", cosT), ("sinT", sinT), ("cosN", cosN), ("sinN", sinN), ("kvg", kvg),
                              ("qng", qng), ("causal", causal)):
                sp.dma_start(dst, d[name]).then_inc(s_cb, 16)
            for n in range(3, len(stream)):
                sp.wait_ge(*used(n - 3))
                load(n)
                if n == 3:
                    sp.wait_ge(s_dd, 4)
                    sp.dma_start(o["wkv_s"], Sd).then_inc(s_dso, 16)
            sp.wait_ge(s_kvn, 5)
            for n in range(NS):
                if n >= 1:
                    sp.wait_ge(s_dv, n)
                sp.dma_start(ckr[0:1, :], kvn[n:n + 1, TT, 0:KVL]).then_inc(s_ckr, 16)
                if n >= NS - 2:
                    i = n - (NS - 2)
                    sp.dma_start(WO[i], d["b_w_out"][i]).then_inc(s_bw[i], 16)
            for k in range(0, KT, 2):
                sp.wait_ge(s_res, KT + k + 2)
                sp.dma_start(o["y"][:, k:k + 2, :], R0[:, k:k + 2, :]).then_inc(s_y, 16)
            sp.wait_ge(s_y, 16 * KT // 2)
            sp.wait_ge(s_Sst, 32 * PAIRS)
            sp.wait_ge(s_store, 16)
            sp.wait_ge(s_dso, 16)
            sp.wait_ge(s_kvo, 160)

        @block.scalar
        def _(act):
            then, mark = counter(act, s_act)
            A = nc.scalar.activation
            nc.scalar.preload_act_table_set("natural_log_exp_and_others")
            for name, dst in (("scanm", scanm), ("maskM", maskM), ("lowm", lowm), ("lv1", lv1), ("lvm", lvm),
                              ("id64", id64), ("bones", bones)):
                act.dma_start(dst, d[name]).then_inc(s_mask, 16)
            act.dma_start(lora1, d["lora1"]).then_inc(s_l1, 16)
            act.dma_start(shin, d["shiftT"]).then_inc(s_l1, 16)
            act.dma_start(ptab[:, :], d["page_table"]).then_inc(s_pt, 16)
            act.dma_start(prow[:, :], d["prow"]).then_inc(s_pt, 16)

            def first_ada_rows(g):
                act.wait_ge(s_ada_mm, g + 1)
                if g >= 2:
                    act.wait_ge(s_adt, g - 1)
                mark(A(arow[g % 2], bk[0:9, g % 2, :], ACT.Identity), s_adr)

            first_ada_rows(0)
            act.wait_ge(s_x, 16)
            mark(A(R2[:, :, :], R0[:, :, :], ACT.Square), s_sq)
            first_ada_rows(1)
            act.wait_ge(s_ms, 1)
            then(A(stat, stat, ACT.Ln))
            mark(A(stat, stat, ACT.Exp, scale=-0.5), s_rstd)
            first_ada_rows(2)
            first_ada_rows(3)
            act.wait_ge(s_a0, 1)
            for k in range(KT // 2, KT):
                last = A(R1[:, k, 0:T], R1[:, k, 0:T], ACT.Identity, scale=A0[:, k, 0:1], bias=mod[:, M_SH0 + k, 0:1])
                mark(last, s_ha)
            act.wait_ge(s_shout, 1)
            act.dma_start(o["shift"], shout).then_inc(s_store, 16)
            act.wait_ge(s_hid, 1)
            then(A(two(lhid)[0:LORA], pjs[0][0:LORA], ACT.Exp, scale=2.0))
            then(A(lhid[0:LORA], lhid[0:LORA], ACT.Ln, bias=1.0))
            mark(A(lhid[0:LORA], lhid[0:LORA], ACT.Exp, scale=-1.0), s_hida)
            act.wait_ge(s_hid, 2)
            mark(A(two(lhid)[LORA:P], pjs[1][LORA:P], ACT.Identity), s_hida)

            def prep(m, part):
                v = m % 2
                if part == "r":
                    act.wait_ge(s_pjm, NUSE * m + U_R + 1)
                    if m >= 1:
                        act.wait_ge(s_pd, 5 * m)
                        act.wait_ge(s_pp, 3 * m)
                    if m >= 2:
                        act.wait_ge(s_yT, m - 1)
                    mark(A(two(rT), pjs[0], ACT.Identity), s_ra)
                if part == "k":
                    act.wait_ge(s_pjm, NUSE * m + U_K + 1)
                    if m == 0:
                        act.wait_ge(s_xmp, 1)
                    mark(A(two(kT), pjs[1], ACT.Identity))
                    mark(A(two(sqk), pjs[1], ACT.Square, scale=vecs[:, V_KK, m:m + 1]), s_ra)
                if part == "v":
                    act.wait_ge(s_pjm, NUSE * m + U_V + 1)
                    mark(A(two(vT), pjs[0], ACT.Identity), s_ra)
                if part == "g":
                    act.wait_ge(s_pjm, NUSE * m + U_G + 1)
                    then(A(two(gT[v]), pjs[1], ACT.Exp, scale=-1.0))
                    then(A(gT[v], gT[v], ACT.Ln, bias=1.0))
                    mark(A(gT[v], gT[v], ACT.Exp, scale=-1.0), s_pa)
                if part == "wa":
                    act.wait_ge(s_pjm, NUSE * m + U_W + 1)
                    if m == 0:
                        act.wait_ge(s_zp, 3)
                    mark(A(two(sg), pjs[0], ACT.Exp, scale=-1.0, bias=nw0[:, m:m + 1]), s_ra)
                    act.wait_ge(s_pjm, NUSE * m + U_A + 1)
                    then(A(two(aT), pjs[1], ACT.Exp, scale=-1.0, bias=na0[:, m:m + 1]), s_ra)
                    then(A(wa, wa, ACT.Ln, bias=1.0))
                    mark(A(wa, wa, ACT.Exp, scale=-1.0), s_pa)
                if part == "kk":
                    act.wait_ge(s_rd, 3 * m + 1)
                    then(A(sqk, sqk, ACT.Ln))
                    mark(A(sqk, sqk, ACT.Exp, scale=-0.5), s_pa)
                if part == "cum":
                    act.wait_ge(s_pd, 5 * m + 1)
                    mark(A(ecum, cum, ACT.Exp, scale=-E05))
                    mark(A(einv, cum, ACT.Exp, scale=E05))
                    mark(A(cumx, cumx, ACT.Exp, scale=-E05), s_pa)
                if part == "tv":
                    act.wait_ge(s_pjm, NUSE * m + U_TV + 1)
                    act.wait_ge(s_zero, 1)
                    mark(A(Vx[v].rearrange("p c (h x) -> p c h x", x=HD)[:, :, 0:3:2, :],
                           pj[:, 0, 0, :].rearrange("p (c h x) -> p c h x", c=TT, h=2), ACT.Identity), s_ra)
                if part == "tb":
                    act.wait_ge(s_pjm, NUSE * m + U_TB + 1)
                    mark(A(BK[v].rearrange("p a c j -> p a (c j)"), pj[:, 1, :, :], ACT.Identity), s_ra)

            def scan(m, ch):
                pr = slice((ch % 2) * C, (ch % 2) * C + C)
                n = 4 * (NCH * m + ch)
                act.wait_ge(s_sc, n + 1)
                if ch == 0 and m >= 1:
                    act.wait_ge(s_Sst, 32 * m)
                mark(A(rhs[pr], bk[pr, 3, 0:P], ACT.Copy, scale=-1.0), s_sce)
                act.wait_ge(s_sc, n + 2)
                mark(A(SAx[pr].rearrange("p (h x) -> p h x", x=HD)[:, 0:3:2, :],
                       bk[pr, 0, 0:P].rearrange("p (h x) -> p h x", h=2), ACT.Identity), s_sce)

            def norm(m):
                act.wait_ge(s_sc, 4 * NCH * (m + 1))
                mark(A(yc, bk[:, 2, :], ACT.Identity), s_gna)
                act.wait_ge(s_ada_mm, ADA_FIRST + m + 1)
                mark(A(adarow, pj[0:9, 0, 1, :], ACT.Identity), s_adr)
                act.wait_ge(s_So, m + 1)
                mark(A(Sout, bk[:, 3, 0:P], ACT.Identity), s_Soa)
                act.wait_ge(s_gnd, m + 1)
                mark(A(ysq, yc, ACT.Square), s_gna)
                act.wait_ge(s_gnp, 2 * m + 2)
                then(A(ysq, bk[:, 1, :], ACT.Ln, scale=1.0 / HD, bias=GN_EPS))
                mark(A(ysq, ysq, ACT.Exp, scale=-0.5), s_gna)

            for part in ("r", "k", "wa", "v", "kk", "cum", "g", "tv", "tb"):
                prep(0, part)
            for m in range(PAIRS):
                more = m + 1 < PAIRS
                if more:
                    for part in ("r", "k", "wa", "v"):
                        prep(m + 1, part)
                for ch in range(NCH):
                    scan(m, ch)
                    if more and ch == 1:
                        prep(m + 1, "kk")
                    if more and ch == 2:
                        prep(m + 1, "cum")
                    if more and ch == 3:
                        prep(m + 1, "g")
                    if more and ch == 6:
                        prep(m + 1, "tv")
                norm(m)
                if more:
                    prep(m + 1, "tb")

            act.wait_ge(s_yT, PAIRS)
            act.wait_ge(s_pp, 3 * PAIRS)
            act.wait_ge(s_Sst, 32 * PAIRS)
            def ada_rows(i):
                act.wait_ge(s_wu, i + 1)
                mark(A(laterow, late_rows(i), ACT.Identity), s_lr)

            def ada_tiles(i):
                act.wait_ge(s_lt, i + 1)
                for t in range(ADA_MT):
                    n = ADA_MT * (LATE + i) + t
                    mark(A(mod[:, n, :], bk[:, 1, 9 * t:9 * t + 9], ACT.Identity, bias=adab[:, n:n + 1]), s_adb)

            act.wait_ge(s_dt, 1)
            mark(A(dturn[0:HD, 0:4, :], pj[0:HD, 0, 0, :].rearrange("p (q j) -> p q j", q=4), ACT.Identity))
            then(A(dturn[0:HD, 4:6, :], pj[0:HD, 0, 1, 0:256].rearrange("p (q j) -> p q j", q=2), ACT.Identity), s_dta)
            for hp in range(2):
                act.dma_start(dq[hp * HD:(hp + 1) * HD], dturn[0:HD, :, hp * HD:(hp + 1) * HD]).then_inc(s_dq, 16)

            def out_tile(layer, t):
                act.wait_ge(s_om, KT * layer + t + 1)
                if t < SPL:
                    ps, sq, y = pj[:, t % 2, 0, :], SQ[:, t, 0:T], Y[:, t, 0:T]
                else:
                    ps, sq, y = pjs[t % 2], two(SQ[:, t, :]), two(Y[:, t, :])
                mark(A(sq, ps, ACT.Square), s_nq)
                mark(A(y, ps, ACT.Identity), s_oa)

            def out_rows(layer):
                act.wait_ge(s_ow, layer + 1)
                mark(A(orow, bk[0:NS, 3, :], ACT.Identity), s_owa)

            def out_rows_turned(layer):
                act.wait_ge(s_odt, layer + 1)
                ps = bk[:, 3, 0:SPL * NS].rearrange("p (t s) -> p t s", t=SPL)
                mark(A(Y[:, 0:SPL, T:N], ps, ACT.Identity))
                mark(A(SQ[:, 0:SPL, T:N], ps, ACT.Square), s_nq)

            nn = [0]

            def rstd(x):
                nn[0] += 1
                act.wait_ge(s_nd, nn[0])
                then(A(x, x, ACT.Ln))
                mark(A(x, x, ACT.Exp, scale=-0.5), s_na)

            ada_rows(0)
            out_tile(0, 0)
            ada_tiles(0)
            for t in range(1, SPL - 1):
                out_tile(0, t)
            act.wait_ge(s_dd, 2)
            then(A(rsd, bag[:, 1:2], ACT.Ln, bias=GN_EPS))
            mark(A(rsd, rsd, ACT.Exp, scale=-0.5), s_dr)
            act.wait_ge(s_dd, 3)
            for hp in range(2):
                act.dma_start(ydt[0:HD, hp * HD:(hp + 1) * HD], yd[hp * HD:(hp + 1) * HD]).then_inc(s_ydm, 16)
            out_tile(0, SPL - 1)
            ada_rows(1)
            out_rows(0)
            out_tile(0, SPL)
            out_rows_turned(0)
            ada_tiles(1)
            for t in range(SPL + 1, KT):
                out_tile(0, t)
            rstd(st)
            ada_rows(2)
            for k in range(KT):
                act.wait_ge(s_res, k + 1)
                mark(A(SQ[:, k, :], R0[:, k, :], ACT.Square), s_nq)
            rstd(st)
            ada_tiles(2)
            act.wait_ge(s_hh, 1)
            act.wait_ge(s_dso, 16)
            for k in range(KT // 2, KT):
                mark(A(H1[:, k, 0:T], HN[:, k, 0:T], ACT.Identity, scale=A0[:, k, 0:1], bias=mod[:, M_SH1 + k, 0:1]), s_hha)
            ada_rows(3)
            ada_tiles(3)

            for t in range(QT + KT):
                act.wait_ge(s_bm, t + 1)
                if t < QT:
                    mark(A(two(SQ[:, t, :]), pjs[t % 2], ACT.Square), s_nq)
                    mark(A(two(qa[:, t, :]), pjs[t % 2], ACT.Identity), s_ba)
                else:
                    g = GATE[:, t - QT, :]
                    then(A(two(g), pjs[t % 2], ACT.Exp, scale=-1.0))
                    then(A(g, g, ACT.Ln, bias=1.0))
                    mark(A(g, g, ACT.Exp, scale=-1.0), s_ba)
                    if t == QT:
                        rstd(st)
                        act.dma_start(UV, d["uv"]).then_inc(s_uv, 16)
            for t in range(5):
                n = P if t < TT else NS
                act.wait_ge(s_kvm, t + 1)
                then(A(rtmp[0:n, 0:KVL], bk[0:n, t % 2, 0:KVL], ACT.Square, accum_out=kss[0:n, 0:1]), s_kva)
                act.wait_ge(s_kvd, t + 1)
                then(A(kss[0:n, 1:2], kss[0:n, 1:2], ACT.Ln))
                mark(A(kss[0:n, 1:2], kss[0:n, 1:2], ACT.Exp, scale=-0.5), s_kvr)
                act.wait_ge(s_kvt, t + 1)
                mark(A(ckvT[:, :, t * P:t * P + n], bk[:, 2, 0:2 * n].rearrange("p (a n) -> p a n", a=2), ACT.Identity))
                mark(A(kpeT[:, t * P:t * P + n], bk[:, 2, 2 * n:3 * n], ACT.Identity), s_kvs)
                act.wait_ge(s_kvn, t + 1)
                act.dma_start(o["ckv"][t * P:t * P + n, :], kvn[0:n, t, 0:KVL]).then_inc(s_kvo, 16)
                act.dma_start(o["kpe"][t * P:t * P + n, :], kvn[0:n, t, KVL:KVL + ROPE]).then_inc(s_kvo, 16)

            for t in range(H):
                act.wait_ge(s_bm, B_Q + t + 1)
                mark(A(two(QN[:, t, :]), pjs[(B_Q + t) % 2], ACT.Identity), s_ba)
            act.wait_ge(s_bd, KT + 4)
            for hp in range(2):
                act.dma_start(qpd[0:ROPE, hp:H:2, :], QP[hp * ROPE:(hp + 1) * ROPE, :, T:N]).then_inc(s_qpd, 16)
            base = B_K
            for t in range(H):
                act.wait_ge(s_bm, base + t + 1)
                mark(A(KN[:, t, :], pj[:, t % 2, 0, :], ACT.Identity), s_ba)
            for t in range(2 * TT):
                act.wait_ge(s_bm, base + H + t + 1)
                mark(A(VN[:, t // 2, (t % 2) * 512:(t % 2) * 512 + 512], bk[:, t % 2, :], ACT.Identity), s_ba)
            act.wait_ge(s_bm, base + H + 2 * TT + 1)
            mark(A(qlat, bk[:, 2, 0:2 * H * NS].rearrange("p (a h s) -> p a h s", a=2, h=H), ACT.Identity), s_ba)

            def row_exp(n):
                w = (n % TT + 1) * P
                act.wait_ge(s_sd1, n + 1)
                act.wait_ge(s_pt1, n)
                mark(A(PN[:, 0:w], bk[:, 0, 0:w], ACT.Exp, scale=SCALE, bias=nmx[:, 0:1], accum_out=den[:, 0:1]), s_sa1)

            def rows_turned(n):
                w = (n % TT + 1) * P
                act.wait_ge(s_pt1, n + 1)
                act.wait_ge(s_po, n)
                mark(A(PTb[:, 0:n % TT + 1, :], bk[:, 1, 0:w].rearrange("p (b q) -> p b q", q=P), ACT.Identity), s_pa1)

            def cache_turned(n):
                act.wait_ge(s_kt, n + 1)
                if n >= 2:
                    act.wait_ge(s_ds, scored(n - 2))
                mark(A(KC[n % 2], pj[:, 0, :, :], ACT.Identity), s_kta)

            def decode_exp(s):
                act.wait_ge(s_dsd, s + 1)
                mark(A(drow, drow, ACT.Exp, scale=SCALE, bias=dnm, accum_out=dden), s_dsa)

            def weights_turned(s):
                act.wait_ge(s_dpt, s + 1)
                act.wait_ge(s_dv, s)
                mark(A(prT[:, 0:NPAGES, :], bk[:, 3, 0:P].rearrange("p (g h) -> p g h", h=H), ACT.Identity))
                mark(A(prT[0:1, NPAGES, :], bk[0:1, 3, P:P + H], ACT.Identity), s_dpa)

            row_exp(0)
            for n in range(NSTEP):
                s, g = n // TT, n % TT
                cache_turned(n)
                rows_turned(n)
                if s >= 1 and g == 1:
                    decode_exp(s - 1)
                if n + 1 < NSTEP:
                    row_exp(n + 1)
                if s >= 1 and g == 2:
                    weights_turned(s - 1)
            decode_exp(NS - 1)
            out_tile(1, 0)
            weights_turned(NS - 1)
            for t in range(1, SPL):
                out_tile(1, t)
            out_rows(1)
            out_tile(1, SPL)
            out_rows_turned(1)
            for t in range(SPL + 1, KT):
                out_tile(1, t)
            rstd(st)

        @block.tensor
        def _(pe):
            mm, tr = nc.tensor.matmul, nc.tensor.transpose
            pe.wait_ge(s_const, 80)

            def first_ada_turn(g):
                pe.wait_ge(s_adr, g + 1)
                if g >= 2:
                    pe.wait_ge(s_ada_out, g - 1)
                for t in range(ADA_MT):
                    last = tr(bk[:, 2 + g % 2, 9 * t:9 * t + 9], arow[g % 2][:, t * P:(t + 1) * P], ident[0:9, 0:9])
                last.then_inc(s_adt, 1)

            for g in range(ADA_FIRST):
                pe.wait_ge(s_ada[g % 2], 16 * (g // 2 + 1))
                if g >= 2:
                    pe.wait_ge(s_adr, g - 1)
                w = ring[:, g % 2, :].rearrange("p (k e) -> p k e", k=KT)
                for k in range(KT):
                    last = mm(bk[0:9, g % 2, :], cT[:, k, :], w[:, k, :], start=(k == 0), stop=(k == KT - 1))
                last.then_inc(s_ada_mm, 1)
                if g >= 1:
                    first_ada_turn(g - 1)
                if g == 1:
                    pe.wait_ge(s_sq, 1)
                    for k in range(KT):
                        for a in range(2):
                            last = mm(pj[:, 0, a, 0:HALF], ones[:, :], R2[:, k, a * HALF:(a + 1) * HALF],
                                      start=(k == 0), stop=(k == KT - 1))
                    last.then_inc(s_ss, 1)
            first_ada_turn(ADA_FIRST - 1)
            pe.wait_ge(s_l1, 32)
            for e in range(2):
                pe.wait_ge(s_xm, e + 1)
                for k in range(KT):
                    for a in range(2):
                        last = mm(pj[e * LORA:(e + 1) * LORA, e, a, 0:HALF], lora1[:, k, e * LORA:(e + 1) * LORA],
                                  XM[:, e, k, a * HALF:(a + 1) * HALF], start=(k == 0), stop=(k == KT - 1))
                last.then_inc(s_hid, 1)

            def project(m, e, k0=0, k1=KT):
                s = e % 2
                if k0 == 0:
                    if m == 0:
                        if e == 3:
                            pe.wait_ge(s_xmp, 1)
                        else:
                            pe.wait_ge(s_xm, (4, 5, 3)[e])
                    if e == 0:
                        pe.wait_ge(s_pw[m % 2], 32 * (m // 2 + 1))
                        if m >= 2:
                            pe.wait_ge(s_ada_out, ADA_FIRST + m - 1)
                        if m >= 1:
                            pe.wait_ge(s_ra, 7 * m - 1)
                        else:
                            pe.wait_ge(s_hida, 2)
                    if e == 1 and m >= 1:
                        pe.wait_ge(s_ra, 7 * m)
                    if e == 2:
                        pe.wait_ge(s_ra, 7 * m + 3)
                    if e == 3:
                        pe.wait_ge(s_ra, 7 * m + 4)
                w = ring[:, m % 2, :].rearrange("p (e k c) -> p e k c", e=4, k=KT)
                for k in range(k0, k1):
                    for a in range(2):
                        last = mm(pj[:, s, a, 0:HALF], w[:, e, k, :], XM[:, e, k, a * HALF:(a + 1) * HALF],
                                  start=(k == 0), stop=(k == KT - 1))
                if k1 == KT:
                    last.then_inc(s_pjm, 1)

            def lora(m, e):
                if m == 0:
                    pe.wait_ge(s_hidr, 1)
                    pe.wait_ge(s_hida, 2)
                pe.wait_ge(s_ra, 7 * m + 1 + e)
                r = slice(e * LORA, (e + 1) * LORA)
                for a in range(2):
                    last = mm(pj[:, e, a, 0:HALF], lora2[r, m % 2, :], lhid[r, a * HALF:(a + 1) * HALF],
                              start=True, stop=True)
                last.then_inc(s_pjm, 1)

            def head_sums(m, which):
                if which == 0:
                    pe.wait_ge(s_ra, 7 * m + 5)
                else:
                    pe.wait_ge(s_pd, 5 * m + 3)
                    pe.wait_ge(s_rd, 3 * m + 2)
                x = sqk if which == 0 else tmb
                for a in range(2):
                    last = mm(pj[:, which, a, 0:HALF], bones, x[:, a * HALF:(a + 1) * HALF], start=True, stop=True)
                last.then_inc(s_pjm, 1)

            def turn_v(m):
                pe.wait_ge(s_rd, 3 * m + 1)
                for t in range(TT):
                    last = tr(pj[:, 0, 0, t * P:(t + 1) * P], vT[:, t * P:(t + 1) * P], ident[:, :])
                last.then_inc(s_pjm, 1)

            def turn_bk(m):
                pe.wait_ge(s_pd, 5 * m + 5)
                pe.wait_ge(s_rd, 3 * m + 3)
                for a, x in ((0, cum), (1, sqk)):
                    for t in range(TT):
                        last = tr(pj[:, 1, a, t * P:(t + 1) * P], x[:, t * P:(t + 1) * P], ident[:, :])
                last.then_inc(s_pjm, 1)

            def chunk_products(m, half):
                v = m % 2
                if half == 1:
                    pe.wait_ge(s_pd, 5 * m + 4)
                    if m >= 1:
                        pe.wait_ge(s_gna, 3 * m - 2)
                        pe.wait_ge(s_Soa, m)
                elif m >= 1:
                    pe.wait_ge(s_gna, 3 * m)
                for h in range(2):
                    r = slice(h * HD, (h + 1) * HD)
                    for u in range(4):
                        t, cp = 2 * half + u // 2, u % 2
                        ch = 2 * t + cp
                        for a, x in ((0, Bt), (1, Kt_)):
                            c0 = (u // 2) * 256 + a * P
                            last = mm(bk[cp * C:(cp + 1) * C, 2 * half + h, c0:c0 + P], x[r, ch * C:(ch + 1) * C],
                                      AR[v][r, ch, :, :].rearrange("p a t -> p (a t)"), start=True, stop=True)
                    last.then_inc(s_M, 1)

            def plain_products(m):
                v = m % 2
                pe.wait_ge(s_Me, 5 * m + 4)
                for h in range(2):
                    r = slice(h * HD, (h + 1) * HD)
                    for ch in range(NCH):
                        t, cp = ch // 2, ch % 2
                        last = mm(bk[cp * C:(cp + 1) * C, h, t * C:(t + 1) * C], AR[v][r, ch, 0, :],
                                  Bt[r, ch * C:(ch + 1) * C], start=True, stop=True)
                last.then_inc(s_M, 1)

            def blocks(out, lhsT, rhs_):
                for b in range(BLK):
                    for cp in range(2):
                        r = slice(cp * C, (cp + 1) * C)
                        last = mm(bk[r, out, b * C:(b + 1) * C], lhsT[r, b, :], rhs_[r, b, :], start=True, stop=True)
                return last

            def level_z(m, l):
                pe.wait_ge(s_Te, (NLEV + 1) * m + l + 1)
                blocks(0, Mab, Tt).then_inc(s_Z, 1)

            def level_t(m, l):
                pe.wait_ge(s_Ze, NLEV * m + l + 1)
                blocks(2, Tm, Zt).then_inc(s_T, 1)
                if l < NLEV - 1:
                    blocks(1, Zt, Tm).then_inc(s_T, 1)

            def ada_slice(m, k):
                if k == 0:
                    pe.wait_ge(s_adl[m % 2], 16 * (m // 2 + 1))
                    pe.wait_ge(s_rd, 3 * m + 4 if m + 1 < PAIRS else 3 * m + 3)
                    pe.wait_ge(s_ada_out, ADA_FIRST + m)
                w = ring[:, m % 2, :].rearrange("p (k e) -> p k e", k=KT)
                last = mm(pj[0:9, 0, 1, :], cT[:, k, :], w[:, k, :], start=(k == 0), stop=(k == KT - 1))
                if k == KT - 1:
                    last.then_inc(s_ada_mm, 1)

            def fill(m, ch, gap):
                if ch < 3 and m + 1 < PAIRS:
                    k = 2 + 2 * ch + gap
                    project(m + 1, 3, k, k + 1)
                k = 2 * (ch - 3) + gap if ch < 6 else ch
                if ch >= 3 and (ch < 6 or gap == 0):
                    ada_slice(m, k)

            def ada_turn(m):
                pe.wait_ge(s_adr, ADA_FIRST + m + 1)
                for t in range(ADA_MT):
                    last = tr(pj[:, 0, 1, 9 * t:9 * t + 9], adarow[:, t * P:(t + 1) * P], ident[0:9, 0:9])
                last.then_inc(s_adt, 1)

            def scan(m, ch):
                v = m % 2
                t, cp = ch // 2, ch % 2
                pr = slice(cp * C, (cp + 1) * C)
                n = NCH * m + ch
                both = lambda x: x.rearrange("p (h x) -> p h x", x=HD)[:, 0:3:2, :]
                pe.wait_ge(s_Se, n + m + 1)
                if ch == 0:
                    pe.wait_ge(s_Te, (NLEV + 1) * (m + 1))
                mm(bk[pr, 3, 0:P], AR[v][:, ch, 0, :], SS[ch % 2], start=True, stop=False)
                for h in range(2):
                    last = mm(bk[pr, 3, h * HD:(h + 1) * HD], MM[pr, h * TT + t, 2, :],
                              Vx[v][pr, t, h * P:h * P + HD], start=False, stop=(h == 1))
                last.then_inc(s_sc, 1)
                fill(m, ch, 0)
                pe.wait_ge(s_sce, 2 * n + 1)
                for h in range(2):
                    last = mm(bk[pr, 0, h * HD:(h + 1) * HD], Tt[pr, h * TT + t, :], rhs[pr, h * HD:(h + 1) * HD],
                              start=True, stop=True)
                last.then_inc(s_sc, 1)
                fill(m, ch, 1)
                pe.wait_ge(s_sce, 2 * n + 2)
                mm(bk[:, 1, 0:P], BK[v][pr, 0, t, :], both(SAx[pr]), start=True, stop=False)
                mm(bk[:, 1, 0:P], BK[v][pr, 1, t, :], both(Vx[v][pr, t, :]), start=False, stop=True).then_inc(s_sc, 1)
                y = bk[:, 2, ch * C:(ch + 1) * C]
                mm(y, SS[ch % 2], AR[v][:, ch, 1, :], start=True, stop=False)
                for h in range(2):
                    mm(y, SAx[pr, h * HD:h * HD + P], MM[pr, h * TT + t, 1, :], start=False, stop=False)
                    last = mm(y, Vx[v][pr, t, h * HD:h * HD + P], MM[pr, h * TT + t, 3, :],
                              start=False, stop=(h == 1))
                last.then_inc(s_sc, 1)

            def norm(m):
                pe.wait_ge(s_gna, 3 * m + 1)
                mm(bk[:, 0, :], bones, yc, start=True, stop=True).then_inc(s_gnp, 1)
                ada_turn(m)
                pe.wait_ge(s_Se, (NCH + 1) * (m + 1))
                tr(bk[:, 3, 0:P], SS[0], ident[:, :]).then_inc(s_So, 1)
                if m + 1 < PAIRS:
                    chunk_products(m + 1, 1)
                pe.wait_ge(s_gna, 3 * m + 2)
                mm(bk[:, 1, :], bones, ysq, start=True, stop=True).then_inc(s_gnp, 1)

            def arrived(n):
                pe.wait_ge(s_w[n % 3], 16 * (n // 3 + 1))

            def late_ada(i, k0, k1):
                n = SI[("ada", LATE + i)]
                if k0 == 0:
                    arrived(n)
                    if i == 0:
                        pe.wait_ge(s_ra, 7 * PAIRS)
                w = ring[:, n % 3, :].rearrange("p (k e) -> p k e", k=KT)
                for k in range(k0, k1):
                    last = mm(late_rows(i), cT[:, k, :], w[:, k, :], start=(k == 0), stop=(k == KT - 1))
                if k1 == KT:
                    last.then_inc(s_wu, 1)

            pe.wait_ge(s_mask, 112)
            project(0, 0)
            project(0, 1)
            lora(0, 0)
            lora(0, 1)
            project(0, 2)
            head_sums(0, 0)
            project(0, 3)
            turn_v(0)
            head_sums(0, 1)
            chunk_products(0, 1)
            turn_bk(0)
            for m in range(PAIRS):
                more = m + 1 < PAIRS
                chunk_products(m, 0)
                if more:
                    project(m + 1, 0, 0, KT // 2)
                plain_products(m)
                if more:
                    project(m + 1, 0, KT // 2, KT)
                for l in range(NLEV):
                    level_z(m, l)
                    if more:
                        if l == 0:
                            project(m + 1, 1, 0, KT // 2)
                        if l == 1:
                            project(m + 1, 1, KT // 2, KT)
                            lora(m + 1, 0)
                        if l == 2:
                            lora(m + 1, 1)
                            project(m + 1, 2, 0, KT // 2)
                        if l == 3:
                            project(m + 1, 2, KT // 2, KT)
                        if l == 4:
                            project(m + 1, 3, 0, 2)
                    elif l >= 1:
                        late_ada(0, 2 * (l - 1), 2 * l)
                    level_t(m, l)
                for ch in range(NCH):
                    scan(m, ch)
                    if more and ch == 0:
                        head_sums(m + 1, 0)
                    if more and ch == 4:
                        turn_v(m + 1)
                    if more and ch == 5:
                        head_sums(m + 1, 1)
                norm(m)
                if more:
                    turn_bk(m + 1)

            pe.wait_ge(s_yT, PAIRS)
            pe.wait_ge(s_Soa, PAIRS)
            pe.wait_ge(s_pp, 3 * PAIRS)
            for q in range(6):
                last = tr(pj[0:HD, 0, q // 4, (q % 4) * P:(q % 4 + 1) * P], decbuf[:, q, :, :].rearrange("p m s -> p (m s)"),
                          ident[:, :])
            last.then_inc(s_dt, 1)

            def ada(i):
                pe.wait_ge(s_lr, i)
                late_ada(i, 0, KT)

            def ada_turn(i):
                pe.wait_ge(s_lr, i + 1)
                pe.wait_ge(s_adb, ADA_MT * i)
                for t in range(ADA_MT):
                    last = tr(bk[:, 1, 9 * t:9 * t + 9], laterow[:, t * P:(t + 1) * P], ident[0:9, 0:9])
                last.then_inc(s_lt, 1)

            def prompt_sum(src, k, last):
                return mm(bk[:, 2, :], ones[:, :], src[:, k, 0:T], start=(k == 0), stop=last)

            def decode_sum(src, k, last):
                return mm(bk[:, 3, 0:NS], ones[:, :], src[:, k, T:N], start=(k == 0), stop=last)

            def out_weights(layer, g):
                if layer == 0:
                    n = SI[("w_out", g)]
                    arrived(n)
                    w = ring[:, n % 3, :]
                else:
                    w = WO[g]
                    pe.wait_ge(s_bw[g], 16)
                return w.rearrange("p (k e) -> p k e", k=KT)

            def out_tile(layer, t, src):
                w = out_weights(layer, t // 4)[:, :, (t % 4) * P:(t % 4 + 1) * P]
                if t >= 2:
                    pe.wait_ge(s_oa, KT * layer + t - 1)
                elif layer == 0 and t == 1:
                    pe.wait_ge(s_lr, 1)
                if t < SPL:
                    for k in range(KT):
                        last = mm(pj[:, t % 2, 0, :], w[:, k, :], src[:, k, 0:T], start=(k == 0), stop=(k == KT - 1))
                else:
                    for k in range(KT):
                        for a in range(2):
                            last = mm(pj[:, t % 2, a, 0:HALF], w[:, k, :], src[:, k, a * HALF:(a + 1) * HALF],
                                      start=(k == 0), stop=(k == KT - 1))
                last.then_inc(s_om, 1)

            def out_rows(layer, src):
                w = out_weights(layer, 0)
                for k in range(KT):
                    last = mm(bk[0:NS, 3, :], src[:, k, T:N], w[:, k, :], start=(k == 0), stop=(k == KT - 1))
                last.then_inc(s_ow, 1)

            def turn_out_rows(layer):
                pe.wait_ge(s_owa, layer + 1)
                for t in range(SPL):
                    last = tr(bk[:, 3, t * NS:(t + 1) * NS], orow[:, t * P:(t + 1) * P], ident[0:NS, 0:NS])
                last.then_inc(s_odt, 1)

            def finish_sums(layer):
                pe.wait_ge(s_nq, (NQ_O, NQ_O1)[layer] + KT + 1)
                for t in range(KT):
                    decode_sum(SQ, t, t == KT - 1)
                pe.wait_ge(s_acc, (KT - 1) * (layer + 1))
                last = mm(bk[:, 2, :], ones[:, :], SQ[:, 0, 0:T], start=True, stop=True)
                last.then_inc(s_ns, 1)

            pe.wait_ge(s_dta, 1)
            out_tile(0, 0, R1)
            ada_turn(0)
            for t in range(1, SPL):
                out_tile(0, t, R1)
            pe.wait_ge(s_ydm, 32)
            tr(pj[:, 1, 1, 0:HD], ydt[0:HD, :], ident[0:HD, 0:HD]).then_inc(s_ydt, 1)
            ada(1)
            pe.wait_ge(s_r1, 1)
            out_rows(0, R1)
            out_tile(0, SPL, R1)
            turn_out_rows(0)
            ada_turn(1)
            for t in range(SPL + 1, KT):
                out_tile(0, t, R1)
            finish_sums(0)
            ada(2)
            pe.wait_ge(s_nd, 1)
            for k in range(KT):
                pe.wait_ge(s_nq, NQ_R + k + 1)
                prompt_sum(SQ, k, k == KT - 1)
                last = decode_sum(SQ, k, k == KT - 1)
            last.then_inc(s_ns, 1)

            ada_turn(2)
            ada(3)
            ada_turn(3)

            pe.wait_ge(s_hh, 2)
            pe.wait_ge(s_hha, KT // 2)
            for t in range(QT + KT):
                g = 0 if t < QT else 1 + (t - QT) // 4
                n = SI[("b_w_in", g)]
                arrived(n)
                wid = 384 if g == 0 else 512
                e = t if g == 0 else (t - QT) % 4
                w = ring[:, n % 3, 0:KT * wid].rearrange("p (k e) -> p k e", k=KT)
                if 2 <= t < QT + 2:
                    pe.wait_ge(s_ba, t - 1)
                if t >= QT + 2:
                    pe.wait_ge(s_bd, t - 2 - QT + 1)
                for k in range(KT):
                    for a in range(2):
                        last = mm(pj[:, t % 2, a, 0:HALF], w[:, k, e * P:(e + 1) * P], H1[:, k, a * HALF:(a + 1) * HALF],
                                  start=(k == 0), stop=(k == KT - 1))
                last.then_inc(s_bm, 1)
                if t == QT:
                    pe.wait_ge(s_nq, NQ_O1)
                    for k in range(QT):
                        prompt_sum(SQ, k, k == QT - 1)
                        last = decode_sum(SQ, k, k == QT - 1)
                    last.then_inc(s_ns, 1)
            n = SI[("kv_w_a", 0)]
            arrived(n)
            kw = ring[:, n % 3, 0:KT * 384].rearrange("p (k e) -> p k e", k=KT)
            pe.wait_ge(s_hh, 3)

            def kv_turn(t):
                c = P if t < TT else NS
                pe.wait_ge(s_kvn, t + 1)
                pe.wait_ge(s_kvs, t)
                pe.wait_ge(s_nd, 3)
                for a in range(3):
                    last = tr(bk[:, 2, a * c:(a + 1) * c], kvn[0:c, t, a * P:(a + 1) * P], ident[0:c, 0:c])
                last.then_inc(s_kvt, 1)

            for t in range(5):
                c = P if t < TT else NS
                if t >= 2:
                    pe.wait_ge(s_kvn, t - 1)
                for k in range(KT):
                    last = mm(bk[0:c, t % 2, 0:384], HK[:, k, t * P:t * P + c], kw[:, k, :],
                              start=(k == 0), stop=(k == KT - 1))
                last.then_inc(s_kvm, 1)
                if t >= 1:
                    kv_turn(t - 1)
            kv_turn(TT)

            pe.wait_ge(s_qn, 1)
            for u in range(16):
                n = SI[("w_q", u // 8)]
                arrived(n)
                w = ring[:, n % 3, 0:QT * D].rearrange("p (k e) -> p k e", k=QT)
                out = pjs[(B_Q + u) % 2] if u < 8 else rope_slot(u)
                if u < 2:
                    pe.wait_ge(s_bd, KT - 1 + u)
                elif u < 8:
                    pe.wait_ge(s_ba, B_Q + u - 1)
                elif u < 12:
                    pe.wait_ge(s_ba, B_PE)
                    pe.wait_ge(s_kvn, 5)
                    pe.wait_ge(s_kvs, 5)
                else:
                    pe.wait_ge(s_bd, KT + (u - 8) // 2 - 1)
                e = u if u < 8 else (u - 8) // 2 + 4 * (u % 2)
                for k in range(QT):
                    for a in range(2):
                        last = mm(out[:, a, :], w[:, k, e * P:(e + 1) * P], qa[:, k, a * HALF:(a + 1) * HALF],
                                  start=(k == 0), stop=(k == QT - 1))
                last.then_inc(s_bm, 1)
            n = SI[("uk", 0)]
            arrived(n)
            uk = ring[:, n % 3, 0:2048].rearrange("p (a e) -> p a e", a=2)
            ukT = ring[:, n % 3, 2048:4096].rearrange("p (h c) -> p h c", h=H)
            pe.wait_ge(s_bd, KT + 3)
            for h in range(H):
                if h >= 2:
                    pe.wait_ge(s_ba, B_PE + h - 1)
                for a in range(2):
                    last = mm(pj[:, h % 2, 0, :], uk[:, a, h * P:(h + 1) * P], ckvT[:, a, 0:T], start=(a == 0), stop=(a == 1))
                last.then_inc(s_bm, 1)
            pe.wait_ge(s_uv, 16)
            pe.wait_ge(s_bd, KT + 4)
            for t in range(2 * TT):
                if t >= 2:
                    pe.wait_ge(s_ba, B_PE + H + t - 1)
                for a in range(2):
                    last = mm(bk[:, t % 2, :], ckvT[:, a, (t // 2) * P:(t // 2 + 1) * P],
                              UV[:, a, (t % 2) * 512:(t % 2) * 512 + 512], start=(a == 0), stop=(a == 1))
                last.then_inc(s_bm, 1)
            pe.wait_ge(s_nd, 3)
            for a in range(2):
                for h in range(H):
                    c0 = (a * H + h) * NS
                    last = mm(bk[:, 2, c0:c0 + NS], ukT[:, h, a * P:(a + 1) * P], QN[:, h, T:N], start=True, stop=True)
            last.then_inc(s_bm, 1)

            def scores(n):
                h, q = n // TT, n % TT
                r = slice((h % 2) * ROPE, (h % 2 + 1) * ROPE)
                w = (q + 1) * P
                qs = slice(q * P, (q + 1) * P)
                pe.wait_ge(s_sa1, n)
                mm(bk[:, 0, 0:w], QN[:, h, qs], KN[:, h, 0:w], start=True, stop=False)
                mm(bk[:, 0, 0:w], QP[r, h // 2, qs], kpeT[r, 0:w], start=False, stop=True).then_inc(s_sm, 1)

            def turn_rows(n):
                pe.wait_ge(s_sd2, n + 1)
                pe.wait_ge(s_pa1, n)
                for b in range(n % TT + 1):
                    last = tr(bk[:, 1, b * P:(b + 1) * P], PN[:, b * P:(b + 1) * P], ident[:, :])
                last.then_inc(s_pt1, 1)

            def row_values(n):
                h, q = n // TT, n % TT
                pe.wait_ge(s_pa1, n + 1)
                if q == 0:
                    pe.wait_ge(s_pog, h)
                for b in range(q + 1):
                    last = mm(bk[:, 2, q * P:(q + 1) * P], VN[:, b, h * P:(h + 1) * P], PTb[:, b, :], start=(b == 0), stop=(b == q))
                last.then_inc(s_po, 1)

            def turn_cache(n):
                s, g = n // TT, n % TT
                v = s % 3
                if g == 0:
                    pe.wait_ge(s_ck[v], 32 * (s // 3 + 1))
                pe.wait_ge(s_kta, n)
                pe.wait_ge(s_ktd, n)
                for k in range(4):
                    ks = slice(k * P, (k + 1) * P)
                    for a in range(2):
                        tr(pj[:, 0, a, ks], CK[v][:, 4 * g + k, a * P:(a + 1) * P], ident[:, :])
                    last = tr(pj[0:ROPE, 1, 0, ks], CR[v][:, 4 * g + k, :], ident[:, :])
                last.then_inc(s_kt, 1)

            def cache_scores(n):
                s, g = n // TT, n % TT
                pe.wait_ge(s_kta, n + 1)
                pe.wait_ge(s_ktd, n + 1)
                pe.wait_ge(s_dse, n)
                out = pj[0:H, 1, 1, :]
                mm(out, qlat[:, 0, :, s], KC[n % 2][:, 0, :], start=True, stop=False)
                mm(out, qlat[:, 1, :, s], KC[n % 2][:, 1, :], start=False, stop=False)
                mm(out, qpd[0:ROPE, :, s], KR[n % 2], start=False, stop=True).then_inc(s_ds, 1)
                if g == TT - 1:
                    out = bk[0:H, 3, 0:1]
                    me = slice(T + s, T + s + 1)
                    pe.wait_ge(s_dvs, s)
                    mm(out, qlat[:, 0, :, s], ckvT[:, 0, me], start=True, stop=False)
                    mm(out, qlat[:, 1, :, s], ckvT[:, 1, me], start=False, stop=False)
                    mm(out, qpd[0:ROPE, :, s], kpeT[0:ROPE, me], start=False, stop=True).then_inc(s_ds, 1)

            def turn_weights(s):
                pe.wait_ge(s_dsa, s + 1)
                pe.wait_ge(s_dvd, s)
                for g in range(NPAGES):
                    tr(bk[:, 3, g * H:(g + 1) * H], drow[:, g * P:(g + 1) * P], ident[0:H, 0:H])
                tr(bk[0:1, 3, P:P + H], drow[:, PAST:PAST + 1], ident[0:H, 0:H]).then_inc(s_dpt, 1)

            def decode_values(s):
                v = s % 3
                pe.wait_ge(s_dpa, s + 1)
                pe.wait_ge(s_ckr, 16 * (s + 1))
                out = bk[0:H, 3, 0:KVL]
                for g in range(NPAGES):
                    mm(out, prT[:, g, :], CK[v][:, g, :], start=(g == 0), stop=False)
                mm(out, prT[0:1, NPAGES, :], ckr[0:1, :], start=False, stop=True).then_inc(s_dv, 1)

            def turn_values(s):
                pe.wait_ge(s_dvs, s + 1)
                if s + 1 < NS:
                    pe.wait_ge(s_dsd, s + 2)
                for a in range(2):
                    last = tr(bk[:, 3, a * H:(a + 1) * H], dval[:, a * P:(a + 1) * P], ident[0:H, 0:H])
                last.then_inc(s_dot, 1)

            pe.wait_ge(s_ba, B_L + 1 - 8)
            pe.wait_ge(s_qpd, 32)
            scores(0)
            for n in range(NSTEP):
                s, g = n // TT, n % TT
                turn_cache(n)
                turn_rows(n)
                if n + 1 < NSTEP:
                    scores(n + 1)
                if s >= 1 and g == 2:
                    turn_weights(s - 1)
                    row_values(n)
                if n >= 1:
                    cache_scores(n - 1)
                if s >= 2 and g == 1:
                    turn_values(s - 2)
                if s >= 1 and g == 3:
                    decode_values(s - 1)
                if s == 0 or g != 2:
                    row_values(n)
            cache_scores(NSTEP - 1)
            pe.wait_ge(s_pog, H)
            out_tile(1, 0, OG)
            turn_values(NS - 2)
            turn_weights(NS - 1)
            out_tile(1, 1, OG)
            decode_values(NS - 1)
            out_tile(1, 2, OG)
            turn_values(NS - 1)
            out_tile(1, 3, OG)
            pe.wait_ge(s_dvd, NS)
            for h in range(H):
                for a in range(2):
                    last = mm(bk[:, 3, P + h * NS:P + (h + 1) * NS], UV[:, a, h * P:(h + 1) * P], olat[:, a, h, :],
                              start=(a == 0), stop=(a == 1))
            last.then_inc(s_do, 1)
            pe.wait_ge(s_pog, H + 1)
            out_rows(1, OG)
            out_tile(1, SPL, OG)
            turn_out_rows(1)
            for t in range(SPL + 1, KT):
                out_tile(1, t, OG)
            finish_sums(1)

        @block.gpsimd
        def _(pool):
            then, mark = counter(pool, s_pool)
            G = nc.gpsimd
            pool.wait_ge(s_const, 80)
            then(G.tensor_scalar(nw0, vecs[:, V_W0, :], -1.0, None, ALU.mult), s_zp)
            then(G.tensor_scalar(na0, vecs[:, V_A0, :], -1.0, None, ALU.mult), s_zp)
            then(G.tensor_scalar(omka, vecs[:, V_KA, :], -1.0, 1.0, ALU.mult, ALU.add), s_zp)
            then(G.memset(SAx[:, HD:2 * HD], 0.0), s_zero)
            then(G.memset(Vx[0][:, :, HD:2 * HD], 0.0), s_zero)
            then(G.memset(Vx[1][:, :, HD:2 * HD], 0.0), s_zero)
            pool.wait_ge(s_r2, 1)
            for k in range(KT):
                then(G.tensor_scalar(XM[:, 3, k, :], R2[:, k, :], vecs[:, V_MU + 3, k:k + 1], None, ALU.mult))
                last = G.tensor_tensor(XM[:, 3, k, :], XM[:, 3, k, :], R1[:, k, :], ALU.add)
                if k < KT - 1:
                    mark(last)
            then(last, s_xmp)
            for m in range(PAIRS):
                v = m % 2
                col = lambda n: vecs[:, n, m:m + 1]
                pool.wait_ge(s_pa, 4 * m + 1)
                if m >= 1:
                    pool.wait_ge(s_pd, 5 * m)
                    pool.wait_ge(s_rd, 3 * m)
                then(G.tensor_scalar(kmT, aT, col(V_KA), omka[:, m:m + 1], ALU.mult, ALU.add))
                pool.wait_ge(s_ra, 7 * m + 2)
                then(G.tensor_tensor(kmT, kmT, kT, ALU.mult), s_pp)
                pool.wait_ge(s_pd, 5 * m + 2)
                then(G.tensor_tensor(bT, kkT, aT, ALU.mult), s_pp)
                pool.wait_ge(s_pa, 4 * m + 4)
                pool.wait_ge(s_rd, 3 * m + 3)
                for q, x in enumerate((rT, kmT, vT, kkT, bT, ecum, bon[v], gT[v])):
                    last = G.tensor_copy(decbuf[:, q, m, :], x[:, T:N])
                    if q < 7:
                        mark(last)
                then(last, s_pp)
            bi = lambda q: dq[:, q, :].unsqueeze(1).to_broadcast([P, HD, HD])
            bj = lambda x: x.unsqueeze(2).to_broadcast([P, HD, HD])
            pool.wait_ge(s_dq, 32)
            mark(G.tensor_tensor(Wd2, bj(dq[:, 2, :]), bi(1), ALU.mult), s_dp)
            pool.wait_ge(s_dd, 1)
            mark(G.tensor_tensor(Sd, Sd, bi(5), ALU.mult), s_dp)
            def add_squares(layer):
                for t in range(1, KT):
                    pool.wait_ge(s_nq, (NQ_O, NQ_O1)[layer] + t + 1 + (t > SPL))
                    then(G.tensor_tensor(SQ[:, 0, 0:T], SQ[:, 0, 0:T], SQ[:, t, 0:T], ALU.add), s_acc)

            add_squares(0)
            pool.wait_ge(s_pidx, 1)

            def rows_of(s_):
                return bass.IndirectOffsetOnAxis(ap=pidx[:, s_:s_ + 1], axis=0)

            def gather_latents(s_):
                G.indirect_dma_start(CKg[s_ % 3], None, d["cache_c"], rows_of(s_)).then_inc(s_ck[s_ % 3], 16)

            def gather_keys(s_):
                G.indirect_dma_start(CRg[s_ % 3], None, d["cache_r"], rows_of(s_)).then_inc(s_ck[s_ % 3], 16)

            pool.wait_ge(s_om, KT)
            gather_latents(0)
            pool.wait_ge(s_bm, B_PE)
            gather_latents(1)
            pool.wait_ge(s_bm, B_K)
            for s_ in range(3):
                gather_keys(s_)
            pool.wait_ge(s_bm, B_L + 1)
            gather_latents(2)
            for s_ in range(3, NS):
                pool.wait_ge(s_dv, s_ - 2)
                gather_latents(s_)
                gather_keys(s_)
            add_squares(1)

        @block.vector
        def _(dve):
            then, mark = counter(dve, s_dve)
            V = nc.vector
            dve.wait_ge(s_const, 80)

            def ada(g):
                dve.wait_ge(s_adt, g + 1)
                mark(V.tensor_tensor(mod[:, ADA_MT * g:ADA_MT * (g + 1), :],
                                     bk[:, 2 + g % 2, 0:36].rearrange("p (t n) -> p t n", n=9),
                                     adab[:, ADA_MT * g:ADA_MT * (g + 1)].unsqueeze(2).to_broadcast([P, ADA_MT, 9]),
                                     ALU.add), s_ada_out)
            ada(0)
            dve.wait_ge(s_ss, 1)
            then(V.tensor_scalar(two(stat), pjs[0], 1.0 / D, EPS, ALU.mult, ALU.add), s_ms)
            dve.wait_ge(s_rstd, 1)
            dve.wait_ge(s_x, 16)
            then(V.tensor_tensor(R1[:, :, :], R0[:, :, :], stat.unsqueeze(1).to_broadcast([P, KT, N]), ALU.mult))
            for g in range(1, ADA_FIRST):
                ada(g)
            dve.wait_ge(s_ada_out, ADA_FIRST)
            then(V.tensor_scalar(A0[:, :, :], mod[:, M_SC0:M_SC0 + KT, :], 1.0, None, ALU.add))
            then(V.tensor_tensor(A0[:, :, :], A0[:, :, :],
                                 vecs[:, V_PRE0, :].unsqueeze(2).to_broadcast([P, KT, 9]), ALU.mult), s_a0)
            for k in range(KT // 2):
                mark(V.tensor_scalar(R1[:, k, 0:T], R1[:, k, 0:T], A0[:, k, 0:1], mod[:, M_SH0 + k, 0:1],
                                     ALU.mult, ALU.add))
            then(V.tensor_tensor(R1[:, :, T:N], R1[:, :, T:N], A0[:, :, 1:9], ALU.mult))
            then(V.tensor_tensor(R1[:, :, T:N], R1[:, :, T:N], mod[:, M_SH0:M_SH0 + KT, 1:9], ALU.add))
            dve.wait_ge(s_ha, KT // 2)
            mark(V.tensor_tensor(R2[:, :, 1:T], R1[:, :, 0:T - 1], R1[:, :, 1:T], ALU.subtract))
            mark(V.tensor_scalar(R2[:, :, 0:1], R1[:, :, 0:1], -1.0, None, ALU.mult))
            dve.wait_ge(s_l1, 32)
            then(V.tensor_tensor(R2[:, :, T:N], shin, R1[:, :, T:N], ALU.subtract), s_r2)
            then(V.tensor_copy(shout, R1[:, :, T - 1:N]), s_shout)
            for n, (e, dst) in enumerate(((4, 0), (5, 1), (2, 2), (0, 0), (1, 1))):
                if n >= 3:
                    dve.wait_ge(s_hid, n - 2)
                for k in range(KT):
                    last = V.scalar_tensor_tensor(XM[:, dst, k, :], R2[:, k, :], vecs[:, V_MU + e, k:k + 1],
                                                  R1[:, k, :], ALU.mult, ALU.add)
                    if k < KT - 1:
                        mark(last)
                then(last, s_xm)
            dve.wait_ge(s_hida, 1)
            then(V.tensor_scalar(lhid[0:LORA], lhid[0:LORA], -2.0, 1.0, ALU.mult, ALU.add), s_hidr)

            def chunk(x):
                return x[:, 0:T].rearrange("p (c t) -> p c t", c=NCH)

            def prep(m, part):
                v = m % 2
                col = lambda n: vecs[:, n, m:m + 1]
                if part == "g":
                    dve.wait_ge(s_pa, 4 * m + 4)
                    if m >= 1:
                        dve.wait_ge(s_pp, 3 * m)
                        dve.wait_ge(s_pjm, NUSE * m)
                    then(V.tensor_tensor(two(gT[v]), pjs[1], two(gT[v]), ALU.mult), s_rd)
                if part == "cum":
                    dve.wait_ge(s_pa, 4 * m + 1)
                    dve.wait_ge(s_mask, 112)
                    then(V.tensor_tensor_scan(cum, scanm, sg, 0.0, ALU.mult, ALU.add))
                    then(V.tensor_tensor(cumx, cum, sg, ALU.subtract), s_pd)
                if part == "ss":
                    dve.wait_ge(s_pjm, NUSE * m + U_SS + 1)
                    then(V.tensor_scalar(two(sqk), pjs[0], 1e-24, None, ALU.max), s_rd)
                if part == "kk":
                    dve.wait_ge(s_pa, 4 * m + 2)
                    then(V.scalar_tensor_tensor(kkT, kT, col(V_KK), sqk, ALU.mult, ALU.mult), s_pd)
                if part == "rk":
                    dve.wait_ge(s_pp, 3 * m + 1)
                    then(V.scalar_tensor_tensor(tmb, rT, col(V_RK), kmT, ALU.mult, ALU.mult), s_pd)
                if part == "bon":
                    dve.wait_ge(s_pjm, NUSE * m + U_BO + 1)
                    then(V.tensor_tensor(two(bon[v]), pjs[1], two(vT), ALU.mult), s_rd)
                if part == "ar":
                    dve.wait_ge(s_pa, 4 * m + 3)
                    then(V.tensor_tensor(AR[v][:, :, 0, :], chunk(kkT), chunk(cumx), ALU.mult))
                    then(V.tensor_tensor(AR[v][:, :, 1, :], chunk(rT), chunk(ecum), ALU.mult))
                    then(V.tensor_copy(pc[:, v, :], ecum[:, C - 1:T:C]))
                if part == "bt":
                    dve.wait_ge(s_pp, 3 * m + 2)
                    then(V.tensor_tensor(Bt, bT[:, 0:T], einv[:, 0:T], ALU.mult))
                    then(V.tensor_tensor(Kt_, kmT[:, 0:T], einv[:, 0:T], ALU.mult), s_pd)
                if part == "bh":
                    pcb = pc[:, v, :].unsqueeze(2).to_broadcast([P, NCH, C])
                    then(V.tensor_tensor(chunk(cum), chunk(Bt), pcb, ALU.mult))
                    then(V.tensor_tensor(chunk(sqk), chunk(Kt_), pcb, ALU.mult), s_pd)

            def masks(m, half):
                if m == 0:
                    dve.wait_ge(s_store, 16)
                for h in range(2):
                    n = 2 * half + h
                    dve.wait_ge(s_M, 5 * m + 2 * (1 - half) + h + 1)
                    b0 = h * TT + 2 * half
                    then(V.tensor_tensor(MM[:, b0:b0 + 2, :, :].rearrange("p b q t -> p b (q t)"),
                                         bk[:, n, :].rearrange("p (b x) -> p b x", b=2),
                                         maskM.unsqueeze(1).to_broadcast([P, 2, 256]), ALU.mult), s_Me)

            def level_one(m):
                dve.wait_ge(s_M, 5 * m + 5)
                then(V.tensor_tensor(Mab.rearrange("p (h b) t -> p h b t", h=2),
                                     bk[:, 0:2, 0:256].rearrange("p h (b t) -> p h b t", b=TT),
                                     lowm.unsqueeze(1).unsqueeze(1).to_broadcast([P, 2, TT, C]), ALU.mult), s_Me)
                idb = id64.unsqueeze(1).to_broadcast([P, BLK, C])
                for x, dst, a in ((MM[:, :, 0, :], Tt, 1), (Mab, Tm, 0)):
                    then(V.scalar_tensor_tensor(dst, x, -1.0, lv1[:, a, :].unsqueeze(1).to_broadcast([P, BLK, C]),
                                                ALU.mult, ALU.mult))
                    then(V.tensor_tensor(dst, dst, idb, ALU.add), s_Te if a else None)

            def level_z(m, l):
                dve.wait_ge(s_Z, NLEV * m + l + 1)
                then(V.tensor_tensor(Zt, bk[:, 0, :].rearrange("p (b t) -> p b t", b=BLK),
                                     lvm[:, l, :].unsqueeze(1).to_broadcast([P, BLK, C]), ALU.mult), s_Ze)

            def level_t(m, l):
                n = (2 * NLEV - 1) * m + 2 * l
                dve.wait_ge(s_T, n + 1)
                mark(V.tensor_tensor(Tt, Tt, bk[:, 2, :].rearrange("p (b t) -> p b t", b=BLK), ALU.subtract), s_Te)
                if l < NLEV - 1:
                    dve.wait_ge(s_T, n + 2)
                    mark(V.tensor_tensor(Tm, Tm, bk[:, 1, :].rearrange("p (b t) -> p b t", b=BLK), ALU.subtract))

            def scan(m, ch):
                v = m % 2
                n = 4 * (NCH * m + ch)
                dve.wait_ge(s_sc, n + 3)
                for h in range(2):
                    r = slice(h * HD, (h + 1) * HD)
                    last = V.scalar_tensor_tensor(SS[(ch + 1) % 2][r, r], SS[ch % 2][r, r], pc[r, v, ch:ch + 1],
                                                  bk[r, 1, r], ALU.mult, ALU.add)
                    if h == 0:
                        mark(last)
                then(last, s_Se)

            def ada_between(j):
                g = ADA_FIRST + j
                dve.wait_ge(s_adt, ADA_FIRST + j + 1)
                mark(V.tensor_tensor(mod[:, ADA_MT * g:ADA_MT * (g + 1), :],
                                     pj[:, 0, 1, 0:36].rearrange("p (t n) -> p t n", n=9),
                                     adab[:, ADA_MT * g:ADA_MT * (g + 1)].unsqueeze(2).to_broadcast([P, ADA_MT, 9]),
                                     ALU.add), s_ada_out)

            def norm(m):
                v = m % 2
                dve.wait_ge(s_gnp, 2 * m + 1)
                then(V.scalar_tensor_tensor(yc, bk[:, 0, :], -1.0 / HD, yc, ALU.mult, ALU.add), s_gnd)
                if m + 1 < PAIRS:
                    prep(m + 1, "bh")
                ada_between(m)
                if m + 1 < PAIRS:
                    masks(m + 1, 1)
                dve.wait_ge(s_gna, 3 * m + 3)
                then(V.tensor_tensor(yc, yc, ysq, ALU.mult))
                then(V.tensor_scalar(yc, yc, vecs[:, V_GNW, m:m + 1], vecs[:, V_GNB, m:m + 1], ALU.mult, ALU.add))
                then(V.tensor_tensor(yc, yc, bon[v][:, 0:T], ALU.add))
                then(V.tensor_tensor(R1[:, m, 0:T], yc, gT[v][:, 0:T], ALU.mult), s_yT)

            then(V.memset(SS[1], 0.0))
            for part in ("cum", "ss", "kk", "rk", "g", "ar", "bon", "bt", "bh"):
                prep(0, part)
            for m in range(PAIRS):
                more = m + 1 < PAIRS
                if m >= 1:
                    dve.wait_ge(s_So, m)
                then(V.memset(SS[0], 0.0), s_Se)
                if m == 0:
                    masks(0, 1)
                masks(m, 0)
                level_one(m)
                for l in range(NLEV):
                    level_z(m, l)
                    level_t(m, l)
                if more:
                    prep(m + 1, "cum")
                for ch in range(NCH):
                    scan(m, ch)
                    if more and ch >= 1:
                        prep(m + 1, (None, "ss", "kk", "rk", "g", "ar", "bon", "bt")[ch])
                norm(m)

            bi = lambda q: dq[:, q, :].unsqueeze(1).to_broadcast([P, HD, HD])
            bj = lambda x: x.unsqueeze(2).to_broadcast([P, HD, HD])
            dve.wait_ge(s_pt, 32)
            then(V.tensor_scalar(pidx[:, :], ptab[:, :], 8.0, prow[:, 0:1], ALU.mult, ALU.add), s_pidx)
            dve.wait_ge(s_dq, 32)
            dve.wait_ge(s_sd, 16)
            then(V.tensor_tensor(wr, dq[:, 0, :], dq[:, 5, :], ALU.mult))
            then(V.tensor_tensor(Wd1, Sd, bi(3), ALU.mult))
            then(V.tensor_reduce(sa, Wd1, AX_X, ALU.add))
            then(V.tensor_tensor(Wd1, Sd, wr.unsqueeze(1).to_broadcast([P, HD, HD]), ALU.mult), s_dd)
            then(V.tensor_reduce(yd, Wd1, AX_X, ALU.add))
            for q, x, sign in ((1, dq[:, 2, :], 1.0), (4, sa, -1.0)):
                then(V.tensor_tensor(wr, dq[:, 0, :], dq[:, q, :], ALU.mult))
                then(V.tensor_reduce(dot, wr, AX_X, ALU.add))
                then(V.tensor_scalar(dot, dot, sign, None, ALU.mult))
                then(V.scalar_tensor_tensor(yd, x, dot, yd, ALU.mult, ALU.add))
            then(V.bn_stats(bst, yd))
            then(V.bn_aggr(bag, bst), s_dd)
            dve.wait_ge(s_dr, 1)
            then(V.tensor_scalar(yd, yd, bag[:, 0:1], rsd, ALU.subtract, ALU.mult), s_dd)
            then(V.tensor_tensor(Wd1, bj(sa), bi(4), ALU.mult))
            dve.wait_ge(s_ydt, 1)
            r1d = R1[:, :, T:N]
            bc = lambda x: x.unsqueeze(2).to_broadcast([P, KT, NS])
            then(V.tensor_tensor(r1d, pj[:, 1, 1, 0:HD].rearrange("p (m s) -> p m s", m=PAIRS), bc(vecs[:, V_GNW, :]), ALU.mult))
            then(V.tensor_tensor(r1d, r1d, bc(vecs[:, V_GNB, :]), ALU.add))
            then(V.tensor_tensor(r1d, r1d, decbuf[:, 6, :, :], ALU.add))
            then(V.tensor_tensor(r1d, r1d, decbuf[:, 7, :, :], ALU.mult), s_r1)
            dve.wait_ge(s_dp, 1)
            then(V.tensor_tensor(Wd2, Wd2, Wd1, ALU.subtract))
            dve.wait_ge(s_dp, 2)
            then(V.tensor_tensor(Sd, Sd, Wd2, ALU.add), s_dd)

            nn = [0]

            def mean(width):
                nn[0] += 1
                dve.wait_ge(s_ns, nn[0])
                mark(V.tensor_scalar(st[:, 0:T], bk[:, 2, :], 1.0 / width, EPS, ALU.mult, ALU.add))
                then(V.tensor_scalar(st[:, T:N], bk[:, 3, 0:NS], 1.0 / width, EPS, ALU.mult, ALU.add), s_nd)
                return nn[0]

            all_k = lambda x: x.unsqueeze(1).to_broadcast([P, KT, N])
            b9 = lambda x: x.unsqueeze(2).to_broadcast([P, KT, 9])

            def residual(layer, gate, post):
                n = mean(D)
                then(V.tensor_tensor(A0[:, :, :], mod[:, gate:gate + KT, :], b9(vecs[:, post, :]), ALU.mult))
                dve.wait_ge(s_na, n)
                dve.wait_ge(s_oa, KT * (layer + 1))
                yd_, sd_ = Y[:, :, T:N], st[:, T:N].unsqueeze(1).to_broadcast([P, KT, NS])
                then(V.tensor_tensor(yd_, yd_, sd_, ALU.mult))
                dve.wait_ge(s_xr, 16)
                then(V.tensor_tensor(yd_, yd_, A0[:, :, 1:9], ALU.mult))
                then(V.tensor_tensor(R0[:, :, T:N], R0[:, :, T:N], yd_, ALU.add))
                for k in range(KT):
                    then(V.tensor_tensor(Y[:, k, 0:T], Y[:, k, 0:T], st[:, 0:T], ALU.mult))
                    mark(V.scalar_tensor_tensor(R0[:, k, 0:T], Y[:, k, 0:T], A0[:, k, 0:1], R0[:, k, 0:T], ALU.mult, ALU.add), s_res)

            residual(0, M_G0, V_POST0)
            dve.wait_ge(s_res, KT)

            def scales(a, sc, g):
                then(V.tensor_scalar(a[:, :, :], mod[:, sc:sc + KT, :], 1.0, None, ALU.add))
                then(V.tensor_tensor(a[:, :, :], a[:, :, :], b9(vecs[:, g, :]), ALU.mult))

            def modulate(x, a, sh, tiles):
                for k in tiles:
                    mark(V.tensor_scalar(x[:, k, 0:T], HN[:, k, 0:T], a[:, k, 0:1], mod[:, sh + k, 0:1], ALU.mult, ALU.add))
                then(V.tensor_tensor(x[:, :, T:N], HN[:, :, T:N], a[:, :, 1:9], ALU.mult))
                then(V.tensor_tensor(x[:, :, T:N], x[:, :, T:N], mod[:, sh:sh + KT, 1:9], ALU.add), s_hh)

            scales(A0, M_SC1, V_PRE1)
            n = mean(D)
            dve.wait_ge(s_na, n)
            then(V.tensor_tensor(HN, R0[:, :, :], all_k(st), ALU.mult), s_hh)
            dve.wait_ge(s_dso, 16)
            modulate(H1, A0, M_SH1, range(KT // 2))
            dve.wait_ge(s_adb, ADA_MT * NADA)
            scales(A1, M_SCK, V_KVN)
            modulate(HK, A1, M_SHK, range(KT))

            n = mean(QL)
            for t in range(KT):
                dve.wait_ge(s_ba, QT + t + 1)
                then(V.tensor_tensor(two(GATE[:, t, :]), two(GATE[:, t, :]), pjs[(QT + t) % 2], ALU.mult), s_bd)
                if t == 0:
                    dve.wait_ge(s_na, n)
                    then(V.tensor_tensor(qa, qa, st.unsqueeze(1).to_broadcast([P, QT, N]), ALU.mult))
                    for k in range(QT):
                        last = V.tensor_scalar(qa[:, k, :], qa[:, k, :], qng[:, k:k + 1], None, ALU.mult)
                        if k < QT - 1:
                            mark(last)
                    then(last, s_qn)
            dve.wait_ge(s_cb, 112)
            for t in range(5):
                c = P if t < TT else NS
                ps = bk[0:c, t % 2, :]
                dve.wait_ge(s_kva, t + 1)
                then(V.tensor_scalar(kss[0:c, 1:2], kss[0:c, 0:1], 1.0 / KVL, EPS, ALU.mult, ALU.add), s_kvd)
                mark(V.tensor_tensor(kvn[0:c, t, 256:320], ps[:, 256:320], cosN[0:c, t, :], ALU.mult))
                then(V.tensor_tensor(rt64[0:c], ps[:, 320:384], sinN[0:c, t, :], ALU.mult))
                then(V.tensor_tensor(kvn[0:c, t, 256:320], kvn[0:c, t, 256:320], rt64[0:c], ALU.add))
                mark(V.tensor_copy(kvn[0:c, t, 320:384], kvn[0:c, t, 256:320]))
                dve.wait_ge(s_kvr, t + 1)
                then(V.scalar_tensor_tensor(kvn[0:c, t, 0:KVL], ps[:, 0:KVL], kss[0:c, 1:2], kvg[0:c], ALU.mult, ALU.mult), s_kvn)

            for i in range(4):
                dve.wait_ge(s_bm, B_PE + 2 * i + 2)
                then(V.tensor_tensor(two(QP[:, i, :]), rope_slot(8 + 2 * i), two(cosT), ALU.mult))
                then(V.tensor_tensor(two(rtmp), rope_slot(9 + 2 * i), two(sinT), ALU.mult))
                then(V.tensor_tensor(QP[:, i, :], QP[:, i, :], rtmp, ALU.add), s_bd)

            def rows(n):
                w = (n % TT + 1) * P
                dve.wait_ge(s_sm, n + 1)
                dve.wait_ge(s_sa1, n)
                then(V.tensor_tensor(bk[:, 0, w - P:w], bk[:, 0, w - P:w], causal, ALU.add))
                then(V.tensor_reduce(mx[:, 0:1], bk[:, 0, 0:w], AX_X, ALU.max))
                then(V.tensor_scalar(nmx[:, 0:1], mx[:, 0:1], -SCALE, None, ALU.mult), s_sd1)
                dve.wait_ge(s_sa1, n + 1)
                then(V.reciprocal(mx[:, 1:2], den[:, 0:1]))
                then(V.tensor_scalar(PN[:, 0:w], PN[:, 0:w], mx[:, 1:2], None, ALU.mult), s_sd2)

            def gate_head(h):
                dve.wait_ge(s_po, TT * (h + 1))
                then(V.tensor_tensor(OG[:, h, 0:T], bk[:, 2, :], GATE[:, h, 0:T], ALU.mult), s_pog)

            def cache_turned(n):
                dve.wait_ge(s_kt, n + 1)
                if n >= 2:
                    dve.wait_ge(s_ds, scored(n - 2))
                mark(V.tensor_copy(KR[n % 2], pj[0:ROPE, 1, 0, :]), s_ktd)

            def scores_stored(n):
                s, g = n // TT, n % TT
                dve.wait_ge(s_ds, scored(n))
                if g == 0:
                    dve.wait_ge(s_dpt, s)
                mark(V.tensor_copy(drow[:, g * 512:(g + 1) * 512], pj[0:H, 1, 1, :]), s_dse)

            def decode_max(s):
                dve.wait_ge(s_ds, 5 * s + 5)
                then(V.tensor_copy(drow[:, PAST:PAST + 1], bk[0:H, 3, 0:1]))
                dve.wait_ge(s_dse, TT * (s + 1))
                then(V.tensor_reduce(dmx, drow, AX_X, ALU.max))
                then(V.tensor_scalar(dnm, dmx, -SCALE, None, ALU.mult), s_dsd)

            def scale_values(s):
                dve.wait_ge(s_dv, s + 1)
                dve.wait_ge(s_dot, s)
                then(V.reciprocal(drc, dden))
                then(V.tensor_scalar(dval, bk[0:H, 3, 0:KVL], drc, None, ALU.mult), s_dvs)

            def decode_latent(s):
                dve.wait_ge(s_dot, s + 1)
                then(V.tensor_copy(olat[:, :, :, s], bk[:, 3, 0:2 * H].rearrange("p (a h) -> p a h", a=2)), s_dvd)

            dve.wait_ge(s_kvo, 160)
            rows(0)
            for n in range(NSTEP):
                s, g = n // TT, n % TT
                if s >= 1 and g == 0:
                    gate_head(s - 1)
                cache_turned(n)
                if s >= 2 and g == 0:
                    scale_values(s - 2)
                if g == 2:
                    scores_stored(n - 2)
                if n + 1 < NSTEP:
                    rows(n + 1)
                if n >= 1 and g != 1:
                    scores_stored(n - 1)
                if s >= 1 and g == 0:
                    decode_max(s - 1)
                if s >= 2 and g == 1:
                    decode_latent(s - 2)
            gate_head(H - 1)
            scale_values(NS - 2)
            scores_stored(NSTEP - 1)
            decode_max(NS - 1)
            decode_latent(NS - 2)
            scale_values(NS - 1)
            decode_latent(NS - 1)
            dve.wait_ge(s_do, 1)
            then(V.tensor_tensor(OG[:, :, T:N], bk[:, 3, P:P + H * NS].rearrange("p (h s) -> p h s", h=H),
                                 GATE[:, :, T:N], ALU.mult), s_pog)
            residual(1, M_G1, V_POST1)


def host_layout(i):
    f = np.float32

    def feat(a):
        a = np.asarray(a)
        lead = a.shape[:-1]
        a = a.reshape(*lead, KT, P)
        return np.moveaxis(a, -1, 0)

    def cols(a, width):
        k, n = a.shape
        return np.ascontiguousarray(a.reshape(k // P, P, n // width, width).transpose(2, 1, 0, 3))

    r = {}
    x = np.concatenate([i["x_prompt"][0], i["x_sample"][:, 0]], 0)
    r["xT"] = np.ascontiguousarray(x.T.reshape(KT, P, N).transpose(1, 0, 2))
    c = np.concatenate([i["c_prompt"], i["c_sample"]], 0)
    r["cT"] = np.ascontiguousarray(c.T.reshape(KT, P, 1 + NS).transpose(1, 0, 2))
    r["shiftT"] = np.ascontiguousarray(i["state_shift"][0].T.reshape(KT, P, NS).transpose(1, 0, 2))
    ada = np.concatenate([i["ada_w"][0], i["ada_w"][1], i["kv_ada_w"]], 1)
    r["ada"] = cols(ada, ADA_COLS).reshape(ADA_GROUPS, P, 4096)
    r["adab"] = np.ascontiguousarray(np.concatenate([i["ada_b"][0], i["ada_b"][1], i["kv_ada_b"]]).reshape(MOD_TILES, P).T)
    vs = [i["norm_pre"][0], i["norm_pre"][1], i["norm_post"][0], i["norm_post"][1], *i["a_mu"][0],
          i["a_w0"][0], i["a_a0"][0], i["a_k_k"][0], i["a_k_a"][0], i["a_r_k"][0].reshape(-1),
          i["a_gn_w"][0], i["a_gn_b"][0], i["kv_norm"]]
    r["vecs"] = np.ascontiguousarray(np.stack([v.reshape(KT, P).T for v in vs], 1))
    w = i["a_w_in"][0]
    r["w_in"] = np.ascontiguousarray(w.reshape(4, KT, P, PAIRS, P).transpose(3, 2, 0, 1, 4)).reshape(PAIRS, P, 4096)
    l1 = np.concatenate([i["a_w1"][0], i["a_a1"][0]], 1)
    r["lora1"] = np.ascontiguousarray(l1.reshape(KT, P, P).transpose(1, 0, 2))
    l2 = np.concatenate([i["a_w2"][0], i["a_a2"][0]], 0)
    r["lora2"] = np.ascontiguousarray(l2.reshape(P, PAIRS, P).transpose(1, 0, 2))
    st = i["state_wkv"][0].reshape(NS, PAIRS, 2, HD, HD).transpose(2, 1, 0, 3, 4)
    r["Sd"] = np.ascontiguousarray(st.reshape(P, HD, HD))
    r["w_out"] = cols(i["a_w_out"][0], 512).reshape(2, P, 4096)
    r["b_w_out"] = cols(i["b_w_out"][0], 512).reshape(2, P, 4096)
    swap = np.r_[ROPE // 2:ROPE, 0:ROPE // 2]
    kva = i["kv_w_a"]
    r["kv_w_a"] = cols(np.concatenate([kva, kva[:, KVL + swap]], 1), 384).reshape(1, P, KT * 384)
    bw = i["b_w_in"][0]
    pad = np.zeros((P, KT * 128), f)
    r["b_w_in"] = np.stack([np.concatenate([cols(bw[:, 0:QL], QL).reshape(P, KT * QL), pad], 1),
                            *cols(bw[:, QL:], 512).reshape(2, P, 4096)])
    wq = i["b_w_q"][0]
    pe = wq[:, :, NOPE:]
    r["w_q"] = np.stack([cols(wq[:, :, 0:NOPE].reshape(QL, H * NOPE), H * NOPE).reshape(P, QT * D),
                         cols(np.concatenate([pe.reshape(QL, -1), pe[:, :, swap].reshape(QL, -1)], 1), D).reshape(P, QT * D)])
    kvb = i["kv_w_b"]
    uk = kvb[:, :, 0:NOPE]
    r["uk"] = np.concatenate([uk.reshape(2, P, H * NOPE).transpose(1, 0, 2).reshape(P, -1),
                              uk.transpose(2, 1, 0).reshape(P, -1)], 1)[None]
    r["uv"] = np.ascontiguousarray(kvb[:, :, NOPE:].reshape(2, P, H * P).transpose(1, 0, 2))
    r["kvg"] = np.broadcast_to(i["kv_a_norm"], (P, KVL)).copy()
    r["qng"] = np.ascontiguousarray(i["b_q_norm"][0].reshape(QT, P).T)
    r["page_table"] = np.ascontiguousarray(np.repeat(i["page_table"].T, PAGE // 16, axis=0))
    r["cache_c"] = i["cache_kv_latent"].reshape(-1, NPAGES * KVL)
    r["cache_r"] = i["cache_k_rope"].reshape(-1, NPAGES * ROPE)
    inv = f(ROPE_THETA) ** (-np.arange(ROPE // 2, dtype=f) / f(ROPE // 2))
    pos = np.concatenate([np.arange(T), np.full(NS, PAST)]).astype(f)
    ang = pos[:, None] * inv[None, :]
    cs = np.concatenate([np.cos(ang), np.cos(ang)], 1).astype(f)
    sn = np.concatenate([-np.sin(ang), np.sin(ang)], 1).astype(f)
    r["cosT"], r["sinT"] = (np.concatenate([a.T, a.T], 0).copy() for a in (cs, sn))
    r["cosN"], r["sinN"] = (np.ascontiguousarray(np.concatenate([a, np.zeros((5 * P - N, ROPE), f)], 0)
                            .reshape(5, P, ROPE).transpose(1, 0, 2)) for a in (cs, sn))
    r["causal"] = np.where(np.arange(P)[None, :] <= np.arange(P)[:, None], 0, NEG).astype(f)
    r["prow"] = (np.arange(P) % 8).astype(f)[:, None]
    r["ident"] = np.eye(P, dtype=f)
    r["ones"] = np.ones((P, P), f)
    s, t = np.meshgrid(np.arange(P) % C, np.arange(C), indexing="ij")
    r["maskM"] = np.concatenate([t > s, t >= s, t > s, t >= s], 1).astype(f)
    r["lowm"] = (t < s).astype(f)
    off = lambda a, b, m: (a // (2 * m) == b // (2 * m)) & (a % (2 * m) >= m) & (b % (2 * m) < m)
    r["lv1"] = np.stack([off(s, t, 1), off(t, s, 1)], 1).astype(f)
    r["lvm"] = np.stack([off(t, s, m) for m in LEVELS], 1).astype(f)
    r["id64"] = (s == t).astype(f)
    hb = np.arange(P) // HD
    r["bones"] = (hb[:, None] == hb[None, :]).astype(f)
    r["scanm"] = np.broadcast_to(np.where(np.arange(N) < T, np.arange(N) % C != 0, False).astype(f), (P, N)).copy()
    return r


OUTS = {"shift": (P, KT, 1 + NS), "wkv_p": (2 * PAIRS, HD, HD), "wkv_s": (P, HD, HD), "ckv": (N, KVL),
        "kpe": (N, ROPE), "y": (P, KT, N)}


def kernel(**inputs):
    import concourse.bacc as bacc
    from concourse.bass_utils import run_bass_kernel_spmd

    nc = bacc.Bacc("TRN2", target_bir_lowering=False, num_devices=1)
    arrays = host_layout({k: np.asarray(v) for k, v in inputs.items()})
    d = {k: nc.dram_tensor(f"in_{k}", a.shape, mybir.dt.from_np(a.dtype), kind="ExternalInput").ap()
         for k, a in arrays.items()}
    o = {k: nc.dram_tensor(f"out_{k}", s, F32, kind="ExternalOutput").ap() for k, s in OUTS.items()}
    build(nc, d, o)
    r = run_bass_kernel_spmd(nc, [{f"in_{k}": a for k, a in arrays.items()}], core_ids=[0]).results[0]
    sh = np.asarray(r["out_shift"]).transpose(2, 1, 0).reshape(1 + NS, D)
    y = np.asarray(r["out_y"]).transpose(2, 1, 0).reshape(N, D)
    wkv_s = np.asarray(r["out_wkv_s"]).reshape(2, PAIRS, NS, HD, HD).transpose(2, 1, 0, 3, 4).reshape(1, NS, 2 * PAIRS, HD, HD)
    ckv, kpe = np.asarray(r["out_ckv"]), np.asarray(r["out_kpe"])
    return (y[None, 0:T], y[T:, None], np.asarray(r["out_wkv_p"])[None, None], sh[0][None, None],
            ckv[None, 0:T], kpe[None, 0:T], wkv_s, sh[1:][None], ckv[T:, None], kpe[T:, None])
```
